# Optimizing a Trainium2 kernel written in Bass

```python
import jax, jax.numpy as jnp
from jax import lax
import numpy as np

D_MODEL = 2048
BATCH = 1
SEQ = 512
DEPTH = 1
DEC_BATCH = 8
DEC_SEQ = 16
PAST_LEN = 512

CHUNK = 64
CONV_DIM = 1024
CONV_WIDTH = 31
DN_HEADS = 8
DN_DK = 128
DN_DV = 128
DN_KEY = DN_HEADS * DN_DK
DN_VAL = DN_HEADS * DN_DV
DN_CONV_WIDTH = 4
DN_CONV_CH = 2 * DN_KEY + DN_VAL
N_BRANCH = 2
PEER_HEADS = 8
PEER_QDIM = 256
PEER_HALF = PEER_QDIM // 2
N_KEYS = 128
N_EXPERTS = N_KEYS * N_KEYS
PEER_TOPK = 16
PEER_BLOCK = 64
EPS = 1e-6
IN_SPLITS = (2 * CONV_DIM, DN_CONV_CH, DN_HEADS, DN_HEADS, DN_VAL, N_BRANCH * D_MODEL)
IN_DIM = sum(IN_SPLITS)

kernel_name = 'streaming_conv_gdn_peer'

def rms_norm(x, g):
    xf = x.astype(jnp.float32)
    y = xf * lax.rsqrt(jnp.mean(xf * xf, axis=-1, keepdims=True) + EPS)
    return (y * g.astype(jnp.float32)).astype(x.dtype)

def layer_norm(x, g, b):
    xf = x.astype(jnp.float32)
    mu = jnp.mean(xf, axis=-1, keepdims=True)
    var = jnp.mean(jnp.square(xf - mu), axis=-1, keepdims=True)
    y = (xf - mu) * lax.rsqrt(var + EPS)
    return (y * g.astype(jnp.float32) + b.astype(jnp.float32)).astype(x.dtype)

def l2_normalize(x):
    return x * lax.rsqrt(jnp.sum(x * x, axis=-1, keepdims=True) + EPS)

def causal_dwconv(x, prefix, w):
    xp = jnp.concatenate([prefix.astype(x.dtype), x], axis=1)
    y = lax.conv_general_dilated(xp, w[:, None, :].astype(x.dtype), window_strides=(1,), padding='VALID',
                                 dimension_numbers=('NWC', 'WIO', 'NWC'), feature_group_count=x.shape[-1])
    return y, xp[:, -(w.shape[0] - 1):]

def gated_delta_chunked(q, k, v, beta, g, s0, chunk):
    bsz, t_len, h, dk = q.shape
    dv = v.shape[-1]
    n_blk = t_len // chunk

    def blk(a):
        return jnp.swapaxes(a.reshape((bsz, n_blk, chunk) + a.shape[2:]), 2, 3)

    q, k, v, beta, g = blk(q), blk(k), blk(v), blk(beta), blk(g)
    G = jnp.cumsum(g, axis=-1)
    causal = jnp.tril(jnp.ones((chunk, chunk), bool))
    strict = jnp.tril(jnp.ones((chunk, chunk), bool), -1)
    decay = jnp.exp(jnp.where(causal, G[..., :, None] - G[..., None, :], -jnp.inf))
    kk = jnp.einsum('bnhid,bnhjd->bnhij', k, k)
    a_mat = jnp.where(strict, beta[..., :, None] * kk * decay, 0.0) + jnp.eye(chunk, dtype=jnp.float32)
    gam = jnp.exp(G)
    rhs = jnp.concatenate([beta[..., None] * v, (beta * gam)[..., None] * k], axis=-1)
    sol = lax.linalg.triangular_solve(a_mat, rhs, left_side=True, lower=True)
    u_blk, w_blk = sol[..., :dv], sol[..., dv:]
    qk = jnp.einsum('bnhid,bnhjd->bnhij', q, k) * decay
    qg = q * gam[..., None]
    kd = k * jnp.exp(G[..., -1:] - G)[..., None]
    gl = jnp.exp(G[..., -1])

    def step(s, inp):
        u_c, w_c, qk_c, qg_c, kd_c, gl_c = inp
        delta = u_c - jnp.einsum('bhck,bhkv->bhcv', w_c, s)
        o = jnp.einsum('bhck,bhkv->bhcv', qg_c, s) + jnp.einsum('bhij,bhjv->bhiv', qk_c, delta)
        s = gl_c[..., None, None] * s + jnp.einsum('bhck,bhcv->bhkv', kd_c, delta)
        return s, o

    xs = (jnp.moveaxis(u_blk, 1, 0), jnp.moveaxis(w_blk, 1, 0), jnp.moveaxis(qk, 1, 0),
          jnp.moveaxis(qg, 1, 0), jnp.moveaxis(kd, 1, 0), jnp.moveaxis(gl, 1, 0))
    s_fin, o = lax.scan(step, s0, xs)
    o = jnp.swapaxes(jnp.moveaxis(o, 0, 1), 2, 3).reshape(bsz, t_len, h, dv)
    return o, s_fin

def mixer(xn, conv_prev, dconv_prev, s_prev, w_in, conv_dw_w, conv_dw_b, conv_ln_g, conv_ln_b, conv_pw2,
          dn_conv_w, dn_a_log, dn_dt_bias, dn_norm_g, dn_w_o, w_out, chunk):
    bsz, t_len, _ = xn.shape
    f32 = jnp.float32
    pts = [sum(IN_SPLITS[:i + 1]) for i in range(len(IN_SPLITS) - 1)]
    glu, qkv, b_raw, a_raw, z, gates = jnp.split(xn @ w_in, pts, axis=-1)
    c_in = glu[..., :CONV_DIM] * jax.nn.sigmoid(glu[..., CONV_DIM:])
    c, conv_new = causal_dwconv(c_in, conv_prev, conv_dw_w)
    c = jax.nn.silu(layer_norm(c + conv_dw_b, conv_ln_g, conv_ln_b))
    y_conv = c @ conv_pw2
    qkv, dconv_new = causal_dwconv(qkv, dconv_prev, dn_conv_w)
    qkv = jax.nn.silu(qkv)
    q, k, v = jnp.split(qkv, [DN_KEY, 2 * DN_KEY], axis=-1)
    q = l2_normalize(q.reshape(bsz, t_len, DN_HEADS, DN_DK).astype(f32)) * (DN_DK ** -0.5)
    k = l2_normalize(k.reshape(bsz, t_len, DN_HEADS, DN_DK).astype(f32))
    v = v.reshape(bsz, t_len, DN_HEADS, DN_DV).astype(f32)
    beta = jax.nn.sigmoid(b_raw.astype(f32))
    g = -jnp.exp(dn_a_log.astype(f32)) * jax.nn.softplus(a_raw.astype(f32) + dn_dt_bias.astype(f32))
    o, s_new = gated_delta_chunked(q, k, v, beta, g, s_prev.astype(f32), chunk)
    o = o * lax.rsqrt(jnp.mean(o * o, axis=-1, keepdims=True) + EPS) * dn_norm_g.astype(f32)
    o = o * jax.nn.silu(z.reshape(bsz, t_len, DN_HEADS, DN_DV).astype(f32))
    y_dn = o.reshape(bsz, t_len, DN_VAL).astype(xn.dtype) @ dn_w_o
    g_conv, g_dn = jnp.split(jax.nn.sigmoid(gates), 2, axis=-1)
    out = (g_conv * y_conv + g_dn * y_dn) @ w_out
    return out, conv_new, dconv_new, s_new.astype(xn.dtype)

def peer(xn, w_q, sub_keys, u, v):
    bsz, t_len, d = xn.shape
    x2 = xn.reshape(-1, d)
    n = x2.shape[0]
    q = (x2 @ w_q).reshape(n, PEER_HEADS, 2, PEER_HALF)
    s = jnp.einsum('nhpd,hpkd->nhpk', q, sub_keys).astype(jnp.float32)
    s_top, i_top = lax.top_k(s, PEER_TOPK)
    cand = (s_top[:, :, 0, :, None] + s_top[:, :, 1, None, :]).reshape(n, PEER_HEADS, PEER_TOPK * PEER_TOPK)
    cand_idx = (i_top[:, :, 0, :, None] * N_KEYS + i_top[:, :, 1, None, :]).reshape(n, PEER_HEADS, PEER_TOPK * PEER_TOPK)
    s_fin, pos = lax.top_k(cand, PEER_TOPK)
    idx = jnp.take_along_axis(cand_idx, pos, axis=-1)
    gate = jax.nn.softmax(s_fin, axis=-1).astype(xn.dtype)
    n_blk = -(-n // PEER_BLOCK)
    pad = n_blk * PEER_BLOCK - n
    xp = jnp.pad(x2, ((0, pad), (0, 0))).reshape(n_blk, PEER_BLOCK, d)
    ip = jnp.pad(idx, ((0, pad), (0, 0), (0, 0))).reshape(n_blk, PEER_BLOCK, PEER_HEADS, PEER_TOPK)
    gp = jnp.pad(gate, ((0, pad), (0, 0), (0, 0))).reshape(n_blk, PEER_BLOCK, PEER_HEADS, PEER_TOPK)

    def block(args):
        xb, ib, gb = args
        hid = jnp.einsum('pd,phkd->phk', xb, u[ib])
        act = jax.nn.gelu(hid) * gb
        return jnp.einsum('phk,phkd->pd', act, v[ib])

    out = lax.map(block, (xp, ip, gp)).reshape(-1, d)[:n]
    return out.reshape(bsz, t_len, d)

def trunk(x, conv_st, dconv_st, dn_st, W, norm_final_g, chunk):
    new_c, new_dc, new_s = [], [], []
    for l in range(DEPTH):
        xn = rms_norm(x, W['norm_mix_g'][l])
        out, c_st, dc_st, s_st = mixer(xn, conv_st[l], dconv_st[l], dn_st[l], W['w_in'][l], W['conv_dw_w'][l],
                                       W['conv_dw_b'][l], W['conv_ln_g'][l], W['conv_ln_b'][l], W['conv_pw2'][l],
                                       W['dn_conv_w'][l], W['dn_a_log'][l], W['dn_dt_bias'][l], W['dn_norm_g'][l],
                                       W['dn_w_o'][l], W['w_out'][l], chunk)
        x = x + out
        x = x + peer(rms_norm(x, W['norm_ffn_g'][l]), W['peer_w_q'][l], W['peer_sub_keys'][l],
                     W['peer_u'][l], W['peer_v'][l])
        new_c.append(c_st)
        new_dc.append(dc_st)
        new_s.append(s_st)
    y = rms_norm(x, norm_final_g)
    return y, jnp.stack(new_c), jnp.stack(new_dc), jnp.stack(new_s)

def setup_inputs(seed: int = 0) -> dict:
    key = jax.random.key(seed)
    ks = jax.random.split(key, 32)
    f32 = jnp.float32

    def nrm(k, shape, s):
        return jax.random.normal(k, shape, f32) * s

    L = DEPTH
    dt = jnp.exp(jax.random.uniform(ks[13], (L, DN_HEADS), f32, np.log(1e-3), np.log(1e-1)))
    return {
        'x_prompt': nrm(ks[0], (BATCH, SEQ, D_MODEL), 1.0),
        'x_sample': nrm(ks[1], (DEC_BATCH, DEC_SEQ, D_MODEL), 1.0),
        'state_conformer_conv': nrm(ks[2], (L, DEC_BATCH, CONV_WIDTH - 1, CONV_DIM), 0.5),
        'state_delta_conv': nrm(ks[3], (L, DEC_BATCH, DN_CONV_WIDTH - 1, DN_CONV_CH), 1.0),
        'state_delta': nrm(ks[4], (L, DEC_BATCH, DN_HEADS, DN_DK, DN_DV), 0.1),
        'norm_mix_g': 1.0 + nrm(ks[5], (L, D_MODEL), 0.02),
        'w_in': nrm(ks[6], (L, D_MODEL, IN_DIM), D_MODEL ** -0.5),
        'conv_dw_w': nrm(ks[7], (L, CONV_WIDTH, CONV_DIM), CONV_WIDTH ** -0.5),
        'conv_dw_b': nrm(ks[8], (L, CONV_DIM), 0.02),
        'conv_ln_g': 1.0 + nrm(ks[9], (L, CONV_DIM), 0.02),
        'conv_ln_b': nrm(ks[10], (L, CONV_DIM), 0.02),
        'conv_pw2': nrm(ks[11], (L, CONV_DIM, D_MODEL), CONV_DIM ** -0.5),
        'dn_conv_w': nrm(ks[12], (L, DN_CONV_WIDTH, DN_CONV_CH), DN_CONV_WIDTH ** -0.5),
        'dn_a_log': jnp.log(jax.random.uniform(ks[14], (L, DN_HEADS), f32, 1.0, 16.0)),
        'dn_dt_bias': dt + jnp.log(-jnp.expm1(-dt)),
        'dn_norm_g': 1.0 + nrm(ks[15], (L, DN_DV), 0.02),
        'dn_w_o': nrm(ks[16], (L, DN_VAL, D_MODEL), DN_VAL ** -0.5),
        'w_out': nrm(ks[17], (L, D_MODEL, D_MODEL), D_MODEL ** -0.5),
        'norm_ffn_g': 1.0 + nrm(ks[18], (L, D_MODEL), 0.02),
        'peer_w_q': nrm(ks[19], (L, D_MODEL, PEER_HEADS * PEER_QDIM), D_MODEL ** -0.5),
        'peer_sub_keys': nrm(ks[20], (L, PEER_HEADS, 2, N_KEYS, PEER_HALF), PEER_HALF ** -0.5),
        'peer_u': nrm(ks[21], (L, N_EXPERTS, D_MODEL), D_MODEL ** -0.5),
        'peer_v': nrm(ks[22], (L, N_EXPERTS, D_MODEL), 0.5),
        'norm_final_g': 1.0 + nrm(ks[23], (D_MODEL,), 0.02),
    }

def reference(x_prompt, x_sample, state_conformer_conv, state_delta_conv, state_delta, norm_mix_g, w_in,
              conv_dw_w, conv_dw_b, conv_ln_g, conv_ln_b, conv_pw2, dn_conv_w, dn_a_log, dn_dt_bias, dn_norm_g,
              dn_w_o, w_out, norm_ffn_g, peer_w_q, peer_sub_keys, peer_u, peer_v, norm_final_g):
    W = {'norm_mix_g': norm_mix_g, 'w_in': w_in, 'conv_dw_w': conv_dw_w, 'conv_dw_b': conv_dw_b,
         'conv_ln_g': conv_ln_g, 'conv_ln_b': conv_ln_b, 'conv_pw2': conv_pw2, 'dn_conv_w': dn_conv_w,
         'dn_a_log': dn_a_log, 'dn_dt_bias': dn_dt_bias, 'dn_norm_g': dn_norm_g, 'dn_w_o': dn_w_o,
         'w_out': w_out, 'norm_ffn_g': norm_ffn_g, 'peer_w_q': peer_w_q, 'peer_sub_keys': peer_sub_keys,
         'peer_u': peer_u, 'peer_v': peer_v}
    bp = x_prompt.shape[0]
    dt_ = x_prompt.dtype
    zc = jnp.zeros((DEPTH, bp, CONV_WIDTH - 1, CONV_DIM), dt_)
    zdc = jnp.zeros((DEPTH, bp, DN_CONV_WIDTH - 1, DN_CONV_CH), dt_)
    zs = jnp.zeros((DEPTH, bp, DN_HEADS, DN_DK, DN_DV), dt_)
    y_prompt, pc, pdc, ps = trunk(x_prompt, zc, zdc, zs, W, norm_final_g, CHUNK)
    y_sample, sc, sdc, ss = trunk(x_sample, state_conformer_conv, state_delta_conv, state_delta, W,
                                  norm_final_g, x_sample.shape[1])
    return (y_prompt, y_sample, pc, pdc, ps, sc, sdc, ss)


_drawn_inputs = setup_inputs


def setup_inputs(seed=0):
    import zlib

    import numpy as np

    out = dict(_drawn_inputs(seed))
    spreads = {}
    factors = {'conv_ln_b': 8.201,
     'dn_norm_g': 9.749,
     'norm_final_g': 23.699,
     'conv_dw_b': 2.795,
     'conv_ln_g': 3.432,
     'norm_ffn_g': 2.727}
    for name, (base, spread) in spreads.items():
        noise = np.random.default_rng([zlib.crc32(name.encode()), seed]).standard_normal(out[name].shape)
        drawn = base * np.exp(spread * noise) if base else spread * noise
        out[name] = __import__('jax').numpy.asarray(drawn.astype(out[name].dtype))
    for name, factor in factors.items():
        out[name] = (out[name] * factor).astype(out[name].dtype)
    return out
```

```python
from contextlib import ExitStack

import concourse.bass as bass
from concourse import mybir

P = 128
D = 2048
NP_TOK = 512
NB, NT = 8, 16
T = NP_TOK + NB * NT
TILES = T // P
PT = NP_TOK // P
KD = D // P
CONV = 1024
CW = 31
NC = CONV // P
H = 8
DCW = 4
PH = 8
TOPK = 16
NK = 128
NE = NK * NK
HP = 2 * PH
SLOTS = PH * TOPK
EPS = 1e-6
LEVELS = 7
OCW = 256
NOC = D // OCW

F32 = mybir.dt.float32
U32 = mybir.dt.uint32
ALU = mybir.AluOpType
ACT = mybir.ActivationFunctionType
X = mybir.AxisListType.X

PCOLS = {}
_o = 0
for _n, _w in (("mix_g", KD), ("conv_w", NC * CW), ("conv_b", NC), ("ln_g", NC), ("ln_b", NC),
               ("dconv_w", 3 * H * DCW), ("dn_g", 1), ("dt_bias", H), ("a_log", H)):
    PCOLS[_n] = (_o, _w)
    _o += _w
PW = _o

IDENT, ONES, TRI_P, TRI_S, BLK_S, LEV0 = range(6)
NCONST = LEV0 + LEVELS

KINDS = ("q", "k", "v", "gate", "glu")
QPAD = NP_TOK + DCW - 1 + NB * (NT + DCW - 1)
CPAD = NP_TOK + CW - 1 + NB * (NT + CW - 1)
QLEN = QPAD - (DCW - 1)
CLEN = CPAD - (CW - 1)
RING = 4


def build(nc, x_prompt, x_sample, consts, params, conv_prefix, dconv_prefix, state_in, w_ba, w_group, w_z,
          w_merge, w_out, w_q, keys, ffn_g, final_g, peer_u, peer_v,
          y_prompt, y_sample, conv_new_p, dconv_new_p, state_new_p, conv_new_s, dconv_new_s, state_new_s):
    with ExitStack() as ctx:
        def sb(name, shape, dt=F32):
            return ctx.enter_context(nc.sbuf_tensor(name, shape, dt))

        def sem(name):
            return ctx.enter_context(nc.semaphore(name))

        XNT, CT, QT, KT, VT, WR, TM = 0, 10240, 15360, 20480, 25600, 30720, 40960
        END = 49152
        arena = sb("arena", [P, END])

        def at(off, *dims):
            n = 1
            for d in dims:
                n *= d
            v = arena[:, off:off + n]
            if len(dims) == 2:
                v = v.rearrange("p (a b) -> p a b", a=dims[0])
            elif len(dims) == 3:
                v = v.rearrange("p (a b c) -> p a b c", a=dims[0], b=dims[1])
            return v

        cst = sb("cst", [P, NCONST, P])
        par = sb("par", [P, PW])
        wba = sb("wba", [P, KD, 2 * H])
        dpre = sb("dpre", [P, 3 * H * NB, DCW - 1])
        dnew_p = sb("dnew_p", [P, 3 * H, DCW - 1])
        dnew_s = sb("dnew_s", [P, 3 * H * NB, DCW - 1])
        small = sb("small", [P, 136])
        epsc = sb("epsc", [P, 1])
        beta = sb("beta", [P, TILES, H])
        glog = sb("glog", [P, TILES, H])
        smalld = sb("smalld", [P, 256])

        ident = cst[:, IDENT, :]
        ones = cst[:, ONES, :]

        def pcol(name, i=0, n=1):
            o = PCOLS[name][0]
            return par[:, o + i:o + i + n]

        ps = [ctx.enter_context(nc.psum_tensor(f"ps{i}", [P, 1024], F32)) for i in range(4)]

        def ps8(i):
            return ps[i][:].rearrange("p (h c) -> p h c", h=8)

        xnT = at(XNT, KD, T)
        cT = at(CT, NC, T)
        qT = at(QT, H, T)
        kT = at(KT, H, T)
        vT = at(VT, H, T)
        xin = at(KT, TILES, D)

        ld_par, ld_x = sem("ld_par"), [sem(f"ld_x{t}") for t in range(TILES)]
        pace = {e: sem(f"pace_{e}") for e in ("sp", "act", "pe", "dve", "pool")}
        ready0 = sem("ready0")
        sumsq, msq, root, xscaled, xtr, xevac = (sem(n) for n in ("sumsq", "msq", "root", "xscaled", "xtr", "xevac"))
        ba_mm, ba_act, ba_dve = sem("ba_mm"), sem("ba_act"), sem("ba_dve")
        a_link, d_link, p_link = sem("a_link"), sem("d_link"), sem("p_link")

        def wreg(eng, name, s, v):
            eng.wait_ge(s, v)
            eng.sem_inc(pace[name], 1)

        class Link:

            def __init__(self, eng, name, s, base=0, loop=False):
                self.eng, self.name, self.s, self.base, self.n, self.loop = eng, name, s, base, 0, loop

            def __call__(self, ins):
                self.n += 1
                ins.then_inc(self.s, 1)
                if self.loop:
                    wreg(self.eng, self.name, self.s, self.base + self.n)
                else:
                    self.eng.wait_ge(self.s, self.base + self.n)

        block = ctx.enter_context(nc.Block())

        pads = {"q": TM, "k": TM + QPAD, "v": TM + 2 * QPAD}
        CPB = TM + 3 * QPAD
        CACC = CPB + CPAD
        QACC = CACC + CPAD
        SIG = QACC + QPAD
        SQ = SIG + T
        RT = SQ + 2 * T
        assert RT + T <= END
        wring = {kd: at(WR + i * D, KD, P) for i, kd in enumerate(KINDS)}
        w_ld = {kd: sem(f"w_ld_{kd}") for kd in KINDS}
        mm = {kd: sem(f"mm_{kd}") for kd in KINDS}
        evac = {kd: sem(f"evac_{kd}") for kd in KINDS}
        conv_done = {kd: sem(f"conv_done_{kd}") for kd in "qkv"}
        silu_done = {kd: sem(f"silu_done_{kd}") for kd in "qkv"}
        stage_done = {kd: sem(f"stage_done_{kd}") for kd in "qkv"}
        prefix_done = {kd: sem(f"prefix_done_{kd}") for kd in "qkvc"}
        sq_done = {kd: sem(f"sq_done_{kd}") for kd in "qk"}
        mm_sum = {kd: sem(f"mm_sum_{kd}") for kd in "qk"}
        norm_root = {kd: sem(f"norm_root_{kd}") for kd in "qk"}
        norm_done = {kd: sem(f"norm_done_{kd}") for kd in "qk"}
        glu_done, cconv_done, cbias_done, cstate_out = sem("glu_done"), sem("cconv_done"), sem("cbias_done"), sem("cstate_out")
        dve_loop, dve_conv = sem("dve_loop"), sem("dve_conv")
        PSK = {"q": 0, "k": 1, "v": 2, "gate": 0, "glu": 1}

        def qpad(kd):
            return at(pads[kd], QPAD)

        def seg(buf, width, lead):
            return buf[:, NP_TOK + lead:NP_TOK + lead + NB * width].rearrange("p (b w) -> p b w", b=NB)

        ln_sum, ln_mean, ln_cent, ln_sq, ln_var, ln_root, ln_scaled, ln_out = (
            sem(n) for n in ("ln_sum", "ln_mean", "ln_cent", "ln_sq", "ln_var", "ln_root", "ln_scaled", "ln_out"))
        ln_sqmm = sem("ln_sqmm")
        LSQ = TM
        LMEAN = TM + 2 * T

        SLOT = [TM + 1024 * i for i in range(8)] + [WR + 8192, WR + 9216]
        kc, qc, vc, eb, qkd, atb, tb, ttb, xb, atl = (at(o, H, P) for o in SLOT)
        st_p = at(WR, H, P)
        st_s = at(WR, H, NB, P)
        st_s_dst = at(WR, 8192)
        dd = {n: sem(f"dd_{n}") for n in (
            "copied", "gsum", "gexp_in", "gexp", "trig", "rows", "ediff", "eexp", "kk", "qk", "at", "atl", "x", "xc",
            "tx", "t", "tt", "ktr", "kd", "ks", "r2", "dl", "dlc", "o2", "sup", "snew", "oroot", "oscaled",
            "otr", "out", "vtr", "vb", "ksT", "ksc", "oss", "dm", "grow", "init")}
        dd_link_d = sem("dd_link_d")
        st_ld, st_out = (ld_x[4], 16), sem("st_out")

        z_ld = [(w_ld["q"], 16 * NC), (w_ld["k"], 16 * NC)]
        z_mm, z_act, z_dve = (mm["glu"], NC), sem("z_act"), sem("z_dve")
        mg_ld = [(w_ld[kd], 16 * NC) for kd in ("v", "gate", "glu")]
        mg_mm = [(mm[kd], NC) for kd in ("q", "k", "v", "gate")]
        mg_sig, mg_out, mg_t = sem("mg_sig"), sem("mg_out"), sem("mg_t")
        mT = at(KT, KD, T)
        x1 = at(XNT, TILES, D)
        wo_ld = [(w_ld[kd], 16 * (NC + H // 2)) for kd in "qk"]
        wo_mm, wo_add, xr_ld = sem("wo_mm"), sem("wo_add"), (ld_x[3], 16)
        xn2 = at(CT, TILES, D)
        xn2T = at(KT, KD, T)
        n2_sumsq, n2_msq, n2_root, n2_done, n2_tr, n2_evac = (
            (sumsq, TILES), (msq, 1), (root, 1), (xscaled, TILES), (xtr, 2 * TILES), (xevac, 2 * TILES))
        g_ld, key_ld = (ld_x[0], 16), (ld_x[1], 16)
        wq_ld = [(w_ld[kd], 16 * (NC + H // 2 + NOC // 2)) for kd in "qk"]
        q_mm, q_evac, s_mm, s_evac, tk_done, tk_link = (sem(n) for n in ("q_mm", "q_evac", "s_mm", "s_evac", "tk_done", "tk_link"))
        KEYS = TM
        QH = TM + 2048
        SC = QH + T
        SC2 = SC + T
        STOP = SC2 + T
        ITOP = STOP + TILES * HP * TOPK
        keyT = at(KEYS, HP, NK)
        stop_ = at(STOP, TILES, HP * TOPK)
        itop = at(ITOP, TILES, HP * TOPK)
        assert ITOP + TILES * HP * TOPK <= END
        itop_u = at(ITOP + TILES * HP * TOPK + TILES * TOPK, TILES, TOPK).bitcast(U32)
        idx_all = at(KT + 9 * D, TILES, SLOTS).bitcast(U32)
        gate_all = at(KT + 9 * D + TILES * SLOTS, TILES, SLOTS)
        posu = at(KT + 4 * D, SLOTS).bitcast(U32)
        sel_link, sel_pre, sel_exp, iota_done = sem("sel_link"), sem("sel_pre"), sem("sel_exp"), sem("iota_done")
        iota16 = sb("iota16", [P, TOPK])
        iota_i = sb("iota_i", [P, TOPK], mybir.dt.int32)
        topbuf = at(ITOP + TILES * HP * TOPK, TILES, TOPK)
        posu2 = at(KT + 4 * D + SLOTS, 2, SLOTS).bitcast(U32)
        gcol = sb("gcol", [P, RING])
        act_w2 = sb("act_w2", [P, RING])
        cur_idx = sb("cur_idx", [P, 2, RING], U32)
        urow = [at(KT + i * D, D) for i in range(RING)]
        vrow = [at(KT + (RING + i) * D, D) for i in range(RING)]
        JUNK = KT + 2 * RING * D
        xcur = at(TM, D)
        acc = at(TM + D, D)
        fing = at(TM + 2 * D, D)
        yout = at(TM + 3 * D, D)
        hid = sb("hid", [P, RING])
        act_w = sb("act_w", [P, RING])
        u_ld = [(sem(f"u_ld{i}"), 0) for i in range(RING)]
        v_ld = [sem(f"v_ld{i}") for i in range(RING)]
        idx_cur, hid_done, gelu_done, coef_done, u_used, v_used, ex_begin, ex_link, ex_tile = (
            sem(n) for n in ("idx_cur", "hid_done", "gelu_done", "coef_done", "u_used", "v_used", "ex_begin", "ex_link", "ex_tile"))
        fin_sq, fin_ms, fin_root, fin_y, y_out, fg_ld = (*(sem(n) for n in ("fin_sq", "fin_ms", "fin_root", "fin_y", "y_out")), (ld_x[2], 16))
        out_done, y_free = sem("out_done"), sem("y_free")
        NG = SLOTS // RING

        def count_s(per, k):
            prompt = {2 * 4: 2 * LEVELS, 2 * 4 - 2: 2 * LEVELS - 2, 2 * 4 + 1: 2 * LEVELS + 1, 4 * 4 - 2: 4 * LEVELS - 2}.get(per, per)
            return PT * prompt + k

        @block.sync
        def _(sp):
            for t in range(TILES):
                src = x_prompt[t * P:(t + 1) * P, :] if t < PT else x_sample
                sp.dma_start(xin[:, t, :], src).then_inc(ld_x[t], 16)
                if t == 0:
                    sp.dma_start(cst[:], consts).then_inc(ld_par, 16)
                    sp.dma_start(par[:], params).then_inc(ld_par, 16)
                    sp.dma_start(wba[:], w_ba).then_inc(ld_par, 16)
            sp.dma_start(dpre[:], dconv_prefix).then_inc(ld_par, 16)
            for kd in KINDS:
                sp.dma_start(wring[kd].rearrange("p k c -> p (k c)"), w_group[KINDS.index(kd)]).then_inc(w_ld[kd], 16)
            with sp.Fori(0, NC - 1) as c:
                for i, kd in enumerate(KINDS):
                    wreg(sp, "sp", mm[kd], c + 1)
                    sp.dma_start(wring[kd].rearrange("p k c -> p (k c)"),
                                 w_group[bass.ds((c + 1) * 5 + i, 1)].rearrange("a p n -> p (a n)")).then_inc(w_ld[kd], 16)
            sp.wait_ge(dd["snew"], PT * 2)
            sp.dma_start(state_new_p, at(WR, H * P)).then_inc(st_out, 16)
            sp.wait_ge(st_out, 16)
            sp.dma_start(st_s_dst, state_in).then_inc(st_ld[0], 16)
            sp.wait_ge(dd["snew"], PT * 2 + 2 * H)
            sp.dma_start(state_new_s, st_s_dst).then_inc(st_out, 16)
            sp.wait_ge(st_out, 32)
            for i in range(2):
                sp.dma_start(at(WR + i * D, D), w_z[i]).then_inc(z_ld[i][0], 16)
            with sp.Fori(0, H // 2 - 1) as i:
                for r in range(2):
                    wreg(sp, "sp", z_mm[0], 2 * i + (r + 1 + z_mm[1]))
                    sp.dma_start(at(WR + r * D, D), w_z[bass.ds(2 * i + r + 2, 1)].rearrange("a p n -> p (a n)")).then_inc(z_ld[r][0], 16)
            sp.wait_ge(z_mm[0], z_mm[1] + H)
            for j in range(3):
                sp.dma_start(at(WR + j * D, D), w_merge[j]).then_inc(mg_ld[j][0], 16)
            with sp.Fori(0, KD - 1) as n:
                for j, m in ((0, 0), (1, 1), (2, 3)):
                    wreg(sp, "sp", mg_mm[m][0], n + (mg_mm[m][1] + 1))
                    sp.dma_start(at(WR + j * D, D), w_merge[bass.ds((n + 1) * 3 + j, 1)].rearrange("a p n -> p (a n)")).then_inc(mg_ld[j][0], 16)
            sp.wait_ge(mg_mm[3][0], mg_mm[3][1] + KD)
            for i in range(2):
                sp.dma_start(at(WR + i * KD * OCW, KD * OCW), w_out[i]).then_inc(wo_ld[i][0], 16)
            sp.dma_start(x1[:, 0:PT, :], x_prompt.rearrange("(t p) d -> p t d", p=P)).then_inc(xr_ld[0], 16)
            sp.dma_start(x1[:, PT, :], x_sample).then_inc(xr_ld[0], 16)
            with sp.Fori(0, NOC // 2 - 1) as i:
                for r in range(2):
                    wreg(sp, "sp", wo_mm, (2 * i + r + 1) * TILES)
                    sp.dma_start(at(WR + r * KD * OCW, KD * OCW),
                                 w_out[bass.ds(2 * i + r + 2, 1)].rearrange("a p n -> p (a n)")).then_inc(wo_ld[r][0], 16)
            sp.wait_ge(wo_mm, NOC * TILES)
            sp.dma_start(at(WR + 4 * D, D), ffn_g).then_inc(g_ld[0], 16)
            sp.dma_start(at(KEYS, HP * NK), keys).then_inc(key_ld[0], 16)
            for i in range(2):
                sp.dma_start(at(WR + i * D, D), w_q[i]).then_inc(wq_ld[i][0], 16)
            with sp.Fori(0, HP // 2 - 1) as i:
                for r in range(2):
                    wreg(sp, "sp", q_mm, 2 * i + r + 1)
                    sp.dma_start(at(WR + r * D, D), w_q[bass.ds(2 * i + r + 2, 1)].rearrange("a p n -> p (a n)")).then_inc(wq_ld[r][0], 16)
            sp.wait_ge(stage_done["v"], NC + 1)
            sp.wait_ge(stage_done["q"], NC + 1)
            sp.wait_ge(stage_done["k"], NC + 1)
            sp.dma_start(dconv_new_p, dnew_p[:]).then_inc(out_done, 16)
            sp.dma_start(dconv_new_s, dnew_s[:]).then_inc(out_done, 16)
            sp.wait_ge(ex_begin, 1)
            sp.dma_start(fing, final_g).then_inc(fg_ld[0], 16)
            sp.sem_inc(y_free, 1)
            for t in range(TILES):
                sp.wait_ge(fin_y, t + 1)
                dst = y_prompt[t * P:(t + 1) * P, :] if t < PT else y_sample
                sp.dma_start(dst, yout).then_inc(y_out, 16)
                sp.wait_ge(y_out, 16 * t + 16)
                sp.sem_inc(y_free, 1)
            sp.wait_ge(y_out, 16 * TILES)
            sp.wait_ge(out_done, 32)
            sp.wait_ge(cstate_out, 32 * NC)

        @block.tensor
        def _(pe):
            pe.wait_ge(ld_par, 48)
            for t in range(TILES):
                pe.wait_ge(xscaled, t + 1)
                for half in range(2):
                    n = 2 * t + half
                    if n >= 4:
                        pe.wait_ge(xevac, n - 3)
                    for k in range(8):
                        kk = half * 8 + k
                        m = pe.transpose(ps[n % 4][:, k * P:(k + 1) * P], xin[:, t, kk * P:(kk + 1) * P], ident)
                    m.then_inc(xtr, 1)
            pe.wait_ge(xevac, 2 * TILES)
            for t in range(TILES):
                for k in range(KD):
                    m = pe.matmul(ps[3][:, t * 2 * H:(t + 1) * 2 * H], xnT[:, k, t * P:(t + 1) * P], wba[:, k, :],
                                  start=k == 0, stop=k == KD - 1)
            m.then_inc(ba_mm, 1)

            def project(out, w, src, n=KD):
                for k in range(n):
                    pe.matmul(out[:, 0:NP_TOK], w[:, k, :], src[:, k, 0:NP_TOK], start=k == 0, stop=k == n - 1)
                    m = pe.matmul(out[:, NP_TOK:T], w[:, k, :], src[:, k, NP_TOK:T], start=k == 0, stop=k == n - 1)
                return m

            def sum_rows(out, src, start=True, stop=True):
                pe.matmul(out[:, 0:NP_TOK], ones, src[:, 0:NP_TOK], start=start, stop=stop)
                return pe.matmul(out[:, NP_TOK:T], ones, src[:, NP_TOK:T], start=start, stop=stop)

            pe.wait_ge(ba_act, 1)
            pe.wait_ge(ba_dve, 1)
            with pe.Fori(0, NC) as c:
                for kd in KINDS:
                    pe.wait_ge(w_ld[kd], c * 16 + 16)
                    if kd == "q":
                        pe.wait_ge(glu_done, c + 1)
                    elif kd == "k":
                        pe.wait_ge(glu_done, c + 1)
                    elif kd == "v":
                        pe.wait_ge(norm_root["k"], c + 1)
                    elif kd == "gate":
                        pe.wait_ge(evac["q"], c + 1)
                    else:
                        pe.wait_ge(evac["k"], c + 1)
                    project(ps[PSK[kd]], wring[kd], xnT).then_inc(mm[kd], 1)
                pe.wait_ge(sq_done["q"], c + 1)
                pe.wait_ge(norm_root["q"], c + 1)
                sum_rows(ps[3], at(SQ, T)).then_inc(mm_sum["q"], 1)
                pe.wait_ge(sq_done["k"], c + 1)
                pe.wait_ge(evac["v"], c + 1)
                sum_rows(ps[2], at(SQ + T, T)).then_inc(mm_sum["k"], 1)

            pe.wait_ge(cbias_done, NC)
            pe.wait_ge(evac["q"], NC + 0)
            pe.wait_ge(glu_done, NC + 1)
            for c in range(NC):
                m = sum_rows(ps[0], cT[:, c, :], start=c == 0, stop=c == NC - 1)
            m.then_inc(ln_sum, 1)
            for c in range(NC):
                pe.wait_ge(ln_sq, c + 1)
                sum_rows(ps[1], at(LSQ + (c % 2) * T, T), start=c == 0, stop=c == NC - 1).then_inc(ln_sqmm, 1)

            def delta(t, streams, w, tot):
                tri = cst[:, TRI_S if streams else TRI_P, :]
                blk = cst[:, BLK_S, :] if streams else ones
                lev = 4 if streams else LEVELS
                w(dd["copied"], tot(1, 1))
                w(dd["init"], tot(1, 1))
                gcur = smalld[:, 0:H]
                pe.matmul(ps[3][:, 0:H], tri, gcur, start=True, stop=True)
                pe.matmul(ps[3][:, H:2 * H], blk, gcur, start=True, stop=True).then_inc(dd["gsum"], 1)
                w(dd["trig"], tot(2, 1))
                for g in range(2):
                    pe.matmul(ps[0][:, g * 512:(g + 1) * 512], ones, at(SLOT[3] + g * 512, 512), start=True, stop=True).then_inc(dd["rows"], 1)
                w(dd["trig"], tot(2, 2))
                for g in range(2):
                    pe.matmul(ps[1][:, g * 512:(g + 1) * 512], ones, at(SLOT[8] + g * 512, 512), start=True, stop=True).then_inc(dd["rows"], 1)
                for h in range(H):
                    m = pe.matmul(ps[2][:, h * P:(h + 1) * P], kc[:, h, :], kc[:, h, :], start=True, stop=True)
                m.then_inc(dd["kk"], 1)
                w(dd["gexp_in"], tot(1, 1))
                for h in range(H):
                    m = pe.matmul(ps[3][:, h * P:(h + 1) * P], kc[:, h, :], qc[:, h, :], start=True, stop=True)
                m.then_inc(dd["qk"], 1)
                w(dd["ediff"], tot(1, 1))
                for h in range(H):
                    m = pe.transpose(ps[0][:, h * P:(h + 1) * P], vc[:, h, :], ident)
                m.then_inc(dd["vtr"], 1)
                for l in range(lev):
                    for g in range(2):
                        w(dd["atl"], tot(2 * lev, 2 * l + g + 1))
                        if l:
                            w(dd["t"], tot(2 * lev - 2, 2 * l - 1 + g))
                        else:
                            w(dd["at"], tot(2, 2))
                        for h in range(4 * g, 4 * g + 4):
                            m = pe.matmul(ps[1][:, h * P:(h + 1) * P], atl[:, h, :], tb[:, h, :], start=True, stop=True)
                        m.then_inc(dd["x"], 1)
                    for g in range(2):
                        w(dd["xc"], tot(2 * lev, 2 * l + g + 1))
                        w(dd["tt"], tot(2 * lev + 1, 2 * l + g if l else 1))
                        if l < lev - 1:
                            for h in range(4 * g, 4 * g + 4):
                                m = pe.matmul(ps[2][:, h * P:(h + 1) * P], ttb[:, h, :], xb[:, h, :], start=True, stop=True)
                            m.then_inc(dd["tx"], 1)
                        for h in range(4 * g, 4 * g + 4):
                            m = pe.matmul(ps[3][:, h * P:(h + 1) * P], xb[:, h, :], ttb[:, h, :], start=True, stop=True)
                        m.then_inc(dd["tx"], 1)
                w(dd["vb"], tot(1, 1))
                for h in range(H):
                    m = pe.transpose(ps[0][:, h * P:(h + 1) * P], kc[:, h, :], ident)
                m.then_inc(dd["ktr"], 1)
                w(dd["tt"], tot(2 * lev + 1, 2 * lev + 1))
                if not streams:
                    for h in range(H):
                        m = pe.matmul(ps[1][:, h * P:(h + 1) * P], kc[:, h, :], st_p[:, h, :], start=True, stop=True)
                    m.then_inc(dd["ks"], 1)
                    for h in range(H):
                        m = pe.matmul(ps[2][:, h * P:(h + 1) * P], qc[:, h, :], st_p[:, h, :], start=True, stop=True)
                    m.then_inc(dd["ks"], 1)
                else:
                    pe.wait_ge(st_ld[0], st_ld[1] + 16)
                    for j, src in enumerate((kc, qc)):
                        for h in range(H):
                            for b in range(NB):
                                m = pe.matmul(ps[1 + j][:, h * P + b * NT:h * P + (b + 1) * NT], st_s[:, h, b, :],
                                              src[:, h, b * NT:(b + 1) * NT], start=True, stop=True)
                        m.then_inc(dd["ksT"], 1)
                    for j in range(2):
                        pe.wait_ge(dd["ksc"], j + 1)
                        for h in range(H):
                            m = pe.transpose(ps[1 + j][:, h * P:(h + 1) * P], (eb if j == 0 else tb)[:, h, :], ident)
                        m.then_inc(dd["ks"], 1)
                w(dd["r2"], tot(1, 1))
                for h in range(H):
                    m = pe.matmul(ps[3][:, h * P:(h + 1) * P], ttb[:, h, :], vc[:, h, :], start=True, stop=True)
                m.then_inc(dd["dl"], 1)
                w(dd["dlc"], tot(1, 1))
                for h in range(H):
                    m = pe.matmul(ps[1][:, h * P:(h + 1) * P], qkd[:, h, :], atl[:, h, :], start=True, stop=True)
                m.then_inc(dd["o2"], 1)
                w(dd["kd"], tot(1, 1))
                if not streams:
                    for h in range(H):
                        m = pe.matmul(ps[3][:, h * P:(h + 1) * P], atb[:, h, :], atl[:, h, :], start=True, stop=True)
                    m.then_inc(dd["sup"], 1)
                else:
                    for h in range(H):
                        pe.wait_ge(dd["dm"], h + 1)
                        if h:
                            pe.wait_ge(dd["snew"], PT * 2 + 2 * h)
                        for g in range(2):
                            pe.matmul(ps[3][:, g * 512:(g + 1) * 512], atb[:, h, :],
                                      at(SLOT[3 if h % 2 else 6] + g * 512, 512), start=True, stop=True).then_inc(dd["sup"], 1)
                w(dd["oscaled"], tot(1, 1))
                for h in range(H):
                    m = pe.transpose(ps[0][:, h * P:(h + 1) * P], xb[:, h, :], ident)
                m.then_inc(dd["otr"], 1)

            pe.wait_ge(ln_root, 1)
            pe.wait_ge(ln_mean, 1)
            with pe.Fori(0, PT) as t:
                delta(t, False, lambda s, v: wreg(pe, "pe", s, v), lambda per, k: t * per + k)
            delta(PT, True, lambda s, v: pe.wait_ge(s, v), lambda per, k: count_s(per, k))

            pe.wait_ge(dd["out"], TILES)
            with pe.Fori(0, H // 2) as i:
                for r in range(2):
                    wreg(pe, "pe", z_ld[r][0], i * 16 + (z_ld[r][1] + 16))
                    wreg(pe, "pe", z_act, 2 * i + r + 1)
                    project(ps[r], at(WR + r * D, KD, P), xnT).then_inc(z_mm[0], 1)
            pe.wait_ge(z_act, H + 2)
            pe.wait_ge(z_dve, H)
            oT = qT
            with pe.Fori(0, KD) as n:
                for j in range(2):
                    wreg(pe, "pe", mg_ld[j][0], n * 16 + (mg_ld[j][1] + 16))
                    wreg(pe, "pe", mg_sig, 2 * n + j + 1)
                    project(ps[j], at(WR + j * D, KD, P), xnT).then_inc(mg_mm[j][0], 1)
                wreg(pe, "pe", mg_ld[2][0], n * 16 + (mg_ld[2][1] + 16))
                wreg(pe, "pe", mg_out, n + 1)
                project(ps[2], at(WR + 2 * D, NC, P), cT, NC).then_inc(mg_mm[2][0], 1)
                project(ps[3], at(WR + 2 * D + NC * P, NC, P), oT, NC).then_inc(mg_mm[3][0], 1)

            pe.wait_ge(mg_out, KD + 1)
            with pe.Fori(0, NOC // 2) as i:
                for r in range(2):
                    wreg(pe, "pe", wo_ld[r][0], i * 16 + (wo_ld[r][1] + 16))
                    w = at(WR + r * KD * OCW, KD, OCW)
                    for t in range(TILES):
                        b = (r * TILES + t) % 5
                        wreg(pe, "pe", wo_add, (2 * i + r) * TILES + t + 1)
                        dst = ps[b // 2][:, (b % 2) * 512:(b % 2) * 512 + OCW]
                        for k in range(KD):
                            m = pe.matmul(dst, mT[:, k, t * P:(t + 1) * P], w[:, k, :], start=k == 0, stop=k == KD - 1)
                        m.then_inc(wo_mm, 1)

            pe.wait_ge(wo_add, NOC * TILES + 5)
            for t in range(TILES):
                pe.wait_ge(n2_done[0], n2_done[1] + t + 1)
                for half in range(2):
                    n = 2 * t + half
                    if n >= 4:
                        pe.wait_ge(n2_evac[0], n2_evac[1] + n - 3)
                    for k in range(8):
                        kk = half * 8 + k
                        m = pe.transpose(ps[n % 4][:, k * P:(k + 1) * P], xn2[:, t, kk * P:(kk + 1) * P], ident)
                    m.then_inc(n2_tr[0], 1)
            pe.wait_ge(n2_evac[0], n2_evac[1] + 2 * TILES)
            pe.wait_ge(key_ld[0], key_ld[1] + 16)
            keys_view = keyT
            with pe.Fori(0, HP // 2) as i:
                for r in range(2):
                    wreg(pe, "pe", wq_ld[r][0], i * 16 + (wq_ld[r][1] + 16))
                    wreg(pe, "pe", q_evac, 2 * i + r + 1)
                    project(ps[r], at(WR + r * D, KD, P), xn2T).then_inc(q_mm, 1)
                    wreg(pe, "pe", q_evac, 2 * i + r + 2)
                    wreg(pe, "pe", s_evac, 2 * i + r + 1)
                    for t in range(TILES):
                        m = pe.matmul(ps[2 + r][:, t * P:(t + 1) * P], at(QH, T)[:, t * P:(t + 1) * P],
                                      keys_view[:, bass.ds(2 * i + r, 1), :].rearrange("p a n -> p (a n)"), start=True, stop=True)
                    m.then_inc(s_mm, 1)

        @block.scalar
        def _(act):
            link = Link(act, "act", a_link)
            act.wait_ge(ready0, 1)
            for t in range(TILES):
                act.wait_ge(ld_x[t], 16)
                link(act.activation(at(CT, D), xin[:, t, :], ACT.Square, accum_out=small[:, t:t + 1]))
                act.sem_inc(sumsq, 1)
            act.wait_ge(msq, 1)
            act.activation(small[:, 16:16 + TILES], small[:, 8:8 + TILES], ACT.Sqrt).then_inc(root, 1)
            act.wait_ge(ba_mm, 1)
            ba = ps[3][:, 0:TILES * 2 * H].rearrange("p (t c) -> p t c", t=TILES)
            act.wait_ge(ba_dve, 1)
            link(act.activation(beta[:], ba[:, :, 0:H], ACT.Sigmoid))
            t1 = small[:, 72:112]
            link(act.activation(t1, small[:, 32:72], ACT.Abs))
            link(act.activation(t1, t1, ACT.Exp, scale=-1.0))
            link(act.activation(t1, t1, ACT.Ln, bias=1.0))
            link(act.activation(small[:, 112:120], pcol("a_log", 0, H), ACT.Exp))
            act.sem_inc(ba_act, 1)

            act.sem_inc(silu_done["v"], 1)
            act.sem_inc(norm_root["q"], 1)
            act.sem_inc(norm_root["k"], 1)
            with act.Fori(0, NC) as c:
                for i, kd in enumerate("qkv"):
                    wreg(act, "act", mm[kd], c + 1)
                    wreg(act, "act", conv_done[kd], c + 1)
                    wreg(act, "act", stage_done[kd], c + 1)
                    src = ps[PSK[kd]]
                    act.activation(qpad(kd)[:, DCW - 1:DCW - 1 + NP_TOK], src[:, 0:NP_TOK], ACT.Copy)
                    act.activation(seg(qpad(kd), NT + DCW - 1, DCW - 1)[:, :, DCW - 1:],
                                   src[:, NP_TOK:T].rearrange("p (b w) -> p b w", b=NB), ACT.Copy).then_inc(evac[kd], 1)
                    dst = {"q": QT, "k": KT, "v": VT}[kd]
                    full = at(dst, H, T)[:, bass.ds(c, 1), :].rearrange("p a n -> p (a n)")
                    wreg(act, "act", conv_done[kd], c + 2)
                    cv = at(QACC, QPAD)
                    act.activation(full[:, 0:NP_TOK], cv[:, 0:NP_TOK], ACT.Silu)
                    act.activation(full[:, NP_TOK:T].rearrange("p (b w) -> p b w", b=NB),
                                   seg(cv, NT + DCW - 1, DCW - 1)[:, :, 0:NT], ACT.Silu).then_inc(silu_done[kd], 1)
                    if kd != "v":
                        wreg(act, "act", silu_done[kd], c + 1)
                        act.activation(at(SQ + i * T, T), full, ACT.Square).then_inc(sq_done[kd], 1)
                wreg(act, "act", mm["gate"], c + 1)
                wreg(act, "act", glu_done, c + 1)
                act.activation(at(SIG, T), ps[0][:, 0:T], ACT.Sigmoid).then_inc(evac["gate"], 1)
                for i, kd in enumerate("qk"):
                    wreg(act, "act", mm_sum[kd], c + 1)
                    wreg(act, "act", norm_done["q" if kd == "k" else "k"], c + (2 if kd == "k" else 1))
                    act.activation(at(RT, T), ps[3 if kd == "q" else 2][:, 0:T], ACT.Sqrt, bias=epsc[:, 0:1]).then_inc(norm_root[kd], 1)
                wreg(act, "act", cconv_done, c + 2)
                cvc = at(CACC, CPAD)
                fullc = cT[:, bass.ds(c, 1), :].rearrange("p a n -> p (a n)")
                act.activation(fullc[:, 0:NP_TOK], cvc[:, 0:NP_TOK], ACT.Identity, bias=par[:, bass.ds(c + PCOLS["conv_b"][0], 1)])
                act.activation(fullc[:, NP_TOK:T].rearrange("p (b w) -> p b w", b=NB),
                               seg(cvc, NT + CW - 1, CW - 1)[:, :, 0:NT], ACT.Identity, bias=par[:, bass.ds(c + PCOLS["conv_b"][0], 1)]).then_inc(cbias_done, 1)

            for kd in "qkv":
                act.wait_ge(stage_done[kd], NC + 1)
            act.wait_ge(ln_sum, 1)
            act.wait_ge(norm_done["k"], NC + 1)
            act.activation(at(LMEAN, T), ps[0][:, 0:T], ACT.Copy, scale=1.0 / CONV).then_inc(ln_mean, 1)
            act.wait_ge(ln_cent, 1)
            for c in range(NC):
                if c >= 2:
                    act.wait_ge(ln_sqmm, c - 1)
                act.activation(at(LSQ + (c % 2) * T, T), cT[:, c, :], ACT.Square).then_inc(ln_sq, 1)
            act.wait_ge(ln_sqmm, NC)
            act.activation(at(LMEAN, T), ps[1][:, 0:T], ACT.Sqrt, bias=epsc[:, 0:1], scale=1.0 / CONV).then_inc(ln_root, 1)
            act.wait_ge(ln_scaled, 1)
            for c in range(NC):
                act.activation(cT[:, c, :], cT[:, c, :], ACT.Silu, bias=pcol("ln_b", c), scale=pcol("ln_g", c)).then_inc(ln_out, 1)

            def delta(t, streams, w, tot, tile):
                lev = 4 if streams else LEVELS
                last_r = ps8(0)
                for dst, src in ((kc, kT), (qc, qT), (vc, vT)):
                    m = act.activation(dst, src[:, :, tile], ACT.Copy)
                m.then_inc(dd["copied"], 1)
                w(dd["gexp_in"], tot(1, 1))
                act.activation(smalld[:, 32:48], smalld[:, 16:32], ACT.Exp).then_inc(dd["gexp"], 1)
                w(dd["rows"], tot(4, 2))
                if streams:
                    act.activation(smalld[:, 64:128].rearrange("p (h b) -> p h b", h=H),
                                   last_r[:, :, NT - 1::NT], ACT.Exp).then_inc(dd["grow"], 1)
                else:
                    act.activation(smalld[:, 64:72], last_r[:, :, P - 1:P].rearrange("p h a -> p (h a)"), ACT.Exp).then_inc(dd["grow"], 1)
                w(dd["ediff"], tot(1, 1))
                act.activation(eb, eb, ACT.Exp).then_inc(dd["eexp"], 1)
                for l in range(lev):
                    for g in range(2):
                        w(dd["x"], tot(2 * lev, 2 * l + g + 1))
                        if l:
                            w(dd["tx"], tot(4 * lev - 2, 4 * l))
                        else:
                            w(dd["at"], tot(2, 2))
                        act.activation(xb[:, 4 * g:4 * g + 4, :], ps8(1)[:, 4 * g:4 * g + 4, :], ACT.Copy).then_inc(dd["xc"], 1)
                if streams:
                    for j in range(2):
                        act.wait_ge(dd["ksT"], j + 1)
                        act.activation(eb if j == 0 else tb, ps8(1 + j), ACT.Copy).then_inc(dd["ksc"], 1)
                w(dd["dl"], tot(1, 1))
                act.activation(atl, ps8(3), ACT.Copy).then_inc(dd["dlc"], 1)
                w(dd["oss"], tot(1, 1))
                act.activation(smalld[:, 144:152], smalld[:, 136:144], ACT.Sqrt).then_inc(dd["oroot"], 1)
                w(dd["otr"], tot(1, 1))
                act.activation(qT[:, :, tile], ps8(0), ACT.Copy).then_inc(dd["out"], 1)

            act.wait_ge(ln_out, NC)
            act.wait_ge(ready0, 2)
            act.wait_ge(cstate_out, 32 * NC)
            with act.Fori(0, PT) as t:
                delta(t, False, lambda s, v: wreg(act, "act", s, v), lambda per, k: t * per + k, bass.ds(t * P, P))
            delta(PT, True, lambda s, v: act.wait_ge(s, v), lambda per, k: count_s(per, k), slice(PT * P, T))

            act.sem_inc(z_act, 2)
            with act.Fori(0, H // 2) as i:
                for r in range(2):
                    wreg(act, "act", z_mm[0], 2 * i + (r + 1 + z_mm[1]))
                    act.activation(at(TM + r * T, T), ps[r][:, 0:T], ACT.Silu).then_inc(z_act, 1)
                wreg(act, "act", z_dve, 2 * i + 2)
            act.sem_inc(mg_sig, 2)
            with act.Fori(0, KD) as n:
                for j in range(2):
                    wreg(act, "act", mg_mm[j][0], n + (mg_mm[j][1] + 1))
                    wreg(act, "act", mg_out, n + 1)
                    act.activation(at(TM + 2 * T + j * T, T), ps[j][:, 0:T], ACT.Sigmoid).then_inc(mg_sig, 1)

            act.wait_ge(wo_add, NOC * TILES + 5)
            link2 = Link(act, "act", a_link, base=link.n)
            for t in range(TILES):
                link2(act.activation(at(KT, D), x1[:, t, :], ACT.Square, accum_out=small[:, t:t + 1]))
                act.sem_inc(n2_sumsq[0], 1)
            act.wait_ge(n2_msq[0], n2_msq[1] + 1)
            act.activation(small[:, 16:16 + TILES], small[:, 8:8 + TILES], ACT.Sqrt).then_inc(n2_root[0], 1)
            act.sem_inc(q_evac, 1)
            act.sem_inc(s_evac, 1)
            with act.Fori(0, HP // 2) as i:
                for r in range(2):
                    wreg(act, "act", q_mm, 2 * i + r + 1)
                    wreg(act, "act", s_evac, 2 * i + r + 1)
                    act.activation(at(QH, T), ps[r][:, 0:T], ACT.Copy).then_inc(q_evac, 1)
                    wreg(act, "act", s_mm, 2 * i + r + 1)
                    wreg(act, "act", tk_done, 2 * i + r + 1)
                    act.activation(at(SC, T), ps[2 + r][:, 0:T], ACT.Copy).then_inc(s_evac, 1)
            for t in range(TILES):
                act.wait_ge(sel_pre, t + 1)
                act.activation(gate_all[:, t, :], gate_all[:, t, :], ACT.Exp).then_inc(sel_exp, 1)
            with act.Fori(0, TILES) as t:
                with act.Fori(0, NG) as g:
                    wreg(act, "act", hid_done, t * NG + g + 1)
                    act.activation(act_w[:], hid[:], ACT.Gelu_apprx_tanh).then_inc(gelu_done, 1)
                wreg(act, "act", fin_sq, t + 1)
                act.activation(small[:, 131:132], small[:, 130:131], ACT.Sqrt).then_inc(fin_root, 1)

        @block.vector
        def _(v):
            v.memset(epsc[:], EPS)
            v.memset(at(pads["q"], DCW - 1), 0.0)
            v.memset(at(pads["k"], DCW - 1), 0.0)
            v.memset(at(pads["v"], DCW - 1), 0.0)
            v.memset(smalld[:], 0.0)
            v.memset(small[:], 0.0).then_inc(ready0, 1)
            link = Link(v, "dve", d_link)
            v.wait_ge(sumsq, TILES)
            link(v.tensor_scalar(small[:, 8:8 + TILES], small[:, 0:TILES], 1.0 / D, EPS, ALU.mult, ALU.add))
            v.sem_inc(msq, 1)
            v.wait_ge(root, 1)
            link(v.reciprocal(small[:, 24:24 + TILES], small[:, 16:16 + TILES]))
            v.wait_ge(ld_par, 64)
            mixg = pcol("mix_g", 0, KD)

            def evac_x(n):
                t, half = n // 2, n % 2
                v.wait_ge(xtr, n + 1)
                v.tensor_tensor(xnT[:, 8 * half:8 * half + 8, t * P:(t + 1) * P], ps8(n % 4),
                                mixg[:, 8 * half:8 * half + 8].unsqueeze(2).to_broadcast([P, 8, P]), ALU.mult).then_inc(xevac, 1)
            for t in range(TILES):
                v.tensor_scalar(xin[:, t, :], xin[:, t, :], small[:, 24 + t:25 + t], None, ALU.mult).then_inc(xscaled, 1)
                if t:
                    evac_x(2 * t - 2)
                    evac_x(2 * t - 1)
            evac_x(2 * TILES - 2)
            evac_x(2 * TILES - 1)
            v.wait_ge(ba_mm, 1)
            ba = ps[3][:, 0:TILES * 2 * H].rearrange("p (t c) -> p t c", t=TILES)
            ax = small[:, 32:72].rearrange("p (t h) -> p t h", t=TILES)
            link(v.tensor_tensor(ax, ba[:, :, H:2 * H], pcol("dt_bias", 0, H).unsqueeze(1).to_broadcast([P, TILES, H]), ALU.add))
            v.sem_inc(ba_dve, 1)
            v.wait_ge(ba_act, 1)
            link(v.scalar_tensor_tensor(ax, ax, 0.0, small[:, 72:112].rearrange("p (t h) -> p t h", t=TILES), ALU.max, ALU.add))
            link(v.scalar_tensor_tensor(glog[:], ax, -1.0, small[:, 112:120].unsqueeze(1).to_broadcast([P, TILES, H]), ALU.mult, ALU.mult))
            v.memset(at(CPB, CW - 1), 0.0)
            for s in (*conv_done.values(), glu_done, cconv_done):
                v.sem_inc(s, 1)
            for s in norm_done.values():
                v.sem_inc(s, 1)

            NTAP = DCW * 3 + CW
            with v.Fori(0, NC) as c:
                n = [0]

                def step(ins):
                    n[0] += 1
                    ins.then_inc(dve_loop, 1)
                    wreg(v, "dve", dve_loop, c * NL + n[0])
                NL = 3 * (DCW - 1) + 2 + CW - 1
                for i, kd in enumerate("qkv"):
                    wreg(v, "dve", evac[kd], c + 1)
                    wreg(v, "dve", prefix_done[kd], c + 1)
                    wreg(v, "dve", silu_done["qkv"[i - 1]], c + 1)
                    pad, dst = at(pads[kd], QPAD), at(QACC, QLEN)
                    for j in range(DCW):
                        wc = par[:, bass.ds(c * DCW + (PCOLS["dconv_w"][0] + i * H * DCW + j), 1)]
                        if j == 0:
                            step(v.tensor_scalar(dst, pad[:, j:j + QLEN], wc, None, ALU.mult))
                        else:
                            ins = v.scalar_tensor_tensor(dst, pad[:, j:j + QLEN], wc, dst, ALU.mult, ALU.add)
                            if j < DCW - 1:
                                step(ins)
                            else:
                                ins.then_inc(conv_done[kd], 1)
                wreg(v, "dve", mm["glu"], c + 1)
                wreg(v, "dve", evac["gate"], c + 1)
                wreg(v, "dve", prefix_done["c"], c * 16 + 16)
                cp, sg = at(CPB, CPAD), at(SIG, T)
                v.tensor_tensor(cp[:, CW - 1:CW - 1 + NP_TOK], ps[1][:, 0:NP_TOK], sg[:, 0:NP_TOK], ALU.mult)
                v.tensor_tensor(seg(cp, NT + CW - 1, CW - 1)[:, :, CW - 1:], ps[1][:, NP_TOK:T].rearrange("p (b w) -> p b w", b=NB),
                                sg[:, NP_TOK:T].rearrange("p (b w) -> p b w", b=NB), ALU.mult).then_inc(glu_done, 1)
                for i, kd in enumerate("qk"):
                    wreg(v, "dve", norm_root[kd], c + 2)
                    full = at(QT if kd == "q" else KT, H, T)[:, bass.ds(c, 1), :].rearrange("p a n -> p (a n)")
                    step(v.reciprocal(at(RT, T), at(RT, T)))
                    v.scalar_tensor_tensor(full, full, float(P) ** -0.5 if kd == "q" else 1.0, at(RT, T), ALU.mult, ALU.mult).then_inc(norm_done[kd], 1)
                wreg(v, "dve", glu_done, c + 2)
                dst = at(CACC, CLEN)
                for j in range(CW):
                    wc = par[:, bass.ds(c * CW + (PCOLS["conv_w"][0] + j), 1)]
                    if j == 0:
                        step(v.tensor_scalar(dst, cp[:, j:j + CLEN], wc, None, ALU.mult))
                    else:
                        ins = v.scalar_tensor_tensor(dst, cp[:, j:j + CLEN], wc, dst, ALU.mult, ALU.add)
                        if j < CW - 1:
                            step(ins)
                        else:
                            ins.then_inc(cconv_done, 1)
                assert n[0] == NL, (n[0], NL)
                wreg(v, "dve", cbias_done, c + 1)

            v.wait_ge(ln_mean, 1)
            mean = at(LMEAN, T).unsqueeze(1).to_broadcast([P, NC, T])
            v.tensor_tensor(cT, cT, mean, ALU.subtract).then_inc(ln_cent, 1)
            v.wait_ge(ln_root, 1)
            link(v.reciprocal(at(LMEAN, T), at(LMEAN, T)))
            v.tensor_tensor(cT, cT, mean, ALU.mult).then_inc(ln_scaled, 1)

            def bc(col):
                return col.unsqueeze(2).to_broadcast([P, H, P])

            def bm(mat, n=H):
                return mat.unsqueeze(1).to_broadcast([P, n, P])

            def delta(t, streams, w, tot, gsrc, bsrc, lk):
                tri = cst[:, TRI_S if streams else TRI_P, :]
                lev = 4 if streams else LEVELS
                gcur, bcur = smalld[:, 0:H], smalld[:, 8:8 + H]
                lk(v.tensor_copy(gcur, gsrc))
                lk(v.tensor_copy(bcur, bsrc))
                v.sem_inc(dd["init"], 1)
                w(dd["copied"], tot(1, 1))
                v.tensor_tensor(eb, bm(tri), bc(gcur), ALU.mult).then_inc(dd["trig"], 1)
                v.tensor_tensor(xb, bm(ident), bc(bcur), ALU.mult).then_inc(dd["trig"], 1)
                w(dd["gsum"], tot(1, 1))
                G, toend = smalld[:, 16:24], smalld[:, 24:32]
                lk(v.tensor_copy(smalld[:, 48:64], ps[3][:, 0:16]))
                lk(v.tensor_copy(G, smalld[:, 48:56]))
                lk(v.tensor_tensor(toend, smalld[:, 56:64], smalld[:, 48:56], ALU.subtract))
                v.sem_inc(dd["gexp_in"], 1)
                w(dd["rows"], tot(4, 4))
                w(dd["grow"], tot(1, 1))
                lk(v.tensor_tensor(eb, ps8(0), bc(smalld[:, 48:56]), ALU.subtract))
                v.tensor_scalar(eb, eb, 0.0, None, ALU.min).then_inc(dd["ediff"], 1)
                w(dd["eexp"], tot(1, 1))
                lk(v.tensor_tensor(eb, eb, bm(tri), ALU.mult))
                w(dd["kk"], tot(1, 1))
                lk(v.tensor_tensor(atb, eb, ps8(2), ALU.mult))
                v.tensor_tensor(atb, atb, ps8(1), ALU.mult).then_inc(dd["at"], 1)
                w(dd["qk"], tot(1, 1))
                v.tensor_tensor(qkd, eb, ps8(3), ALU.mult).then_inc(dd["at"], 1)
                lk(v.tensor_copy(tb, bm(ident)))
                v.tensor_copy(ttb, bm(ident)).then_inc(dd["tt"], 1)
                w(dd["at"], tot(2, 2))
                w(dd["gexp"], tot(1, 1))
                w(dd["vtr"], tot(1, 1))
                v.tensor_tensor(vc, ps8(0), bc(bcur), ALU.mult).then_inc(dd["vb"], 1)
                lk(v.tensor_tensor(smalld[:, 128:136], bcur, smalld[:, 32:40], ALU.mult))
                for g in range(2):
                    hs = slice(4 * g, 4 * g + 4)
                    v.tensor_tensor(atl[:, hs, :], atb[:, hs, :], bm(cst[:, LEV0, :], 4), ALU.mult).then_inc(dd["atl"], 1)
                for l in range(lev):
                    for g in range(2):
                        hs = slice(4 * g, 4 * g + 4)
                        if l < lev - 1:
                            w(dd["x"], tot(2 * lev, 2 * l + g + 1))
                            v.tensor_tensor(atl[:, hs, :], atb[:, hs, :], bm(cst[:, LEV0 + l + 1, :], 4), ALU.mult).then_inc(dd["atl"], 1)
                    if l == 0:
                        w(dd["tt"], tot(2 * lev + 1, 1))
                    for g in range(2):
                        hs = slice(4 * g, 4 * g + 4)
                        if l < lev - 1:
                            w(dd["tx"], tot(4 * lev - 2, 4 * l + 2 * g + 1))
                            if l:
                                w(dd["t"], tot(2 * lev - 2, 2 * l - 1 + g))
                            v.tensor_tensor(tb[:, hs, :], tb[:, hs, :], ps8(2)[:, hs, :], ALU.subtract).then_inc(dd["t"], 1)
                            w(dd["tx"], tot(4 * lev - 2, 4 * l + 2 * g + 2))
                        else:
                            w(dd["tx"], tot(4 * lev - 2, 4 * l + g + 1))
                        if l:
                            w(dd["tt"], tot(2 * lev + 1, 2 * l + g))
                        v.tensor_tensor(ttb[:, hs, :], ttb[:, hs, :], ps8(3)[:, hs, :], ALU.subtract).then_inc(dd["tt"], 1)
                w(dd["ktr"], tot(1, 1))
                v.tensor_tensor(atb, ps8(0), bc(smalld[:, 40:48]), ALU.mult).then_inc(dd["kd"], 1)
                w(dd["ks"], tot(2, 1))
                w(dd["vb"], tot(1, 1))
                w(dd["tt"], tot(2 * lev + 1, 2 * lev + 1))
                if streams:
                    w(dd["ks"], tot(2, 2))
                lk(v.tensor_tensor(tb, ps8(1), bc(smalld[:, 128:136]), ALU.mult))
                v.tensor_tensor(vc, vc, tb, ALU.subtract).then_inc(dd["r2"], 1)
                w(dd["ks"], tot(2, 2))
                lk(v.tensor_tensor(xb, ps8(2), bc(smalld[:, 32:40]), ALU.mult))
                w(dd["o2"], tot(1, 1))
                lk(v.tensor_tensor(xb, xb, ps8(1), ALU.add))
                w(dd["r2"], tot(1, 1))
                lk(v.tensor_tensor(eb, xb, xb, ALU.mult))
                lk(v.tensor_reduce(smalld[:, 152:160], eb, X, ALU.add))
                lk(v.tensor_scalar(smalld[:, 136:144], smalld[:, 152:160], 1.0 / P, EPS, ALU.mult, ALU.add))
                v.sem_inc(dd["oss"], 1)
                w(dd["oroot"], tot(1, 1))
                lk(v.reciprocal(smalld[:, 160:168], smalld[:, 144:152]))
                v.tensor_tensor(xb, xb, bc(smalld[:, 160:168]), ALU.mult).then_inc(dd["oscaled"], 1)
                if not streams:
                    w(dd["sup"], tot(1, 1))
                    lk(v.tensor_tensor(st_p, st_p, bc(smalld[:, 64:72]), ALU.mult))
                    v.tensor_tensor(st_p, st_p, ps8(3), ALU.add).then_inc(dd["snew"], 2)
                    w(dd["snew"], tot(2, 2))
                else:
                    bmask = cst[:, BLK_S, :]
                    w(dd["dlc"], tot(1, 1))
                    w(dd["oscaled"], tot(1, 1))
                    for h in range(H):
                        dmb = at(SLOT[3 if h % 2 else 6], NB, P)
                        if h >= 2:
                            v.wait_ge(dd["sup"], PT + 2 * (h - 1))
                        v.tensor_tensor(dmb, atl[:, h, :].unsqueeze(1).to_broadcast([P, NB, P]),
                                        bmask[:, NT - 1::NT].unsqueeze(2).to_broadcast([P, NB, P]), ALU.mult).then_inc(dd["dm"], 1)
                        glb = smalld[:, 64 + NB * h:64 + NB * h + NB].unsqueeze(2).to_broadcast([P, NB, P])
                        lk(v.tensor_tensor(st_s[:, h, :, :], st_s[:, h, :, :], glb, ALU.mult))
                        v.wait_ge(dd["sup"], PT + 2 * h + 2)
                        v.tensor_tensor(st_s[:, h, :, :], st_s[:, h, :, :], ps8(3), ALU.add).then_inc(dd["snew"], 2)

            v.wait_ge(ln_out, NC)
            link(v.memset(st_p, 0.0))
            v.sem_inc(ready0, 1)
            with v.Fori(0, PT) as t:
                NLK = 18
                lk = Link(v, "dve", dd_link_d, base=t * NLK, loop=True)
                delta(t, False, lambda s, val: wreg(v, "dve", s, val), lambda per, k: t * per + k,
                      glog[:, bass.ds(t, 1), :].rearrange("p a h -> p (a h)"), beta[:, bass.ds(t, 1), :].rearrange("p a h -> p (a h)"), lk)
                assert lk.n == NLK, lk.n
            delta(PT, True, lambda s, val: v.wait_ge(s, val), lambda per, k: count_s(per, k), glog[:, PT, :], beta[:, PT, :],
                  Link(v, "dve", dd_link_d, base=PT * NLK))

            oT = qT
            v.wait_ge(dd["out"], TILES)
            with v.Fori(0, H // 2) as i:
                for r in range(2):
                    wreg(v, "dve", z_act, 2 * i + r + 3)
                    dst = oT[:, bass.ds(2 * i + r, 1), :].rearrange("p a n -> p (a n)")
                    v.scalar_tensor_tensor(dst, at(TM + r * T, T), pcol("dn_g"), dst, ALU.mult, ALU.mult).then_inc(z_dve, 1)
            v.sem_inc(mg_out, 1)
            with v.Fori(0, KD) as n:
                s0, s1 = at(TM + 2 * T, T), at(TM + 3 * T, T)
                wreg(v, "dve", mg_sig, 2 * n + 4)
                wreg(v, "dve", mg_mm[2][0], n + (mg_mm[2][1] + 1))
                v.tensor_tensor(s0, s0, ps[2][:, 0:T], ALU.mult).then_inc(mg_t, 1)
                wreg(v, "dve", mg_mm[3][0], n + (mg_mm[3][1] + 1))
                v.tensor_tensor(s1, s1, ps[3][:, 0:T], ALU.mult).then_inc(mg_t, 1)
                wreg(v, "dve", mg_t, 2 * n + 2)
                v.tensor_tensor(mT[:, bass.ds(n, 1), :].rearrange("p a n -> p (a n)"), s0, s1, ALU.add).then_inc(mg_out, 1)
            v.sem_inc(wo_add, 5)
            v.wait_ge(xr_ld[0], xr_ld[1] + 32)
            with v.Fori(0, NOC // 2) as i:
                for r in range(2):
                    for t in range(TILES):
                        b = (r * TILES + t) % 5
                        wreg(v, "dve", wo_mm, (2 * i + r) * TILES + t + 1)
                        dst = x1[:, t, bass.ds((2 * i + r) * OCW, OCW)]
                        v.tensor_tensor(dst, dst, ps[b // 2][:, (b % 2) * 512:(b % 2) * 512 + OCW], ALU.add).then_inc(wo_add, 1)
            v.wait_ge(n2_sumsq[0], n2_sumsq[1] + TILES)
            link(v.tensor_scalar(small[:, 8:8 + TILES], small[:, 0:TILES], 1.0 / D, EPS, ALU.mult, ALU.add))
            v.sem_inc(n2_msq[0], 1)
            v.wait_ge(n2_root[0], n2_root[1] + 1)
            link(v.reciprocal(small[:, 24:24 + TILES], small[:, 16:16 + TILES]))
            v.wait_ge(g_ld[0], g_ld[1] + 16)

            def evac_n2(n):
                t, half = n // 2, n % 2
                v.wait_ge(n2_tr[0], n2_tr[1] + n + 1)
                v.tensor_copy(xn2T[:, 8 * half:8 * half + 8, t * P:(t + 1) * P], ps8(n % 4)).then_inc(n2_evac[0], 1)
            for t in range(TILES):
                v.scalar_tensor_tensor(xn2[:, t, :], x1[:, t, :], small[:, 24 + t:25 + t], at(WR + 4 * D, D), ALU.mult, ALU.mult).then_inc(n2_done[0], 1)
                if t:
                    evac_n2(2 * t - 2)
                    evac_n2(2 * t - 1)
            evac_n2(2 * TILES - 2)
            evac_n2(2 * TILES - 1)
            v.sem_inc(tk_done, 1)
            NTK = 3 * TILES + 2
            with v.Fori(0, HP) as j:
                n = [0]

                def tk(ins):
                    n[0] += 1
                    ins.then_inc(tk_link, 1)
                wreg(v, "dve", s_evac, j + 2)
                sc, sc2 = at(SC, TILES, P), at(SC2, TILES, P)
                top = topbuf
                for t in range(TILES):
                    tk(v.max(top[:, t, 0:8], sc[:, t, :]))
                wreg(v, "dve", tk_link, j * NTK + TILES)
                for t in range(TILES):
                    v.max_index(itop_u[:, t, 0:8], top[:, t, 0:8], sc[:, t, :])
                    tk(v.match_replace(sc2[:, t, :], top[:, t, 0:8], sc[:, t, :], -3.0e38))
                wreg(v, "dve", tk_link, j * NTK + 2 * TILES)
                for t in range(TILES):
                    tk(v.max(top[:, t, 8:16], sc2[:, t, :]))
                wreg(v, "dve", tk_link, j * NTK + 3 * TILES)
                for t in range(TILES):
                    ins = v.max_index(itop_u[:, t, 8:16], top[:, t, 8:16], sc2[:, t, :])
                tk(ins)
                wreg(v, "dve", tk_link, j * NTK + 3 * TILES + 1)
                v.tensor_copy(stop_[:, :, bass.ds(j * TOPK, TOPK)], top)
                tk(v.tensor_copy(itop[:, :, bass.ds(j * TOPK, TOPK)], itop_u))
                wreg(v, "dve", tk_link, j * NTK + NTK)
                v.sem_inc(tk_done, 1)
            sl = Link(v, "dve", sel_link)
            v.wait_ge(iota_done, 1)
            cand = at(KT, PH, TOPK * TOPK)
            cand2 = at(KT + 2048, PH, TOPK * TOPK)
            oh = at(KT + 4096, PH * TOPK, TOPK)
            oh4 = at(KT + 4096, PH, TOPK, TOPK)
            val = at(KT + 6144, PH * TOPK)
            posf = at(KT + 6144 + 128, 2, PH * TOPK)
            got = at(KT + 6144 + 384, 2, PH * TOPK)
            stf = at(KT + 6144 + 640, PH, TOPK)
            red = at(KT + 6144 + 768, PH)
            posi = posu2
            for t in range(TILES):
                s4 = stop_[:, t, :].rearrange("p (h q k) -> p h q k", h=PH, q=2)
                i4 = itop[:, t, :].rearrange("p (h q k) -> p h q k", h=PH, q=2)
                sl(v.tensor_tensor(cand.rearrange("p h (a b) -> p h a b", a=TOPK), s4[:, :, 0, :].unsqueeze(3).to_broadcast([P, PH, TOPK, TOPK]),
                                   s4[:, :, 1, :].unsqueeze(2).to_broadcast([P, PH, TOPK, TOPK]), ALU.add))
                pu = posu.rearrange("p (h k) -> p h k", h=PH)
                for h in range(PH):
                    ins = v.max(stf[:, h, 0:8], cand[:, h, :])
                sl(ins)
                for h in range(PH):
                    v.max_index(pu[:, h, 0:8], stf[:, h, 0:8], cand[:, h, :])
                    ins = v.match_replace(cand2[:, h, :], stf[:, h, 0:8], cand[:, h, :], -3.0e38)
                sl(ins)
                for h in range(PH):
                    ins = v.max(stf[:, h, 8:16], cand2[:, h, :])
                sl(ins)
                for h in range(PH):
                    ins = v.max_index(pu[:, h, 8:16], stf[:, h, 8:16], cand2[:, h, :])
                sl(ins)
                gt = gate_all[:, t, :].rearrange("p (h k) -> p h k", h=PH)
                v.tensor_tensor(gt, stf, stf[:, :, 0:1].to_broadcast([P, PH, TOPK]), ALU.subtract).then_inc(sel_pre, 1)
                v.tensor_scalar(posi[:, 0, :], posu, 4, None, ALU.logical_shift_right)
                sl(v.tensor_scalar(posi[:, 1, :], posu, 15, None, ALU.bitwise_and))
                sl(v.tensor_copy(posf, posi))
                for q in range(2):
                    sl(v.tensor_tensor(oh, iota16[:].unsqueeze(1).to_broadcast([P, PH * TOPK, TOPK]),
                                       posf[:, q, :].unsqueeze(2).to_broadcast([P, PH * TOPK, TOPK]), ALU.is_equal))
                    for h in range(PH):
                        ins = v.tensor_tensor(oh4[:, h], oh4[:, h], i4[:, h, q, :].unsqueeze(1).to_broadcast([P, TOPK, TOPK]), ALU.mult)
                    sl(ins)
                    sl(v.tensor_reduce(got[:, q, :], oh, X, ALU.add))
                sl(v.scalar_tensor_tensor(val, got[:, 0, :], float(NK), got[:, 1, :], ALU.mult, ALU.add))
                sl(v.tensor_copy(idx_all[:, t, :], val))
                v.wait_ge(sel_exp, t + 1)
                sl(v.tensor_reduce(red, gt, X, ALU.add))
                sl(v.reciprocal(red, red))
                sl(v.tensor_tensor(gt, gt, red.unsqueeze(2).to_broadcast([P, PH, TOPK]), ALU.mult))
            v.sem_inc(ex_begin, 1)
            v.sem_inc(u_used, RING)
            v.sem_inc(v_used, RING)
            with v.Fori(0, TILES) as t:
                v.tensor_copy(xcur, xn2[:, bass.ds(t, 1), :].rearrange("p a n -> p (a n)")).then_inc(ex_tile, 1)
                v.tensor_copy(acc, x1[:, bass.ds(t, 1), :].rearrange("p a n -> p (a n)")).then_inc(ex_tile, 1)
                wreg(v, "dve", ex_tile, 2 * t + 2)
                with v.Fori(0, NG) as g:
                    it = t * NG + g
                    v.tensor_copy(gcol[:], gate_all[:, bass.ds(t, 1), bass.ds(g * RING, RING)].rearrange("p a n -> p (a n)")).then_inc(coef_done, 1)
                    for r in range(RING):
                        wreg(v, "dve", u_ld[r][0], it * 16 + (u_ld[r][1] + 16))
                        v.tensor_tensor_reduce(out=urow[r], in0=urow[r], in1=xcur, scale=1.0, scalar=0.0, op0=ALU.mult, op1=ALU.add,
                                               accum_out=hid[:, r:r + 1]).then_inc(u_used, 1)
                    wreg(v, "dve", u_used, it * RING + 2 * RING)
                    v.sem_inc(hid_done, 1)
                    wreg(v, "dve", gelu_done, it + 1)
                    wreg(v, "dve", coef_done, 2 * it + 1)
                    v.tensor_tensor(act_w2[:], act_w[:], gcol[:], ALU.mult).then_inc(coef_done, 1)
                    wreg(v, "dve", coef_done, 2 * it + 2)
                    for r in range(RING):
                        wreg(v, "dve", v_ld[r], it * 16 + 16)
                        v.scalar_tensor_tensor(acc, vrow[r], act_w2[:, r:r + 1], acc, ALU.mult, ALU.add).then_inc(v_used, 1)
                        wreg(v, "dve", v_used, it * RING + RING + r + 1)
                v.tensor_tensor_reduce(out=at(JUNK, D), in0=acc, in1=acc, scale=1.0 / D, scalar=EPS, op0=ALU.mult, op1=ALU.add,
                                       accum_out=small[:, 130:131]).then_inc(fin_ms, 1)
                wreg(v, "dve", fin_ms, 2 * t + 1)
                v.sem_inc(fin_sq, 1)
                wreg(v, "dve", fin_root, t + 1)
                v.reciprocal(small[:, 132:133], small[:, 131:132]).then_inc(fin_ms, 1)
                wreg(v, "dve", fin_ms, 2 * t + 2)
                v.wait_ge(fg_ld[0], fg_ld[1] + 16)
                wreg(v, "dve", y_free, t + 1)
                v.scalar_tensor_tensor(yout, acc, small[:, 132:133], fing, ALU.mult, ALU.mult).then_inc(fin_y, 1)
                wreg(v, "dve", fin_y, t + 1)

        @block.gpsimd
        def _(pool):
            pool.iota(iota_i[:], pattern=[[1, TOPK]], base=0, channel_multiplier=0).then_inc(p_link, 1)
            pool.wait_ge(p_link, 1)
            pool.tensor_copy(iota16[:], iota_i[:]).then_inc(iota_done, 1)
            pool.wait_ge(ld_par, 64)
            for s in stage_done.values():
                pool.sem_inc(s, 1)
            pool.wait_ge(cconv_done, 1)
            with pool.Fori(0, NC) as c:
                for i, kd in enumerate("qkv"):
                    wreg(pool, "pool", conv_done[kd], c + 1)
                    sg = seg(qpad(kd), NT + DCW - 1, DCW - 1)
                    pool.tensor_copy(sg[:, :, 0:DCW - 1], dpre[:, bass.ds(c * NB + i * H * NB, NB), :]).then_inc(prefix_done[kd], 1)
                for i, kd in enumerate("qkv"):
                    wreg(pool, "pool", evac[kd], c + 1)
                    pool.tensor_copy(dnew_p[:, bass.ds(c + i * H, 1), :].rearrange("p a n -> p (a n)"), qpad(kd)[:, NP_TOK:NP_TOK + DCW - 1])
                    pool.tensor_copy(dnew_s[:, bass.ds(c * NB + i * H * NB, NB), :],
                                     seg(qpad(kd), NT + DCW - 1, DCW - 1)[:, :, NT:]).then_inc(stage_done[kd], 1)
                wreg(pool, "pool", cconv_done, c + 1)
                cp = at(CPB, CPAD)
                sg = seg(cp, NT + CW - 1, CW - 1)
                pool.dma_start(sg[:, :, 0:CW - 1], conv_prefix[bass.ds(c, 1)].rearrange("a p b n -> p (a b) n")).then_inc(prefix_done["c"], 16)
                wreg(pool, "pool", glu_done, c + 2)
                pool.dma_start(conv_new_p[bass.ds(c, 1)].rearrange("a p n -> p (a n)"), cp[:, NP_TOK:NP_TOK + CW - 1]).then_inc(cstate_out, 16)
                pool.dma_start(conv_new_s[bass.ds(c * NB, NB)].rearrange("b p n -> p b n"), sg[:, :, NT:]).then_inc(cstate_out, 16)
                wreg(pool, "pool", cstate_out, c * 32 + 32)
            pool.wait_ge(ex_begin, 1)
            with pool.Fori(0, TILES) as t:
                with pool.Fori(0, NG // 2) as g2:
                    for half in range(2):
                        it = t * NG + g2 * 2 + half
                        pool.tensor_copy(cur_idx[:, half, :], idx_all[:, bass.ds(t, 1), bass.ds((g2 * 2 + half) * RING, RING)]
                                         .rearrange("p a n -> p (a n)")).then_inc(idx_cur, 1)
                        wreg(pool, "pool", idx_cur, it + 1)
                        for table, rows, used, ld in ((peer_u, urow, u_used, [s for s, _ in u_ld]), (peer_v, vrow, v_used, v_ld)):
                            for r in range(RING):
                                wreg(pool, "pool", used, it * RING + r + 1)
                                pool.indirect_dma_start(out=rows[r], out_offset=None, in_=table,
                                                        in_offset=bass.IndirectOffsetOnAxis(ap=cur_idx[:, half, r:r + 1], axis=0)
                                                        ).then_inc(ld[r], 16)


def constant_matrices():
    import numpy as np
    i = np.arange(P)
    r, c = i[:, None], i[None, :]
    blk = (r // NT == c // NT)
    mats = [r == c, np.ones((P, P), bool), r <= c, (r <= c) & blk, blk]
    for l in range(LEVELS):
        s = 1 << l
        mats.append((r // (2 * s) == c // (2 * s)) & (r % (2 * s) < s) & (c % (2 * s) >= s))
    return np.ascontiguousarray(np.stack([m.astype(np.float32) for m in mats], 1))


def kernel(**inp):
    import numpy as np
    import concourse.bacc as bacc
    from concourse.bass_utils import run_bass_kernel_spmd as run

    a = {k: np.asarray(v) for k, v in inp.items()}

    def cols(v):
        return v.reshape(-1, P).T

    def tiles(w):
        k, n = w.shape
        return w.reshape(k // P, P, n // P, P).transpose(2, 1, 0, 3).reshape(n // P, P, k)

    w_in = a["w_in"][0]
    o = 2 * CONV + 3 * H * P
    w_glu, w_qkv, w_ba, w_z, w_g = (w_in[:, :2 * CONV], w_in[:, 2 * CONV:o], w_in[:, o:o + 2 * H],
                                    w_in[:, o + 2 * H:o + 2 * H + H * P], w_in[:, o + 2 * H + H * P:])
    tg, tq = tiles(w_glu), tiles(w_qkv)
    w_group = np.stack([tq[:H], tq[H:2 * H], tq[2 * H:], tg[NC:], tg[:NC]], 1).reshape(5 * NC, P, D)
    tgt, tp, to = tiles(w_g), tiles(a["conv_pw2"][0]), tiles(a["dn_w_o"][0])
    w_merge = np.stack([tgt[:KD], tgt[KD:], np.concatenate([tp, to], 2)], 1).reshape(3 * KD, P, D)
    cw = a["conv_dw_w"][0].T.reshape(NC, P, CW).transpose(1, 0, 2).reshape(P, -1)
    dw = a["dn_conv_w"][0].T.reshape(3 * H, P, DCW).transpose(1, 0, 2).reshape(P, -1)
    params = np.concatenate([cols(a["norm_mix_g"][0]), cw, cols(a["conv_dw_b"][0]), cols(a["conv_ln_g"][0]), cols(a["conv_ln_b"][0]),
                             dw, cols(a["dn_norm_g"][0]), np.broadcast_to(a["dn_dt_bias"][0], (P, H)),
                             np.broadcast_to(a["dn_a_log"][0], (P, H))], 1)
    ins = {
        "x_prompt": a["x_prompt"][0],
        "x_sample": a["x_sample"].reshape(P, D),
        "consts": constant_matrices(),
        "params": params,
        "conv_prefix": a["state_conformer_conv"][0].reshape(NB, CW - 1, NC, P).transpose(2, 3, 0, 1),
        "dconv_prefix": a["state_delta_conv"][0].reshape(NB, DCW - 1, 3 * H, P).transpose(3, 2, 0, 1).reshape(P, 3 * H * NB, DCW - 1),
        "state_in": a["state_delta"][0].transpose(2, 1, 0, 3).reshape(P, H * NB * P),
        "w_ba": w_ba.reshape(KD, P, 2 * H).transpose(1, 0, 2),
        "w_group": w_group,
        "w_z": tiles(w_z),
        "w_merge": w_merge,
        "w_out": a["w_out"][0].reshape(KD, P, NOC, OCW).transpose(2, 1, 0, 3).reshape(NOC, P, KD * OCW),
        "w_q": tiles(a["peer_w_q"][0]),
        "keys": a["peer_sub_keys"][0].reshape(HP, NK, P).transpose(2, 0, 1).reshape(P, HP * NK),
        "ffn_g": np.broadcast_to(a["norm_ffn_g"][0], (P, D)),
        "final_g": np.broadcast_to(a["norm_final_g"], (P, D)),
        "peer_u": a["peer_u"][0],
        "peer_v": a["peer_v"][0],
    }
    outs = {
        "y_prompt": (NP_TOK, D), "y_sample": (P, D),
        "conv_new_p": (NC, P, CW - 1), "dconv_new_p": (P, 3 * H, DCW - 1), "state_new_p": (P, H * P),
        "conv_new_s": (NC * NB, P, CW - 1), "dconv_new_s": (P, 3 * H * NB, DCW - 1), "state_new_s": (P, H * NB * P),
    }
    nc = bacc.Bacc("TRN2", target_bir_lowering=False, num_devices=1)
    arrays = {f"in_{k}": np.ascontiguousarray(v) for k, v in ins.items()}
    args = [nc.dram_tensor(k, v.shape, F32, kind="ExternalInput").ap() for k, v in arrays.items()]
    args += [nc.dram_tensor(f"out_{k}", s, F32, kind="ExternalOutput").ap() for k, s in outs.items()]
    build(nc, *args)
    r = run(nc, [arrays], core_ids=[0])
    g = {k: r.results[0][f"out_{k}"] for k in outs}
    return (
        g["y_prompt"].reshape(1, NP_TOK, D),
        g["y_sample"].reshape(NB, NT, D),
        g["conv_new_p"].transpose(2, 0, 1).reshape(1, 1, CW - 1, CONV),
        g["dconv_new_p"].transpose(2, 1, 0).reshape(1, 1, DCW - 1, 3 * H * P),
        g["state_new_p"].reshape(P, H, P).transpose(1, 0, 2).reshape(1, 1, H, P, P),
        g["conv_new_s"].reshape(NC, NB, P, CW - 1).transpose(1, 3, 0, 2).reshape(1, NB, CW - 1, CONV),
        g["dconv_new_s"].reshape(P, 3 * H, NB, DCW - 1).transpose(2, 3, 1, 0).reshape(1, NB, DCW - 1, 3 * H * P),
        g["state_new_s"].reshape(P, H, NB, P).transpose(2, 1, 0, 3).reshape(1, NB, H, P, P),
    )
```

```python
from contextlib import ExitStack

import concourse.bass as bass
from concourse import mybir

P = 128
D = 2048
NP_TOK = 512
NB, NT = 8, 16
T = NP_TOK + NB * NT
TILES = T // P
PT = NP_TOK // P
KD = D // P
CONV = 1024
CW = 31
NC = CONV // P
H = 8
DCW = 4
PH = 8
TOPK = 16
NK = 128
NE = NK * NK
HP = 2 * PH
SLOTS = PH * TOPK
EPS = 1e-6
LEVELS = 7
OCW = 256
NOC = D // OCW

F32 = mybir.dt.float32
F32R = mybir.dt.float32r
U32 = mybir.dt.uint32
ALU = mybir.AluOpType
ACT = mybir.ActivationFunctionType
X = mybir.AxisListType.X

PCOLS = {}
_o = 0
for _n, _w in (("mix_g", KD), ("conv_w", NC * CW), ("conv_b", NC), ("ln_g", NC), ("ln_b", NC),
               ("dconv_w", 3 * H * DCW), ("dn_g", 1), ("dt_bias", H), ("a_log", H)):
    PCOLS[_n] = (_o, _w)
    _o += _w
PW = _o

IDENT, ONES, TRI_P, TRI_S, BLK_S, LEV0 = range(6)
NCONST = LEV0 + LEVELS

KINDS = ("q", "k", "v", "gate", "glu")
QPAD = NP_TOK + DCW - 1 + NB * (NT + DCW - 1)
CPAD = NP_TOK + CW - 1 + NB * (NT + CW - 1)
QLEN = QPAD - (DCW - 1)
CLEN = CPAD - (CW - 1)
DT = 3
TD = DT * P
GT = TILES - DT
ET = 4
CHUNKS = NK // ET
UNIT = 8 * P
NU = 2 * ET + D // P // 2
RING = 2
STEPS = NU // (2 * RING)
GTOK = 48
GB = 8


def build(nc, x_prompt, x_sample, consts, params, conv_prefix, dconv_prefix, state_in, w_ba, w_group, w_z,
          w_merge, w_out, w_q, keys, ffn_g, final_g, peer_u, peer_v, u_units, v_units,
          y_prompt, y_sample, conv_new_p, dconv_new_p, state_new_p, conv_new_s, dconv_new_s, state_new_s):
    with ExitStack() as ctx:
        first = ctx.enter_context(ExitStack())

        def sb(name, shape, dt=F32):
            return first.enter_context(nc.sbuf_tensor(name, shape, dt))

        first_sems = []

        def sem(name):
            first_sems.append(first.enter_context(nc.semaphore(name)))
            return first_sems[-1]

        cst = ctx.enter_context(nc.sbuf_tensor("cst", [P, NCONST, P], F32))
        ps = [ctx.enter_context(nc.psum_tensor(f"ps{i}", [P, 1024], F32)) for i in range(4)]

        XNT, CT, QT, KT, VT, WR, TM = 0, 10240, 15360, 20480, 25600, 30720, 40960
        END = 49152
        arena = sb("arena", [P, END])

        def at(off, *dims):
            n = 1
            for d in dims:
                n *= d
            v = arena[:, off:off + n]
            if len(dims) == 2:
                v = v.rearrange("p (a b) -> p a b", a=dims[0])
            elif len(dims) == 3:
                v = v.rearrange("p (a b c) -> p a b c", a=dims[0], b=dims[1])
            return v

        par = sb("par", [P, PW])
        wba = sb("wba", [P, KD, 2 * H])
        dpre = sb("dpre", [P, 3 * H * NB, DCW - 1])
        dnew_p = sb("dnew_p", [P, 3 * H, DCW - 1])
        dnew_s = sb("dnew_s", [P, 3 * H * NB, DCW - 1])
        small = sb("small", [P, 136])
        epsc = sb("epsc", [P, 1])
        beta = sb("beta", [P, TILES, H])
        glog = sb("glog", [P, TILES, H])
        smalld = sb("smalld", [P, 256])

        ident = cst[:, IDENT, :]
        ones = cst[:, ONES, :]

        def pcol(name, i=0, n=1):
            o = PCOLS[name][0]
            return par[:, o + i:o + i + n]

        def ps8(i):
            return ps[i][:].rearrange("p (h c) -> p h c", h=8)

        xnT = at(XNT, KD, T)
        cT = at(CT, NC, T)
        qT = at(QT, H, T)
        kT = at(KT, H, T)
        vT = at(VT, H, T)
        xin = at(KT, TILES, D)

        ld_par, ld_x = sem("ld_par"), [sem(f"ld_x{t}") for t in range(TILES)]
        pace = {e: sem(f"pace_{e}") for e in ("sp", "act", "pe", "dve", "pool")}
        ready0 = sem("ready0")
        sumsq, msq, root, xscaled, xtr, xevac = (sem(n) for n in ("sumsq", "msq", "root", "xscaled", "xtr", "xevac"))
        ba_mm, ba_act, ba_dve = sem("ba_mm"), sem("ba_act"), sem("ba_dve")
        a_link, d_link, p_link = sem("a_link"), sem("d_link"), sem("p_link")

        def wreg(eng, name, s, v):
            eng.wait_ge(s, v)
            eng.sem_inc(pace[name], 1)

        class Link:

            def __init__(self, eng, name, s, base=0, loop=False):
                self.eng, self.name, self.s, self.base, self.n, self.loop = eng, name, s, base, 0, loop

            def __call__(self, ins):
                self.n += 1
                ins.then_inc(self.s, 1)
                if self.loop:
                    wreg(self.eng, self.name, self.s, self.base + self.n)
                else:
                    self.eng.wait_ge(self.s, self.base + self.n)

        mixer = ctx.enter_context(ExitStack())
        block = mixer.enter_context(nc.Block())

        pads = {"q": TM, "k": TM + QPAD, "v": TM + 2 * QPAD}
        CPB = TM + 3 * QPAD
        CACC = CPB + CPAD
        QACC = CACC + CPAD
        SIG = QACC + QPAD
        SQ = SIG + T
        RT = SQ + 2 * T
        assert RT + T <= END
        wring = {kd: at(WR + i * D, KD, P) for i, kd in enumerate(KINDS)}
        w_ld = {kd: sem(f"w_ld_{kd}") for kd in KINDS}
        mm = {kd: sem(f"mm_{kd}") for kd in KINDS}
        evac = {kd: sem(f"evac_{kd}") for kd in KINDS}
        conv_done = {kd: sem(f"conv_done_{kd}") for kd in "qkv"}
        silu_done = {kd: sem(f"silu_done_{kd}") for kd in "qkv"}
        stage_done = {kd: sem(f"stage_done_{kd}") for kd in "qkv"}
        prefix_done = {kd: sem(f"prefix_done_{kd}") for kd in "qkvc"}
        sq_done = {kd: sem(f"sq_done_{kd}") for kd in "qk"}
        mm_sum = {kd: sem(f"mm_sum_{kd}") for kd in "qk"}
        norm_root = {kd: sem(f"norm_root_{kd}") for kd in "qk"}
        norm_done = {kd: sem(f"norm_done_{kd}") for kd in "qk"}
        glu_done, cconv_done, cbias_done, cstate_out = sem("glu_done"), sem("cconv_done"), sem("cbias_done"), sem("cstate_out")
        dve_loop, dve_conv = sem("dve_loop"), sem("dve_conv")
        PSK = {"q": 0, "k": 1, "v": 2, "gate": 0, "glu": 1}

        def qpad(kd):
            return at(pads[kd], QPAD)

        def seg(buf, width, lead):
            return buf[:, NP_TOK + lead:NP_TOK + lead + NB * width].rearrange("p (b w) -> p b w", b=NB)

        ln_sum, ln_mean, ln_cent, ln_sq, ln_var, ln_root, ln_scaled, ln_out = (
            sem(n) for n in ("ln_sum", "ln_mean", "ln_cent", "ln_sq", "ln_var", "ln_root", "ln_scaled", "ln_out"))
        ln_sqmm = sem("ln_sqmm")
        LSQ = TM
        LMEAN = TM + 2 * T

        SLOT = [TM + 1024 * i for i in range(8)] + [WR + 8192, WR + 9216]
        kc, qc, vc, eb, qkd, atb, tb, ttb, xb, atl = (at(o, H, P) for o in SLOT)
        st_p = at(WR, H, P)
        st_s = at(WR, H, NB, P)
        st_s_dst = at(WR, 8192)
        dd = {n: sem(f"dd_{n}") for n in (
            "copied", "gsum", "gexp_in", "gexp", "trig", "rows", "ediff", "eexp", "kk", "qk", "at", "atl", "x", "xc",
            "tx", "t", "tt", "ktr", "kd", "ks", "r2", "dl", "dlc", "o2", "sup", "snew", "oroot", "oscaled",
            "otr", "out", "vtr", "vb", "ksT", "ksc", "oss", "dm", "grow", "init")}
        dd_link_d = sem("dd_link_d")
        st_ld, st_out = (ld_x[4], 16), sem("st_out")

        z_ld = [(w_ld["q"], 16 * NC), (w_ld["k"], 16 * NC)]
        z_mm, z_act, z_dve = (mm["glu"], NC), sem("z_act"), sem("z_dve")
        mg_ld = [(w_ld[kd], 16 * NC) for kd in ("v", "gate", "glu")]
        mg_mm = [(mm[kd], NC) for kd in ("q", "k", "v", "gate")]
        mg_sig, mg_out, mg_t = sem("mg_sig"), sem("mg_out"), sem("mg_t")
        mT = at(KT, KD, T)
        x1 = at(XNT, TILES, D)
        wo_ld = [(w_ld[kd], 16 * (NC + H // 2)) for kd in "qk"]
        wo_mm, wo_add, xr_ld = sem("wo_mm"), sem("wo_add"), (ld_x[3], 16)
        xn2 = at(CT, TILES, D)
        xn2T = at(KT, KD, T)
        n2_sumsq, n2_msq, n2_root, n2_done, n2_tr, n2_evac = (
            (sumsq, TILES), (msq, 1), (root, 1), (xscaled, TILES), (xtr, 2 * TILES), (xevac, 2 * TILES))
        g_ld, key_ld = (ld_x[0], 16), (ld_x[1], 16)
        wq_ld = [(w_ld[kd], 16 * (NC + H // 2 + NOC // 2)) for kd in "qk"]
        q_mm, q_evac, s_mm, s_evac, tk_done, tk_link = (sem(n) for n in ("q_mm", "q_evac", "s_mm", "s_evac", "tk_done", "tk_link"))
        KEYS = TM
        QH = TM + 2048
        SC = QH + T
        SC2 = SC + T
        STOP = SC2 + T
        ITOP = STOP + TILES * HP * TOPK
        keyT = at(KEYS, HP, NK)
        stop_ = at(STOP, TILES, HP * TOPK)
        itop = at(ITOP, TILES, HP * TOPK)
        assert ITOP + TILES * HP * TOPK <= END
        itop_u = at(ITOP + TILES * HP * TOPK + TILES * TOPK, TILES, TOPK).bitcast(U32)
        chosen = at(WR, 3 * DT, SLOTS)
        GIDX = WR + 3 * DT * SLOTS
        gidx = at(GIDX, GT, SLOTS).bitcast(U32)
        ggate = at(GIDX + GT * SLOTS, GT, SLOTS)
        SELW = (3 * DT + 2 * GT) * SLOTS

        def gate_of(t):
            return chosen[:, 3 * t + 2, :] if t < DT else ggate[:, t - DT, :]
        posu = at(KT + 4 * D, SLOTS).bitcast(U32)
        sel_link, sel_pre, sel_exp, iota_done = sem("sel_link"), sem("sel_pre"), sem("sel_exp"), sem("iota_done")
        iota16 = sb("iota16", [P, TOPK])
        out_done = sem("out_done")
        iota_i = sb("iota_i", [P, TOPK], mybir.dt.int32)
        topbuf = at(ITOP + TILES * HP * TOPK, TILES, TOPK)
        posu2 = at(KT + 4 * D + SLOTS, 2, SLOTS).bitcast(U32)
        spilled, selected = sem("spilled"), sem("selected")
        x1_spill = nc.dram_tensor("x1_spill", (P, TILES * D), F32, kind="Internal").ap()
        xg_spill = nc.dram_tensor("xg_spill", (P, GT * D), F32, kind="Internal").ap()
        xT_spill = nc.dram_tensor("xT_spill", (P, KD, TD), F32, kind="Internal").ap()
        sel_spill = nc.dram_tensor("sel_spill", (P, SELW), F32, kind="Internal").ap()
        gates_dram = nc.dram_tensor("gates_dram", (NK, P, TD), F32, kind="Internal").ap()
        def count_s(per, k):
            prompt = {2 * 4: 2 * LEVELS, 2 * 4 - 2: 2 * LEVELS - 2, 2 * 4 + 1: 2 * LEVELS + 1, 4 * 4 - 2: 4 * LEVELS - 2}.get(per, per)
            return PT * prompt + k

        @block.sync
        def _(sp):
            for t in range(TILES):
                src = x_prompt[t * P:(t + 1) * P, :] if t < PT else x_sample
                sp.dma_start(xin[:, t, :], src).then_inc(ld_x[t], 16)
                if t == 0:
                    sp.dma_start(cst[:], consts).then_inc(ld_par, 16)
                    sp.dma_start(par[:], params).then_inc(ld_par, 16)
                    sp.dma_start(wba[:], w_ba).then_inc(ld_par, 16)
            sp.dma_start(dpre[:], dconv_prefix).then_inc(ld_par, 16)
            for kd in KINDS:
                sp.dma_start(wring[kd].rearrange("p k c -> p (k c)"), w_group[KINDS.index(kd)]).then_inc(w_ld[kd], 16)
            with sp.Fori(0, NC - 1) as c:
                for i, kd in enumerate(KINDS):
                    wreg(sp, "sp", mm[kd], c + 1)
                    sp.dma_start(wring[kd].rearrange("p k c -> p (k c)"),
                                 w_group[bass.ds((c + 1) * 5 + i, 1)].rearrange("a p n -> p (a n)")).then_inc(w_ld[kd], 16)
            sp.wait_ge(dd["snew"], PT * 2)
            sp.dma_start(state_new_p, at(WR, H * P)).then_inc(st_out, 16)
            sp.wait_ge(st_out, 16)
            sp.dma_start(st_s_dst, state_in).then_inc(st_ld[0], 16)
            sp.wait_ge(dd["snew"], PT * 2 + 2 * H)
            sp.dma_start(state_new_s, st_s_dst).then_inc(st_out, 16)
            sp.wait_ge(st_out, 32)
            for i in range(2):
                sp.dma_start(at(WR + i * D, D), w_z[i]).then_inc(z_ld[i][0], 16)
            with sp.Fori(0, H // 2 - 1) as i:
                for r in range(2):
                    wreg(sp, "sp", z_mm[0], 2 * i + (r + 1 + z_mm[1]))
                    sp.dma_start(at(WR + r * D, D), w_z[bass.ds(2 * i + r + 2, 1)].rearrange("a p n -> p (a n)")).then_inc(z_ld[r][0], 16)
            sp.wait_ge(z_mm[0], z_mm[1] + H)
            for j in range(3):
                sp.dma_start(at(WR + j * D, D), w_merge[j]).then_inc(mg_ld[j][0], 16)
            with sp.Fori(0, KD - 1) as n:
                for j, m in ((0, 0), (1, 1), (2, 3)):
                    wreg(sp, "sp", mg_mm[m][0], n + (mg_mm[m][1] + 1))
                    sp.dma_start(at(WR + j * D, D), w_merge[bass.ds((n + 1) * 3 + j, 1)].rearrange("a p n -> p (a n)")).then_inc(mg_ld[j][0], 16)
            sp.wait_ge(mg_mm[3][0], mg_mm[3][1] + KD)
            for i in range(2):
                sp.dma_start(at(WR + i * KD * OCW, KD * OCW), w_out[i]).then_inc(wo_ld[i][0], 16)
            sp.dma_start(x1[:, 0:PT, :], x_prompt.rearrange("(t p) d -> p t d", p=P)).then_inc(xr_ld[0], 16)
            sp.dma_start(x1[:, PT, :], x_sample).then_inc(xr_ld[0], 16)
            with sp.Fori(0, NOC // 2 - 1) as i:
                for r in range(2):
                    wreg(sp, "sp", wo_mm, (2 * i + r + 1) * TILES)
                    sp.dma_start(at(WR + r * KD * OCW, KD * OCW),
                                 w_out[bass.ds(2 * i + r + 2, 1)].rearrange("a p n -> p (a n)")).then_inc(wo_ld[r][0], 16)
            sp.wait_ge(wo_mm, NOC * TILES)
            sp.dma_start(at(WR + 4 * D, D), ffn_g).then_inc(g_ld[0], 16)
            sp.dma_start(at(KEYS, HP * NK), keys).then_inc(key_ld[0], 16)
            for i in range(2):
                sp.dma_start(at(WR + i * D, D), w_q[i]).then_inc(wq_ld[i][0], 16)
            sp.wait_ge(wo_add, NOC * TILES + 5)
            sp.dma_start(x1_spill, at(XNT, TILES * D)).then_inc(spilled, 16)
            sp.wait_ge(n2_evac[0], n2_evac[1] + 2 * TILES)
            sp.dma_start(xg_spill, at(CT + DT * D, GT * D)).then_inc(spilled, 16)
            sp.dma_start(xT_spill, xn2T[:, :, 0:TD]).then_inc(spilled, 16)
            with sp.Fori(0, HP // 2 - 1) as i:
                for r in range(2):
                    wreg(sp, "sp", q_mm, 2 * i + r + 1)
                    sp.dma_start(at(WR + r * D, D), w_q[bass.ds(2 * i + r + 2, 1)].rearrange("a p n -> p (a n)")).then_inc(wq_ld[r][0], 16)
            sp.wait_ge(stage_done["v"], NC + 1)
            sp.wait_ge(stage_done["q"], NC + 1)
            sp.wait_ge(stage_done["k"], NC + 1)
            sp.dma_start(dconv_new_p, dnew_p[:]).then_inc(out_done, 16)
            sp.dma_start(dconv_new_s, dnew_s[:]).then_inc(out_done, 16)
            sp.wait_ge(selected, 1)
            sp.dma_start(sel_spill, at(WR, SELW)).then_inc(spilled, 16)
            sp.wait_ge(spilled, 64)
            sp.wait_ge(out_done, 32)
            sp.wait_ge(cstate_out, 32 * NC)

        @block.tensor
        def _(pe):
            pe.wait_ge(ld_par, 48)
            for t in range(TILES):
                pe.wait_ge(xscaled, t + 1)
                for half in range(2):
                    n = 2 * t + half
                    if n >= 4:
                        pe.wait_ge(xevac, n - 3)
                    for k in range(8):
                        kk = half * 8 + k
                        m = pe.transpose(ps[n % 4][:, k * P:(k + 1) * P], xin[:, t, kk * P:(kk + 1) * P], ident)
                    m.then_inc(xtr, 1)
            pe.wait_ge(xevac, 2 * TILES)
            for t in range(TILES):
                for k in range(KD):
                    m = pe.matmul(ps[3][:, t * 2 * H:(t + 1) * 2 * H], xnT[:, k, t * P:(t + 1) * P], wba[:, k, :],
                                  start=k == 0, stop=k == KD - 1)
            m.then_inc(ba_mm, 1)

            def project(out, w, src, n=KD):
                for k in range(n):
                    pe.matmul(out[:, 0:NP_TOK], w[:, k, :], src[:, k, 0:NP_TOK], start=k == 0, stop=k == n - 1)
                    m = pe.matmul(out[:, NP_TOK:T], w[:, k, :], src[:, k, NP_TOK:T], start=k == 0, stop=k == n - 1)
                return m

            def sum_rows(out, src, start=True, stop=True):
                pe.matmul(out[:, 0:NP_TOK], ones, src[:, 0:NP_TOK], start=start, stop=stop)
                return pe.matmul(out[:, NP_TOK:T], ones, src[:, NP_TOK:T], start=start, stop=stop)

            pe.wait_ge(ba_act, 1)
            pe.wait_ge(ba_dve, 1)
            with pe.Fori(0, NC) as c:
                for kd in KINDS:
                    pe.wait_ge(w_ld[kd], c * 16 + 16)
                    if kd == "q":
                        pe.wait_ge(glu_done, c + 1)
                    elif kd == "k":
                        pe.wait_ge(glu_done, c + 1)
                    elif kd == "v":
                        pe.wait_ge(norm_root["k"], c + 1)
                    elif kd == "gate":
                        pe.wait_ge(evac["q"], c + 1)
                    else:
                        pe.wait_ge(evac["k"], c + 1)
                    project(ps[PSK[kd]], wring[kd], xnT).then_inc(mm[kd], 1)
                pe.wait_ge(sq_done["q"], c + 1)
                pe.wait_ge(norm_root["q"], c + 1)
                sum_rows(ps[3], at(SQ, T)).then_inc(mm_sum["q"], 1)
                pe.wait_ge(sq_done["k"], c + 1)
                pe.wait_ge(evac["v"], c + 1)
                sum_rows(ps[2], at(SQ + T, T)).then_inc(mm_sum["k"], 1)

            pe.wait_ge(cbias_done, NC)
            pe.wait_ge(evac["q"], NC + 0)
            pe.wait_ge(glu_done, NC + 1)
            for c in range(NC):
                m = sum_rows(ps[0], cT[:, c, :], start=c == 0, stop=c == NC - 1)
            m.then_inc(ln_sum, 1)
            for c in range(NC):
                pe.wait_ge(ln_sq, c + 1)
                sum_rows(ps[1], at(LSQ + (c % 2) * T, T), start=c == 0, stop=c == NC - 1).then_inc(ln_sqmm, 1)

            def delta(t, streams, w, tot):
                tri = cst[:, TRI_S if streams else TRI_P, :]
                blk = cst[:, BLK_S, :] if streams else ones
                lev = 4 if streams else LEVELS
                w(dd["copied"], tot(1, 1))
                w(dd["init"], tot(1, 1))
                gcur = smalld[:, 0:H]
                pe.matmul(ps[3][:, 0:H], tri, gcur, start=True, stop=True)
                pe.matmul(ps[3][:, H:2 * H], blk, gcur, start=True, stop=True).then_inc(dd["gsum"], 1)
                w(dd["trig"], tot(2, 1))
                for g in range(2):
                    pe.matmul(ps[0][:, g * 512:(g + 1) * 512], ones, at(SLOT[3] + g * 512, 512), start=True, stop=True).then_inc(dd["rows"], 1)
                w(dd["trig"], tot(2, 2))
                for g in range(2):
                    pe.matmul(ps[1][:, g * 512:(g + 1) * 512], ones, at(SLOT[8] + g * 512, 512), start=True, stop=True).then_inc(dd["rows"], 1)
                for h in range(H):
                    m = pe.matmul(ps[2][:, h * P:(h + 1) * P], kc[:, h, :], kc[:, h, :], start=True, stop=True)
                m.then_inc(dd["kk"], 1)
                w(dd["gexp_in"], tot(1, 1))
                for h in range(H):
                    m = pe.matmul(ps[3][:, h * P:(h + 1) * P], kc[:, h, :], qc[:, h, :], start=True, stop=True)
                m.then_inc(dd["qk"], 1)
                w(dd["ediff"], tot(1, 1))
                for h in range(H):
                    m = pe.transpose(ps[0][:, h * P:(h + 1) * P], vc[:, h, :], ident)
                m.then_inc(dd["vtr"], 1)
                for l in range(lev):
                    for g in range(2):
                        w(dd["atl"], tot(2 * lev, 2 * l + g + 1))
                        if l:
                            w(dd["t"], tot(2 * lev - 2, 2 * l - 1 + g))
                        else:
                            w(dd["at"], tot(2, 2))
                        for h in range(4 * g, 4 * g + 4):
                            m = pe.matmul(ps[1][:, h * P:(h + 1) * P], atl[:, h, :], tb[:, h, :], start=True, stop=True)
                        m.then_inc(dd["x"], 1)
                    for g in range(2):
                        w(dd["xc"], tot(2 * lev, 2 * l + g + 1))
                        w(dd["tt"], tot(2 * lev + 1, 2 * l + g if l else 1))
                        if l < lev - 1:
                            for h in range(4 * g, 4 * g + 4):
                                m = pe.matmul(ps[2][:, h * P:(h + 1) * P], ttb[:, h, :], xb[:, h, :], start=True, stop=True)
                            m.then_inc(dd["tx"], 1)
                        for h in range(4 * g, 4 * g + 4):
                            m = pe.matmul(ps[3][:, h * P:(h + 1) * P], xb[:, h, :], ttb[:, h, :], start=True, stop=True)
                        m.then_inc(dd["tx"], 1)
                w(dd["vb"], tot(1, 1))
                for h in range(H):
                    m = pe.transpose(ps[0][:, h * P:(h + 1) * P], kc[:, h, :], ident)
                m.then_inc(dd["ktr"], 1)
                w(dd["tt"], tot(2 * lev + 1, 2 * lev + 1))
                if not streams:
                    for h in range(H):
                        m = pe.matmul(ps[1][:, h * P:(h + 1) * P], kc[:, h, :], st_p[:, h, :], start=True, stop=True)
                    m.then_inc(dd["ks"], 1)
                    for h in range(H):
                        m = pe.matmul(ps[2][:, h * P:(h + 1) * P], qc[:, h, :], st_p[:, h, :], start=True, stop=True)
                    m.then_inc(dd["ks"], 1)
                else:
                    pe.wait_ge(st_ld[0], st_ld[1] + 16)
                    for j, src in enumerate((kc, qc)):
                        for h in range(H):
                            for b in range(NB):
                                m = pe.matmul(ps[1 + j][:, h * P + b * NT:h * P + (b + 1) * NT], st_s[:, h, b, :],
                                              src[:, h, b * NT:(b + 1) * NT], start=True, stop=True)
                        m.then_inc(dd["ksT"], 1)
                    for j in range(2):
                        pe.wait_ge(dd["ksc"], j + 1)
                        for h in range(H):
                            m = pe.transpose(ps[1 + j][:, h * P:(h + 1) * P], (eb if j == 0 else tb)[:, h, :], ident)
                        m.then_inc(dd["ks"], 1)
                w(dd["r2"], tot(1, 1))
                for h in range(H):
                    m = pe.matmul(ps[3][:, h * P:(h + 1) * P], ttb[:, h, :], vc[:, h, :], start=True, stop=True)
                m.then_inc(dd["dl"], 1)
                w(dd["dlc"], tot(1, 1))
                for h in range(H):
                    m = pe.matmul(ps[1][:, h * P:(h + 1) * P], qkd[:, h, :], atl[:, h, :], start=True, stop=True)
                m.then_inc(dd["o2"], 1)
                w(dd["kd"], tot(1, 1))
                if not streams:
                    for h in range(H):
                        m = pe.matmul(ps[3][:, h * P:(h + 1) * P], atb[:, h, :], atl[:, h, :], start=True, stop=True)
                    m.then_inc(dd["sup"], 1)
                else:
                    for h in range(H):
                        pe.wait_ge(dd["dm"], h + 1)
                        if h:
                            pe.wait_ge(dd["snew"], PT * 2 + 2 * h)
                        for g in range(2):
                            pe.matmul(ps[3][:, g * 512:(g + 1) * 512], atb[:, h, :],
                                      at(SLOT[3 if h % 2 else 6] + g * 512, 512), start=True, stop=True).then_inc(dd["sup"], 1)
                w(dd["oscaled"], tot(1, 1))
                for h in range(H):
                    m = pe.transpose(ps[0][:, h * P:(h + 1) * P], xb[:, h, :], ident)
                m.then_inc(dd["otr"], 1)

            pe.wait_ge(ln_root, 1)
            pe.wait_ge(ln_mean, 1)
            with pe.Fori(0, PT) as t:
                delta(t, False, lambda s, v: wreg(pe, "pe", s, v), lambda per, k: t * per + k)
            delta(PT, True, lambda s, v: pe.wait_ge(s, v), lambda per, k: count_s(per, k))

            pe.wait_ge(dd["out"], TILES)
            with pe.Fori(0, H // 2) as i:
                for r in range(2):
                    wreg(pe, "pe", z_ld[r][0], i * 16 + (z_ld[r][1] + 16))
                    wreg(pe, "pe", z_act, 2 * i + r + 1)
                    project(ps[r], at(WR + r * D, KD, P), xnT).then_inc(z_mm[0], 1)
            pe.wait_ge(z_act, H + 2)
            pe.wait_ge(z_dve, H)
            oT = qT
            with pe.Fori(0, KD) as n:
                for j in range(2):
                    wreg(pe, "pe", mg_ld[j][0], n * 16 + (mg_ld[j][1] + 16))
                    wreg(pe, "pe", mg_sig, 2 * n + j + 1)
                    project(ps[j], at(WR + j * D, KD, P), xnT).then_inc(mg_mm[j][0], 1)
                wreg(pe, "pe", mg_ld[2][0], n * 16 + (mg_ld[2][1] + 16))
                wreg(pe, "pe", mg_out, n + 1)
                project(ps[2], at(WR + 2 * D, NC, P), cT, NC).then_inc(mg_mm[2][0], 1)
                project(ps[3], at(WR + 2 * D + NC * P, NC, P), oT, NC).then_inc(mg_mm[3][0], 1)

            pe.wait_ge(mg_out, KD + 1)
            with pe.Fori(0, NOC // 2) as i:
                for r in range(2):
                    wreg(pe, "pe", wo_ld[r][0], i * 16 + (wo_ld[r][1] + 16))
                    w = at(WR + r * KD * OCW, KD, OCW)
                    for t in range(TILES):
                        b = (r * TILES + t) % 5
                        wreg(pe, "pe", wo_add, (2 * i + r) * TILES + t + 1)
                        dst = ps[b // 2][:, (b % 2) * 512:(b % 2) * 512 + OCW]
                        for k in range(KD):
                            m = pe.matmul(dst, mT[:, k, t * P:(t + 1) * P], w[:, k, :], start=k == 0, stop=k == KD - 1)
                        m.then_inc(wo_mm, 1)

            pe.wait_ge(wo_add, NOC * TILES + 5)
            for t in range(TILES):
                pe.wait_ge(n2_done[0], n2_done[1] + t + 1)
                for half in range(2):
                    n = 2 * t + half
                    if n >= 4:
                        pe.wait_ge(n2_evac[0], n2_evac[1] + n - 3)
                    for k in range(8):
                        kk = half * 8 + k
                        m = pe.transpose(ps[n % 4][:, k * P:(k + 1) * P], xn2[:, t, kk * P:(kk + 1) * P], ident)
                    m.then_inc(n2_tr[0], 1)
            pe.wait_ge(n2_evac[0], n2_evac[1] + 2 * TILES)
            pe.wait_ge(key_ld[0], key_ld[1] + 16)
            keys_view = keyT
            with pe.Fori(0, HP // 2) as i:
                for r in range(2):
                    wreg(pe, "pe", wq_ld[r][0], i * 16 + (wq_ld[r][1] + 16))
                    wreg(pe, "pe", q_evac, 2 * i + r + 1)
                    project(ps[r], at(WR + r * D, KD, P), xn2T).then_inc(q_mm, 1)
                    wreg(pe, "pe", q_evac, 2 * i + r + 2)
                    wreg(pe, "pe", s_evac, 2 * i + r + 1)
                    for t in range(TILES):
                        m = pe.matmul(ps[2 + r][:, t * P:(t + 1) * P], at(QH, T)[:, t * P:(t + 1) * P],
                                      keys_view[:, bass.ds(2 * i + r, 1), :].rearrange("p a n -> p (a n)"), start=True, stop=True)
                    m.then_inc(s_mm, 1)

        @block.scalar
        def _(act):
            link = Link(act, "act", a_link)
            act.wait_ge(ready0, 1)
            for t in range(TILES):
                act.wait_ge(ld_x[t], 16)
                link(act.activation(at(CT, D), xin[:, t, :], ACT.Square, accum_out=small[:, t:t + 1]))
                act.sem_inc(sumsq, 1)
            act.wait_ge(msq, 1)
            act.activation(small[:, 16:16 + TILES], small[:, 8:8 + TILES], ACT.Sqrt).then_inc(root, 1)
            act.wait_ge(ba_mm, 1)
            ba = ps[3][:, 0:TILES * 2 * H].rearrange("p (t c) -> p t c", t=TILES)
            act.wait_ge(ba_dve, 1)
            link(act.activation(beta[:], ba[:, :, 0:H], ACT.Sigmoid))
            t1 = small[:, 72:112]
            link(act.activation(t1, small[:, 32:72], ACT.Abs))
            link(act.activation(t1, t1, ACT.Exp, scale=-1.0))
            link(act.activation(t1, t1, ACT.Ln, bias=1.0))
            link(act.activation(small[:, 112:120], pcol("a_log", 0, H), ACT.Exp))
            act.sem_inc(ba_act, 1)

            act.sem_inc(silu_done["v"], 1)
            act.sem_inc(norm_root["q"], 1)
            act.sem_inc(norm_root["k"], 1)
            with act.Fori(0, NC) as c:
                for i, kd in enumerate("qkv"):
                    wreg(act, "act", mm[kd], c + 1)
                    wreg(act, "act", conv_done[kd], c + 1)
                    wreg(act, "act", stage_done[kd], c + 1)
                    src = ps[PSK[kd]]
                    act.activation(qpad(kd)[:, DCW - 1:DCW - 1 + NP_TOK], src[:, 0:NP_TOK], ACT.Copy)
                    act.activation(seg(qpad(kd), NT + DCW - 1, DCW - 1)[:, :, DCW - 1:],
                                   src[:, NP_TOK:T].rearrange("p (b w) -> p b w", b=NB), ACT.Copy).then_inc(evac[kd], 1)
                    dst = {"q": QT, "k": KT, "v": VT}[kd]
                    full = at(dst, H, T)[:, bass.ds(c, 1), :].rearrange("p a n -> p (a n)")
                    wreg(act, "act", conv_done[kd], c + 2)
                    cv = at(QACC, QPAD)
                    act.activation(full[:, 0:NP_TOK], cv[:, 0:NP_TOK], ACT.Silu)
                    act.activation(full[:, NP_TOK:T].rearrange("p (b w) -> p b w", b=NB),
                                   seg(cv, NT + DCW - 1, DCW - 1)[:, :, 0:NT], ACT.Silu).then_inc(silu_done[kd], 1)
                    if kd != "v":
                        wreg(act, "act", silu_done[kd], c + 1)
                        act.activation(at(SQ + i * T, T), full, ACT.Square).then_inc(sq_done[kd], 1)
                wreg(act, "act", mm["gate"], c + 1)
                wreg(act, "act", glu_done, c + 1)
                act.activation(at(SIG, T), ps[0][:, 0:T], ACT.Sigmoid).then_inc(evac["gate"], 1)
                for i, kd in enumerate("qk"):
                    wreg(act, "act", mm_sum[kd], c + 1)
                    wreg(act, "act", norm_done["q" if kd == "k" else "k"], c + (2 if kd == "k" else 1))
                    act.activation(at(RT, T), ps[3 if kd == "q" else 2][:, 0:T], ACT.Sqrt, bias=epsc[:, 0:1]).then_inc(norm_root[kd], 1)
                wreg(act, "act", cconv_done, c + 2)
                cvc = at(CACC, CPAD)
                fullc = cT[:, bass.ds(c, 1), :].rearrange("p a n -> p (a n)")
                act.activation(fullc[:, 0:NP_TOK], cvc[:, 0:NP_TOK], ACT.Identity, bias=par[:, bass.ds(c + PCOLS["conv_b"][0], 1)])
                act.activation(fullc[:, NP_TOK:T].rearrange("p (b w) -> p b w", b=NB),
                               seg(cvc, NT + CW - 1, CW - 1)[:, :, 0:NT], ACT.Identity, bias=par[:, bass.ds(c + PCOLS["conv_b"][0], 1)]).then_inc(cbias_done, 1)

            for kd in "qkv":
                act.wait_ge(stage_done[kd], NC + 1)
            act.wait_ge(ln_sum, 1)
            act.wait_ge(norm_done["k"], NC + 1)
            act.activation(at(LMEAN, T), ps[0][:, 0:T], ACT.Copy, scale=1.0 / CONV).then_inc(ln_mean, 1)
            act.wait_ge(ln_cent, 1)
            for c in range(NC):
                if c >= 2:
                    act.wait_ge(ln_sqmm, c - 1)
                act.activation(at(LSQ + (c % 2) * T, T), cT[:, c, :], ACT.Square).then_inc(ln_sq, 1)
            act.wait_ge(ln_sqmm, NC)
            act.activation(at(LMEAN, T), ps[1][:, 0:T], ACT.Sqrt, bias=epsc[:, 0:1], scale=1.0 / CONV).then_inc(ln_root, 1)
            act.wait_ge(ln_scaled, 1)
            for c in range(NC):
                act.activation(cT[:, c, :], cT[:, c, :], ACT.Silu, bias=pcol("ln_b", c), scale=pcol("ln_g", c)).then_inc(ln_out, 1)

            def delta(t, streams, w, tot, tile):
                lev = 4 if streams else LEVELS
                last_r = ps8(0)
                for dst, src in ((kc, kT), (qc, qT), (vc, vT)):
                    m = act.activation(dst, src[:, :, tile], ACT.Copy)
                m.then_inc(dd["copied"], 1)
                w(dd["gexp_in"], tot(1, 1))
                act.activation(smalld[:, 32:48], smalld[:, 16:32], ACT.Exp).then_inc(dd["gexp"], 1)
                w(dd["rows"], tot(4, 2))
                if streams:
                    act.activation(smalld[:, 64:128].rearrange("p (h b) -> p h b", h=H),
                                   last_r[:, :, NT - 1::NT], ACT.Exp).then_inc(dd["grow"], 1)
                else:
                    act.activation(smalld[:, 64:72], last_r[:, :, P - 1:P].rearrange("p h a -> p (h a)"), ACT.Exp).then_inc(dd["grow"], 1)
                w(dd["ediff"], tot(1, 1))
                act.activation(eb, eb, ACT.Exp).then_inc(dd["eexp"], 1)
                for l in range(lev):
                    for g in range(2):
                        w(dd["x"], tot(2 * lev, 2 * l + g + 1))
                        if l:
                            w(dd["tx"], tot(4 * lev - 2, 4 * l))
                        else:
                            w(dd["at"], tot(2, 2))
                        act.activation(xb[:, 4 * g:4 * g + 4, :], ps8(1)[:, 4 * g:4 * g + 4, :], ACT.Copy).then_inc(dd["xc"], 1)
                if streams:
                    for j in range(2):
                        act.wait_ge(dd["ksT"], j + 1)
                        act.activation(eb if j == 0 else tb, ps8(1 + j), ACT.Copy).then_inc(dd["ksc"], 1)
                w(dd["dl"], tot(1, 1))
                act.activation(atl, ps8(3), ACT.Copy).then_inc(dd["dlc"], 1)
                w(dd["oss"], tot(1, 1))
                act.activation(smalld[:, 144:152], smalld[:, 136:144], ACT.Sqrt).then_inc(dd["oroot"], 1)
                w(dd["otr"], tot(1, 1))
                act.activation(qT[:, :, tile], ps8(0), ACT.Copy).then_inc(dd["out"], 1)

            act.wait_ge(ln_out, NC)
            act.wait_ge(ready0, 2)
            act.wait_ge(cstate_out, 32 * NC)
            with act.Fori(0, PT) as t:
                delta(t, False, lambda s, v: wreg(act, "act", s, v), lambda per, k: t * per + k, bass.ds(t * P, P))
            delta(PT, True, lambda s, v: act.wait_ge(s, v), lambda per, k: count_s(per, k), slice(PT * P, T))

            act.sem_inc(z_act, 2)
            with act.Fori(0, H // 2) as i:
                for r in range(2):
                    wreg(act, "act", z_mm[0], 2 * i + (r + 1 + z_mm[1]))
                    act.activation(at(TM + r * T, T), ps[r][:, 0:T], ACT.Silu).then_inc(z_act, 1)
                wreg(act, "act", z_dve, 2 * i + 2)
            act.sem_inc(mg_sig, 2)
            with act.Fori(0, KD) as n:
                for j in range(2):
                    wreg(act, "act", mg_mm[j][0], n + (mg_mm[j][1] + 1))
                    wreg(act, "act", mg_out, n + 1)
                    act.activation(at(TM + 2 * T + j * T, T), ps[j][:, 0:T], ACT.Sigmoid).then_inc(mg_sig, 1)

            act.wait_ge(wo_add, NOC * TILES + 5)
            link2 = Link(act, "act", a_link, base=link.n)
            for t in range(TILES):
                link2(act.activation(at(KT, D), x1[:, t, :], ACT.Square, accum_out=small[:, t:t + 1]))
                act.sem_inc(n2_sumsq[0], 1)
            act.wait_ge(n2_msq[0], n2_msq[1] + 1)
            act.activation(small[:, 16:16 + TILES], small[:, 8:8 + TILES], ACT.Sqrt).then_inc(n2_root[0], 1)
            act.sem_inc(q_evac, 1)
            act.sem_inc(s_evac, 1)
            with act.Fori(0, HP // 2) as i:
                for r in range(2):
                    wreg(act, "act", q_mm, 2 * i + r + 1)
                    wreg(act, "act", s_evac, 2 * i + r + 1)
                    act.activation(at(QH, T), ps[r][:, 0:T], ACT.Copy).then_inc(q_evac, 1)
                    wreg(act, "act", s_mm, 2 * i + r + 1)
                    wreg(act, "act", tk_done, 2 * i + r + 1)
                    act.activation(at(SC, T), ps[2 + r][:, 0:T], ACT.Copy).then_inc(s_evac, 1)
            for t in range(TILES):
                act.wait_ge(sel_pre, t + 1)
                act.activation(gate_of(t), gate_of(t), ACT.Exp).then_inc(sel_exp, 1)

        @block.vector
        def _(v):
            v.memset(epsc[:], EPS)
            v.memset(at(pads["q"], DCW - 1), 0.0)
            v.memset(at(pads["k"], DCW - 1), 0.0)
            v.memset(at(pads["v"], DCW - 1), 0.0)
            v.memset(smalld[:], 0.0)
            v.memset(small[:], 0.0).then_inc(ready0, 1)
            link = Link(v, "dve", d_link)
            v.wait_ge(sumsq, TILES)
            link(v.tensor_scalar(small[:, 8:8 + TILES], small[:, 0:TILES], 1.0 / D, EPS, ALU.mult, ALU.add))
            v.sem_inc(msq, 1)
            v.wait_ge(root, 1)
            link(v.reciprocal(small[:, 24:24 + TILES], small[:, 16:16 + TILES]))
            v.wait_ge(ld_par, 64)
            mixg = pcol("mix_g", 0, KD)

            def evac_x(n):
                t, half = n // 2, n % 2
                v.wait_ge(xtr, n + 1)
                v.tensor_tensor(xnT[:, 8 * half:8 * half + 8, t * P:(t + 1) * P], ps8(n % 4),
                                mixg[:, 8 * half:8 * half + 8].unsqueeze(2).to_broadcast([P, 8, P]), ALU.mult).then_inc(xevac, 1)
            for t in range(TILES):
                v.tensor_scalar(xin[:, t, :], xin[:, t, :], small[:, 24 + t:25 + t], None, ALU.mult).then_inc(xscaled, 1)
                if t:
                    evac_x(2 * t - 2)
                    evac_x(2 * t - 1)
            evac_x(2 * TILES - 2)
            evac_x(2 * TILES - 1)
            v.wait_ge(ba_mm, 1)
            ba = ps[3][:, 0:TILES * 2 * H].rearrange("p (t c) -> p t c", t=TILES)
            ax = small[:, 32:72].rearrange("p (t h) -> p t h", t=TILES)
            link(v.tensor_tensor(ax, ba[:, :, H:2 * H], pcol("dt_bias", 0, H).unsqueeze(1).to_broadcast([P, TILES, H]), ALU.add))
            v.sem_inc(ba_dve, 1)
            v.wait_ge(ba_act, 1)
            link(v.scalar_tensor_tensor(ax, ax, 0.0, small[:, 72:112].rearrange("p (t h) -> p t h", t=TILES), ALU.max, ALU.add))
            link(v.scalar_tensor_tensor(glog[:], ax, -1.0, small[:, 112:120].unsqueeze(1).to_broadcast([P, TILES, H]), ALU.mult, ALU.mult))
            v.memset(at(CPB, CW - 1), 0.0)
            for s in (*conv_done.values(), glu_done, cconv_done):
                v.sem_inc(s, 1)
            for s in norm_done.values():
                v.sem_inc(s, 1)

            NTAP = DCW * 3 + CW
            with v.Fori(0, NC) as c:
                n = [0]

                def step(ins):
                    n[0] += 1
                    ins.then_inc(dve_loop, 1)
                    wreg(v, "dve", dve_loop, c * NL + n[0])
                NL = 3 * (DCW - 1) + 2 + CW - 1
                for i, kd in enumerate("qkv"):
                    wreg(v, "dve", evac[kd], c + 1)
                    wreg(v, "dve", prefix_done[kd], c + 1)
                    wreg(v, "dve", silu_done["qkv"[i - 1]], c + 1)
                    pad, dst = at(pads[kd], QPAD), at(QACC, QLEN)
                    for j in range(DCW):
                        wc = par[:, bass.ds(c * DCW + (PCOLS["dconv_w"][0] + i * H * DCW + j), 1)]
                        if j == 0:
                            step(v.tensor_scalar(dst, pad[:, j:j + QLEN], wc, None, ALU.mult))
                        else:
                            ins = v.scalar_tensor_tensor(dst, pad[:, j:j + QLEN], wc, dst, ALU.mult, ALU.add)
                            if j < DCW - 1:
                                step(ins)
                            else:
                                ins.then_inc(conv_done[kd], 1)
                wreg(v, "dve", mm["glu"], c + 1)
                wreg(v, "dve", evac["gate"], c + 1)
                wreg(v, "dve", prefix_done["c"], c * 16 + 16)
                cp, sg = at(CPB, CPAD), at(SIG, T)
                v.tensor_tensor(cp[:, CW - 1:CW - 1 + NP_TOK], ps[1][:, 0:NP_TOK], sg[:, 0:NP_TOK], ALU.mult)
                v.tensor_tensor(seg(cp, NT + CW - 1, CW - 1)[:, :, CW - 1:], ps[1][:, NP_TOK:T].rearrange("p (b w) -> p b w", b=NB),
                                sg[:, NP_TOK:T].rearrange("p (b w) -> p b w", b=NB), ALU.mult).then_inc(glu_done, 1)
                for i, kd in enumerate("qk"):
                    wreg(v, "dve", norm_root[kd], c + 2)
                    full = at(QT if kd == "q" else KT, H, T)[:, bass.ds(c, 1), :].rearrange("p a n -> p (a n)")
                    step(v.reciprocal(at(RT, T), at(RT, T)))
                    v.scalar_tensor_tensor(full, full, float(P) ** -0.5 if kd == "q" else 1.0, at(RT, T), ALU.mult, ALU.mult).then_inc(norm_done[kd], 1)
                wreg(v, "dve", glu_done, c + 2)
                dst = at(CACC, CLEN)
                for j in range(CW):
                    wc = par[:, bass.ds(c * CW + (PCOLS["conv_w"][0] + j), 1)]
                    if j == 0:
                        step(v.tensor_scalar(dst, cp[:, j:j + CLEN], wc, None, ALU.mult))
                    else:
                        ins = v.scalar_tensor_tensor(dst, cp[:, j:j + CLEN], wc, dst, ALU.mult, ALU.add)
                        if j < CW - 1:
                            step(ins)
                        else:
                            ins.then_inc(cconv_done, 1)
                assert n[0] == NL, (n[0], NL)
                wreg(v, "dve", cbias_done, c + 1)

            v.wait_ge(ln_mean, 1)
            mean = at(LMEAN, T).unsqueeze(1).to_broadcast([P, NC, T])
            v.tensor_tensor(cT, cT, mean, ALU.subtract).then_inc(ln_cent, 1)
            v.wait_ge(ln_root, 1)
            link(v.reciprocal(at(LMEAN, T), at(LMEAN, T)))
            v.tensor_tensor(cT, cT, mean, ALU.mult).then_inc(ln_scaled, 1)

            def bc(col):
                return col.unsqueeze(2).to_broadcast([P, H, P])

            def bm(mat, n=H):
                return mat.unsqueeze(1).to_broadcast([P, n, P])

            def delta(t, streams, w, tot, gsrc, bsrc, lk):
                tri = cst[:, TRI_S if streams else TRI_P, :]
                lev = 4 if streams else LEVELS
                gcur, bcur = smalld[:, 0:H], smalld[:, 8:8 + H]
                lk(v.tensor_copy(gcur, gsrc))
                lk(v.tensor_copy(bcur, bsrc))
                v.sem_inc(dd["init"], 1)
                w(dd["copied"], tot(1, 1))
                v.tensor_tensor(eb, bm(tri), bc(gcur), ALU.mult).then_inc(dd["trig"], 1)
                v.tensor_tensor(xb, bm(ident), bc(bcur), ALU.mult).then_inc(dd["trig"], 1)
                w(dd["gsum"], tot(1, 1))
                G, toend = smalld[:, 16:24], smalld[:, 24:32]
                lk(v.tensor_copy(smalld[:, 48:64], ps[3][:, 0:16]))
                lk(v.tensor_copy(G, smalld[:, 48:56]))
                lk(v.tensor_tensor(toend, smalld[:, 56:64], smalld[:, 48:56], ALU.subtract))
                v.sem_inc(dd["gexp_in"], 1)
                w(dd["rows"], tot(4, 4))
                w(dd["grow"], tot(1, 1))
                lk(v.tensor_tensor(eb, ps8(0), bc(smalld[:, 48:56]), ALU.subtract))
                v.tensor_scalar(eb, eb, 0.0, None, ALU.min).then_inc(dd["ediff"], 1)
                w(dd["eexp"], tot(1, 1))
                lk(v.tensor_tensor(eb, eb, bm(tri), ALU.mult))
                w(dd["kk"], tot(1, 1))
                lk(v.tensor_tensor(atb, eb, ps8(2), ALU.mult))
                v.tensor_tensor(atb, atb, ps8(1), ALU.mult).then_inc(dd["at"], 1)
                w(dd["qk"], tot(1, 1))
                v.tensor_tensor(qkd, eb, ps8(3), ALU.mult).then_inc(dd["at"], 1)
                lk(v.tensor_copy(tb, bm(ident)))
                v.tensor_copy(ttb, bm(ident)).then_inc(dd["tt"], 1)
                w(dd["at"], tot(2, 2))
                w(dd["gexp"], tot(1, 1))
                w(dd["vtr"], tot(1, 1))
                v.tensor_tensor(vc, ps8(0), bc(bcur), ALU.mult).then_inc(dd["vb"], 1)
                lk(v.tensor_tensor(smalld[:, 128:136], bcur, smalld[:, 32:40], ALU.mult))
                for g in range(2):
                    hs = slice(4 * g, 4 * g + 4)
                    v.tensor_tensor(atl[:, hs, :], atb[:, hs, :], bm(cst[:, LEV0, :], 4), ALU.mult).then_inc(dd["atl"], 1)
                for l in range(lev):
                    for g in range(2):
                        hs = slice(4 * g, 4 * g + 4)
                        if l < lev - 1:
                            w(dd["x"], tot(2 * lev, 2 * l + g + 1))
                            v.tensor_tensor(atl[:, hs, :], atb[:, hs, :], bm(cst[:, LEV0 + l + 1, :], 4), ALU.mult).then_inc(dd["atl"], 1)
                    if l == 0:
                        w(dd["tt"], tot(2 * lev + 1, 1))
                    for g in range(2):
                        hs = slice(4 * g, 4 * g + 4)
                        if l < lev - 1:
                            w(dd["tx"], tot(4 * lev - 2, 4 * l + 2 * g + 1))
                            if l:
                                w(dd["t"], tot(2 * lev - 2, 2 * l - 1 + g))
                            v.tensor_tensor(tb[:, hs, :], tb[:, hs, :], ps8(2)[:, hs, :], ALU.subtract).then_inc(dd["t"], 1)
                            w(dd["tx"], tot(4 * lev - 2, 4 * l + 2 * g + 2))
                        else:
                            w(dd["tx"], tot(4 * lev - 2, 4 * l + g + 1))
                        if l:
                            w(dd["tt"], tot(2 * lev + 1, 2 * l + g))
                        v.tensor_tensor(ttb[:, hs, :], ttb[:, hs, :], ps8(3)[:, hs, :], ALU.subtract).then_inc(dd["tt"], 1)
                w(dd["ktr"], tot(1, 1))
                v.tensor_tensor(atb, ps8(0), bc(smalld[:, 40:48]), ALU.mult).then_inc(dd["kd"], 1)
                w(dd["ks"], tot(2, 1))
                w(dd["vb"], tot(1, 1))
                w(dd["tt"], tot(2 * lev + 1, 2 * lev + 1))
                if streams:
                    w(dd["ks"], tot(2, 2))
                lk(v.tensor_tensor(tb, ps8(1), bc(smalld[:, 128:136]), ALU.mult))
                v.tensor_tensor(vc, vc, tb, ALU.subtract).then_inc(dd["r2"], 1)
                w(dd["ks"], tot(2, 2))
                lk(v.tensor_tensor(xb, ps8(2), bc(smalld[:, 32:40]), ALU.mult))
                w(dd["o2"], tot(1, 1))
                lk(v.tensor_tensor(xb, xb, ps8(1), ALU.add))
                w(dd["r2"], tot(1, 1))
                lk(v.tensor_tensor(eb, xb, xb, ALU.mult))
                lk(v.tensor_reduce(smalld[:, 152:160], eb, X, ALU.add))
                lk(v.tensor_scalar(smalld[:, 136:144], smalld[:, 152:160], 1.0 / P, EPS, ALU.mult, ALU.add))
                v.sem_inc(dd["oss"], 1)
                w(dd["oroot"], tot(1, 1))
                lk(v.reciprocal(smalld[:, 160:168], smalld[:, 144:152]))
                v.tensor_tensor(xb, xb, bc(smalld[:, 160:168]), ALU.mult).then_inc(dd["oscaled"], 1)
                if not streams:
                    w(dd["sup"], tot(1, 1))
                    lk(v.tensor_tensor(st_p, st_p, bc(smalld[:, 64:72]), ALU.mult))
                    v.tensor_tensor(st_p, st_p, ps8(3), ALU.add).then_inc(dd["snew"], 2)
                    w(dd["snew"], tot(2, 2))
                else:
                    bmask = cst[:, BLK_S, :]
                    w(dd["dlc"], tot(1, 1))
                    w(dd["oscaled"], tot(1, 1))
                    for h in range(H):
                        dmb = at(SLOT[3 if h % 2 else 6], NB, P)
                        if h >= 2:
                            v.wait_ge(dd["sup"], PT + 2 * (h - 1))
                        v.tensor_tensor(dmb, atl[:, h, :].unsqueeze(1).to_broadcast([P, NB, P]),
                                        bmask[:, NT - 1::NT].unsqueeze(2).to_broadcast([P, NB, P]), ALU.mult).then_inc(dd["dm"], 1)
                        glb = smalld[:, 64 + NB * h:64 + NB * h + NB].unsqueeze(2).to_broadcast([P, NB, P])
                        lk(v.tensor_tensor(st_s[:, h, :, :], st_s[:, h, :, :], glb, ALU.mult))
                        v.wait_ge(dd["sup"], PT + 2 * h + 2)
                        v.tensor_tensor(st_s[:, h, :, :], st_s[:, h, :, :], ps8(3), ALU.add).then_inc(dd["snew"], 2)

            v.wait_ge(ln_out, NC)
            link(v.memset(st_p, 0.0))
            v.sem_inc(ready0, 1)
            with v.Fori(0, PT) as t:
                NLK = 18
                lk = Link(v, "dve", dd_link_d, base=t * NLK, loop=True)
                delta(t, False, lambda s, val: wreg(v, "dve", s, val), lambda per, k: t * per + k,
                      glog[:, bass.ds(t, 1), :].rearrange("p a h -> p (a h)"), beta[:, bass.ds(t, 1), :].rearrange("p a h -> p (a h)"), lk)
                assert lk.n == NLK, lk.n
            delta(PT, True, lambda s, val: v.wait_ge(s, val), lambda per, k: count_s(per, k), glog[:, PT, :], beta[:, PT, :],
                  Link(v, "dve", dd_link_d, base=PT * NLK))

            oT = qT
            v.wait_ge(dd["out"], TILES)
            with v.Fori(0, H // 2) as i:
                for r in range(2):
                    wreg(v, "dve", z_act, 2 * i + r + 3)
                    dst = oT[:, bass.ds(2 * i + r, 1), :].rearrange("p a n -> p (a n)")
                    v.scalar_tensor_tensor(dst, at(TM + r * T, T), pcol("dn_g"), dst, ALU.mult, ALU.mult).then_inc(z_dve, 1)
            v.sem_inc(mg_out, 1)
            with v.Fori(0, KD) as n:
                s0, s1 = at(TM + 2 * T, T), at(TM + 3 * T, T)
                wreg(v, "dve", mg_sig, 2 * n + 4)
                wreg(v, "dve", mg_mm[2][0], n + (mg_mm[2][1] + 1))
                v.tensor_tensor(s0, s0, ps[2][:, 0:T], ALU.mult).then_inc(mg_t, 1)
                wreg(v, "dve", mg_mm[3][0], n + (mg_mm[3][1] + 1))
                v.tensor_tensor(s1, s1, ps[3][:, 0:T], ALU.mult).then_inc(mg_t, 1)
                wreg(v, "dve", mg_t, 2 * n + 2)
                v.tensor_tensor(mT[:, bass.ds(n, 1), :].rearrange("p a n -> p (a n)"), s0, s1, ALU.add).then_inc(mg_out, 1)
            v.sem_inc(wo_add, 5)
            v.wait_ge(xr_ld[0], xr_ld[1] + 32)
            with v.Fori(0, NOC // 2) as i:
                for r in range(2):
                    for t in range(TILES):
                        b = (r * TILES + t) % 5
                        wreg(v, "dve", wo_mm, (2 * i + r) * TILES + t + 1)
                        dst = x1[:, t, bass.ds((2 * i + r) * OCW, OCW)]
                        v.tensor_tensor(dst, dst, ps[b // 2][:, (b % 2) * 512:(b % 2) * 512 + OCW], ALU.add).then_inc(wo_add, 1)
            v.wait_ge(n2_sumsq[0], n2_sumsq[1] + TILES)
            link(v.tensor_scalar(small[:, 8:8 + TILES], small[:, 0:TILES], 1.0 / D, EPS, ALU.mult, ALU.add))
            v.sem_inc(n2_msq[0], 1)
            v.wait_ge(n2_root[0], n2_root[1] + 1)
            link(v.reciprocal(small[:, 24:24 + TILES], small[:, 16:16 + TILES]))
            v.wait_ge(g_ld[0], g_ld[1] + 16)

            def evac_n2(n):
                t, half = n // 2, n % 2
                v.wait_ge(n2_tr[0], n2_tr[1] + n + 1)
                v.tensor_copy(xn2T[:, 8 * half:8 * half + 8, t * P:(t + 1) * P], ps8(n % 4)).then_inc(n2_evac[0], 1)
            for t in range(TILES):
                v.scalar_tensor_tensor(xn2[:, t, :], x1[:, t, :], small[:, 24 + t:25 + t], at(WR + 4 * D, D), ALU.mult, ALU.mult).then_inc(n2_done[0], 1)
                if t:
                    evac_n2(2 * t - 2)
                    evac_n2(2 * t - 1)
            evac_n2(2 * TILES - 2)
            evac_n2(2 * TILES - 1)
            v.sem_inc(tk_done, 1)
            NTK = 3 * TILES + 2
            with v.Fori(0, HP) as j:
                n = [0]

                def tk(ins):
                    n[0] += 1
                    ins.then_inc(tk_link, 1)
                wreg(v, "dve", s_evac, j + 2)
                sc, sc2 = at(SC, TILES, P), at(SC2, TILES, P)
                top = topbuf
                for t in range(TILES):
                    tk(v.max(top[:, t, 0:8], sc[:, t, :]))
                wreg(v, "dve", tk_link, j * NTK + TILES)
                for t in range(TILES):
                    v.max_index(itop_u[:, t, 0:8], top[:, t, 0:8], sc[:, t, :])
                    tk(v.match_replace(sc2[:, t, :], top[:, t, 0:8], sc[:, t, :], -3.0e38))
                wreg(v, "dve", tk_link, j * NTK + 2 * TILES)
                for t in range(TILES):
                    tk(v.max(top[:, t, 8:16], sc2[:, t, :]))
                wreg(v, "dve", tk_link, j * NTK + 3 * TILES)
                for t in range(TILES):
                    ins = v.max_index(itop_u[:, t, 8:16], top[:, t, 8:16], sc2[:, t, :])
                tk(ins)
                wreg(v, "dve", tk_link, j * NTK + 3 * TILES + 1)
                v.tensor_copy(stop_[:, :, bass.ds(j * TOPK, TOPK)], top)
                tk(v.tensor_copy(itop[:, :, bass.ds(j * TOPK, TOPK)], itop_u))
                wreg(v, "dve", tk_link, j * NTK + NTK)
                v.sem_inc(tk_done, 1)
            v.wait_ge(s_evac, HP + 1)
            v.wait_ge(spilled, 48)
            sl = Link(v, "dve", sel_link)
            v.wait_ge(iota_done, 1)
            cand = at(KT, PH, TOPK * TOPK)
            cand2 = at(KT + 2048, PH, TOPK * TOPK)
            oh = at(KT + 4096, PH * TOPK, TOPK)
            oh4 = at(KT + 4096, PH, TOPK, TOPK)
            val = at(KT + 6144, PH * TOPK)
            posf = at(KT + 6144 + 128, 2, PH * TOPK)
            got = at(KT + 6144 + 384, 2, PH * TOPK)
            stf = at(KT + 6144 + 640, PH, TOPK)
            red = at(KT + 6144 + 768, PH)
            posi = posu2
            for t in range(TILES):
                s4 = stop_[:, t, :].rearrange("p (h q k) -> p h q k", h=PH, q=2)
                i4 = itop[:, t, :].rearrange("p (h q k) -> p h q k", h=PH, q=2)
                sl(v.tensor_tensor(cand.rearrange("p h (a b) -> p h a b", a=TOPK), s4[:, :, 0, :].unsqueeze(3).to_broadcast([P, PH, TOPK, TOPK]),
                                   s4[:, :, 1, :].unsqueeze(2).to_broadcast([P, PH, TOPK, TOPK]), ALU.add))
                pu = posu.rearrange("p (h k) -> p h k", h=PH)
                for h in range(PH):
                    ins = v.max(stf[:, h, 0:8], cand[:, h, :])
                sl(ins)
                for h in range(PH):
                    v.max_index(pu[:, h, 0:8], stf[:, h, 0:8], cand[:, h, :])
                    ins = v.match_replace(cand2[:, h, :], stf[:, h, 0:8], cand[:, h, :], -3.0e38)
                sl(ins)
                for h in range(PH):
                    ins = v.max(stf[:, h, 8:16], cand2[:, h, :])
                sl(ins)
                for h in range(PH):
                    ins = v.max_index(pu[:, h, 8:16], stf[:, h, 8:16], cand2[:, h, :])
                sl(ins)
                gt = gate_of(t).rearrange("p (h k) -> p h k", h=PH)
                v.tensor_tensor(gt, stf, stf[:, :, 0:1].to_broadcast([P, PH, TOPK]), ALU.subtract).then_inc(sel_pre, 1)
                v.tensor_scalar(posi[:, 0, :], posu, 4, None, ALU.logical_shift_right)
                sl(v.tensor_scalar(posi[:, 1, :], posu, 15, None, ALU.bitwise_and))
                sl(v.tensor_copy(posf, posi))
                for q in range(2):
                    sl(v.tensor_tensor(oh, iota16[:].unsqueeze(1).to_broadcast([P, PH * TOPK, TOPK]),
                                       posf[:, q, :].unsqueeze(2).to_broadcast([P, PH * TOPK, TOPK]), ALU.is_equal))
                    for h in range(PH):
                        ins = v.tensor_tensor(oh4[:, h], oh4[:, h], i4[:, h, q, :].unsqueeze(1).to_broadcast([P, TOPK, TOPK]), ALU.mult)
                    sl(ins)
                    sl(v.tensor_reduce(chosen[:, 3 * t + q, :] if t < DT else got[:, q, :], oh, X, ALU.add))
                if t >= DT:
                    sl(v.scalar_tensor_tensor(val, got[:, 0, :], float(NK), got[:, 1, :], ALU.mult, ALU.add))
                    sl(v.tensor_copy(gidx[:, t - DT, :], val))
                v.wait_ge(sel_exp, t + 1)
                sl(v.tensor_reduce(red, gt, X, ALU.add))
                sl(v.reciprocal(red, red))
                sl(v.tensor_tensor(gt, gt, red.unsqueeze(2).to_broadcast([P, PH, TOPK]), ALU.mult))
            v.sem_inc(selected, 1)

        @block.gpsimd
        def _(pool):
            pool.iota(iota_i[:], pattern=[[1, TOPK]], base=0, channel_multiplier=0).then_inc(p_link, 1)
            pool.wait_ge(p_link, 1)
            pool.tensor_copy(iota16[:], iota_i[:]).then_inc(iota_done, 1)
            pool.wait_ge(ld_par, 64)
            for s in stage_done.values():
                pool.sem_inc(s, 1)
            pool.wait_ge(cconv_done, 1)
            with pool.Fori(0, NC) as c:
                for i, kd in enumerate("qkv"):
                    wreg(pool, "pool", conv_done[kd], c + 1)
                    sg = seg(qpad(kd), NT + DCW - 1, DCW - 1)
                    pool.tensor_copy(sg[:, :, 0:DCW - 1], dpre[:, bass.ds(c * NB + i * H * NB, NB), :]).then_inc(prefix_done[kd], 1)
                for i, kd in enumerate("qkv"):
                    wreg(pool, "pool", evac[kd], c + 1)
                    pool.tensor_copy(dnew_p[:, bass.ds(c + i * H, 1), :].rearrange("p a n -> p (a n)"), qpad(kd)[:, NP_TOK:NP_TOK + DCW - 1])
                    pool.tensor_copy(dnew_s[:, bass.ds(c * NB + i * H * NB, NB), :],
                                     seg(qpad(kd), NT + DCW - 1, DCW - 1)[:, :, NT:]).then_inc(stage_done[kd], 1)
                wreg(pool, "pool", cconv_done, c + 1)
                cp = at(CPB, CPAD)
                sg = seg(cp, NT + CW - 1, CW - 1)
                pool.dma_start(sg[:, :, 0:CW - 1], conv_prefix[bass.ds(c, 1)].rearrange("a p b n -> p (a b) n")).then_inc(prefix_done["c"], 16)
                wreg(pool, "pool", glu_done, c + 2)
                pool.dma_start(conv_new_p[bass.ds(c, 1)].rearrange("a p n -> p (a n)"), cp[:, NP_TOK:NP_TOK + CW - 1]).then_inc(cstate_out, 16)
                pool.dma_start(conv_new_s[bass.ds(c * NB, NB)].rearrange("b p n -> p b n"), sg[:, :, NT:]).then_inc(cstate_out, 16)
                wreg(pool, "pool", cstate_out, c * 32 + 32)

        mixer.close()

        with nc.Block() as between:
            @between.gpsimd
            def _(pool):
                for s in first_sems:
                    pool.sem_clear(s)
        first.close()

        def sb2(name, shape, dt=F32):
            return ctx.enter_context(nc.sbuf_tensor(name, shape, dt))

        def sem2(name):
            return ctx.enter_context(nc.semaphore(name))

        xhi, xlo = sb2("xhi", [P, KD, TD], F32R), sb2("xlo", [P, KD, TD], F32R)
        whi, wlo = sb2("whi", [P, 2, UNIT], F32R), sb2("wlo", [P, 2, UNIT], F32R)
        ahi, alo = sb2("ahi", [P, ET, TD], F32R), sb2("alo", [P, ET, TD], F32R)
        rows2 = sb2("rows2", [P, 2 * GT * D])
        x1g = rows2[:, 0:GT * D].rearrange("p (t d) -> p t d", t=GT)
        xg = rows2[:, GT * D:2 * GT * D].rearrange("p (t d) -> p t d", t=GT)
        xT = rows2[:, 0:KD * TD].rearrange("p (k t) -> p k t", k=KD)
        assert KD * TD <= 2 * GT * D
        sel = sb2("sel", [P, SELW])
        chosen2 = sel[:, 0:3 * DT * SLOTS].rearrange("p (a s) -> p a s", s=SLOTS)
        gidx2 = sel[:, 3 * DT * SLOTS:(3 * DT + GT) * SLOTS].rearrange("p (a s) -> p a s", s=SLOTS).bitcast(U32)
        ggate2 = sel[:, (3 * DT + GT) * SLOTS:].rearrange("p (a s) -> p a s", s=SLOTS)
        gbuf, hbuf = sb2("gbuf", [P, 2, TD]), sb2("hbuf", [P, 2, TD])
        work = sb2("work", [P, KD * TD + 4 * D + 4 * UNIT])

        def wk(off, *dims):
            n = 1
            for d in dims:
                n *= d
            w = work[:, off:off + n]
            if len(dims) == 2:
                w = w.rearrange("p (a b) -> p a b", a=dims[0])
            return w

        ROWS, RAW = KD * TD, KD * TD + 4 * D
        accT = wk(0, KD, TD)
        urow = [wk(ROWS + i * D, D) for i in range(2)]
        vrow = [wk(ROWS + (2 + i) * D, D) for i in range(2)]
        raw = [wk(RAW + i * UNIT, UNIT) for i in range(4)]
        stage = [wk(0, NK, GTOK), wk(NK * GTOK, NK, GTOK)]
        OH = 2 * NK * GTOK
        oneh = [[wk(OH + (2 * i + q) * GB * NK, GB, NK) for q in range(2)] for i in range(2)]
        selT = wk(OH + 4 * GB * NK, 3, TD)
        fin_dense = wk(ROWS, DT, D)
        fin_gain = wk(ROWS + DT * D, D)
        fin_junk = wk(RAW, D)
        iota_i2, iota_k = sb2("iota_i2", [P, NK], mybir.dt.int32), sb2("iota_k", [P, NK])
        cur_idx = sb2("cur_idx", [P, 2, RING], U32)
        hid, act_w, gcol, act_w2 = (sb2(n, [P, RING]) for n in ("hid", "act_w", "gcol", "act_w2"))
        fin_small = sb2("fin_small", [P, 3, TILES])

        pace2 = {e: sem2(f"pace2_{e}") for e in ("sp", "act", "pe", "dve", "pool")}

        def wait_count(eng, name, s, v):
            eng.wait_ge(s, v)
            eng.sem_inc(pace2[name], 1)

        sel_ld, xT_ld, rows_ld, xsplit, iota_ready = (sem2(n) for n in ("sel_ld", "xT_ld", "rows_ld", "xsplit", "iota_ready"))
        sel_tr, sel_cp, oh_key, oh_row, oh_done, g_mm, g_evac = (
            sem2(n) for n in ("sel_tr", "sel_cp", "oh_key", "oh_row", "oh_done", "g_mm", "g_evac"))
        g_out = [sem2("g_out0"), sem2("g_out1")]
        un_ld = [sem2(f"un_ld{i}") for i in range(4)]
        gt_ld = [sem2("gt_ld0"), sem2("gt_ld1")]
        hi_done, lo_done, unit_free, hid_mm, v_mm = (sem2(n) for n in ("hi_done", "lo_done", "unit_free", "hid_mm", "v_mm"))
        gelu_done, a_raw, a_split, a_done, v_add, zeroed = (sem2(n) for n in ("gelu_done", "a_raw", "a_split", "a_done", "v_add", "zeroed"))
        idx_cur, ghid, ggelu, gcoef, u_used, v_used = (sem2(n) for n in ("idx_cur", "ghid", "ggelu", "gcoef", "u_used", "v_used"))
        u_ld = [sem2(f"u_ld{i}") for i in range(RING)]
        v_ld = [sem2(f"v_ld{i}") for i in range(RING)]
        f_begin, f_tr, f_add, f_ld, f_ss, f_ms, f_root, f_y, f_out = (
            sem2("f_" + n) for n in ("begin", "tr", "add", "ld", "ss", "ms", "root", "y", "out"))
        NBB = GTOK // GB
        NGG = TD // GTOK
        CPG = CHUNKS // GT
        block2 = ctx.enter_context(nc.Block())

        def fin_rows(t):
            return fin_dense[:, t, :] if t < DT else x1g[:, t - DT, :]

        FIN_ORDER = [*range(DT, TILES), *range(DT)]

        @block2.sync
        def _(sp):
            sp.dma_start(sel[:], sel_spill).then_inc(sel_ld, 16)
            sp.dma_start(xT, xT_spill).then_inc(xT_ld, 16)
            sp.wait_ge(xsplit, 2)
            sp.dma_start(rows2[:, 0:GT * D], x1_spill[:, DT * D:]).then_inc(rows_ld, 16)
            sp.dma_start(rows2[:, GT * D:], xg_spill).then_inc(rows_ld, 16)
            for n in range(NGG):
                sp.wait_ge(g_evac, (n + 1) * NBB + 2)
                sp.dma_start(gates_dram.rearrange("i j t -> j i t")[:, :, n * GTOK:(n + 1) * GTOK], stage[n % 2]).then_inc(g_out[n % 2], 16)
            for n in range(2):
                sp.wait_ge(g_out[n], 16 * (NGG // 2))
            sp.wait_ge(g_mm, NGG * NBB + 2)
            sp.wait_ge(sel_cp, 3)
            with sp.Fori(0, CHUNKS) as c:
                for m in range(NU):
                    wait_count(sp, "sp", lo_done, c * NU + m + 1)
                    src = u_units[bass.ds(c * (2 * ET) + m, 1)] if m < 2 * ET else v_units[bass.ds(c * (NU - 2 * ET) + m - 2 * ET, 1)]
                    sp.dma_start(raw[m % 4], src.rearrange("a p n -> p (a n)")).then_inc(un_ld[m % 4], 16)
                    if m % 2 == 0 and 2 <= m <= 2 * ET:
                        e = m // 2 - 1
                        wait_count(sp, "sp", a_raw, c * ET + e + 1)
                        sp.dma_start(gbuf[:, e % 2, :], gates_dram[bass.ds(c * ET + e, 1)].rearrange("a p n -> p (a n)")).then_inc(gt_ld[e % 2], 16)
            sp.wait_ge(f_begin, 1)
            sp.dma_start(fin_gain, final_g).then_inc(f_ld, 16)
            sp.dma_start(wk(ROWS, DT * D), x1_spill[:, 0:DT * D]).then_inc(f_ld, 16)
            for i, t in enumerate(FIN_ORDER):
                sp.wait_ge(f_y, i + 1)
                dst = y_prompt[t * P:(t + 1) * P, :] if t < PT else y_sample
                sp.dma_start(dst, fin_rows(t)).then_inc(f_out, 16)
            sp.wait_ge(f_out, 16 * TILES)

        @block2.tensor
        def _(pe):
            pe.wait_ge(sel_ld, 16)
            for a in range(3):
                for t in range(DT):
                    m = pe.transpose(ps[a // 2][:, (a % 2) * 512 + t * P:(a % 2) * 512 + (t + 1) * P], chosen2[:, 3 * t + a, :], ident)
            m.then_inc(sel_tr, 1)
            pe.wait_ge(sel_cp, 3)
            pe.sem_inc(g_mm, 2)
            with pe.Fori(0, NGG * NBB // 2) as i:
                for r in range(2):
                    wait_count(pe, "pe", oh_key, 2 * i + r + 1)
                    wait_count(pe, "pe", oh_done, 2 * i + r + 1)
                    wait_count(pe, "pe", g_evac, 2 * i + r + 1)
                    for b in range(GB):
                        m = pe.matmul(ps[2 + r][:, b * P:(b + 1) * P], oneh[r][0][:, b, :], oneh[r][1][:, b, :], start=True, stop=True)
                    m.then_inc(g_mm, 1)
            pe.wait_ge(g_evac, NGG * NBB + 2)
            pe.wait_ge(xsplit, 2)
            pe.sem_inc(unit_free, 2)
            with pe.Fori(0, CHUNKS) as c:
                for m in range(NU):
                    wait_count(pe, "pe", hi_done, c * NU + m + 1)
                    if m < 2 * ET:
                        e, half = m // 2, m % 2
                        out = ps[0][:, (e % 2) * 512:(e % 2) * 512 + TD]
                        if half == 0:
                            wait_count(pe, "pe", gelu_done, c * ET + e + 1)
                        h3, l3 = (w[:, m % 2, :].rearrange("p (k c) -> p k c", k=8) for w in (whi, wlo))
                        for k in range(8):
                            pe.matmul(out, h3[:, k, :], xhi[:, 8 * half + k, :], start=half == 0 and k == 0, stop=False)
                            pe.matmul(out, h3[:, k, :], xlo[:, 8 * half + k, :], start=False, stop=False)
                        wait_count(pe, "pe", lo_done, c * NU + m + 5)
                        for k in range(8):
                            mmi = pe.matmul(out, l3[:, k, :], xhi[:, 8 * half + k, :], start=False, stop=half == 1 and k == 7)
                        mmi.then_inc(unit_free, 1)
                        if half == 1:
                            wait_count(pe, "pe", unit_free, c * NU + m + 3)
                            pe.sem_inc(hid_mm, 1)
                    else:
                        h4, l4 = (w[:, m % 2, :].rearrange("p (d e c) -> p d e c", d=2, e=ET) for w in (whi, wlo))
                        for q in range(2):
                            d = 2 * (m - 2 * ET) + q
                            out = ps[1 + (d % 4) // 2][:, (d % 2) * 512:(d % 2) * 512 + TD]
                            wait_count(pe, "pe", v_add, c * KD + d + 1)
                            for e in range(ET):
                                if d == 0:
                                    wait_count(pe, "pe", a_done, c * ET + e + 3)
                                pe.matmul(out, h4[:, q, e, :], ahi[:, e, :], start=e == 0, stop=False)
                                pe.matmul(out, h4[:, q, e, :], alo[:, e, :], start=False, stop=False)
                            if q == 0:
                                wait_count(pe, "pe", lo_done, c * NU + m + 5)
                            for e in range(ET):
                                mmi = pe.matmul(out, l4[:, q, e, :], ahi[:, e, :], start=False, stop=e == ET - 1)
                            mmi.then_inc(v_mm, 1)
                        wait_count(pe, "pe", v_mm, c * KD + d + 1)
                        pe.sem_inc(unit_free, 1)
            pe.wait_ge(f_begin, 1)
            for t in range(DT):
                for half in range(2):
                    n = 2 * t + half
                    if n >= 4:
                        pe.wait_ge(f_add, n - 3)
                    for k in range(8):
                        mt = pe.transpose(ps[n % 4][:, k * P:(k + 1) * P], accT[:, half * 8 + k, t * P:(t + 1) * P], ident)
                    mt.then_inc(f_tr, 1)

        @block2.scalar
        def _(act):
            act.sem_inc(g_evac, 2)
            for n in range(NGG):
                if n >= 2:
                    act.wait_ge(g_out[n % 2], 16 * (n // 2))
                for b in range(NBB):
                    q = n * NBB + b
                    act.wait_ge(g_mm, q + 3)
                    act.activation(stage[n % 2][:, :, b * GB:(b + 1) * GB],
                                   ps[2 + q % 2][:].rearrange("p (b i) -> p i b", b=GB), ACT.Copy).then_inc(g_evac, 1)
            act.sem_inc(gelu_done, 2)

            def gelu_tile(c, e):
                wait_count(act, "act", hid_mm, c * ET + e + 1)
                wait_count(act, "act", a_done, c * ET + e + 1)
                act.activation(hbuf[:, e % 2, :], ps[0][:, (e % 2) * 512:(e % 2) * 512 + TD], ACT.Gelu_apprx_tanh).then_inc(gelu_done, 1)

            with act.Fori(0, CHUNKS) as c:
                for m in range(NU):
                    wait_count(act, "act", un_ld[m % 4], (c * (NU // 4) + m // 4) * 16 + 16)
                    wait_count(act, "act", unit_free, c * NU + m + 1)
                    act.activation(whi[:, m % 2, :], raw[m % 4], ACT.Copy).then_inc(hi_done, 1)
                    if 3 <= m < 2 * ET and m % 2 == 1:
                        gelu_tile(c, m // 2 - 1)
                    if m == 2 * ET:
                        gelu_tile(c, ET - 1)
                    if m % 4 == 2:
                        wait_count(act, "act", ghid, c * STEPS + m // 4 + 1)
                        act.activation(act_w[:], hid[:], ACT.Gelu_apprx_tanh).then_inc(ggelu, 1)
            for i in range(TILES):
                act.wait_ge(f_ss, i + 1)
                act.activation(fin_small[:, 1, i:i + 1], fin_small[:, 0, i:i + 1], ACT.Sqrt).then_inc(f_root, 1)

        @block2.vector
        def _(v):
            v.wait_ge(sel_tr, 1)
            for a in range(3):
                v.tensor_copy(selT[:, a, :], ps[a // 2][:, (a % 2) * 512:(a % 2) * 512 + TD]).then_inc(sel_cp, 1)
            v.wait_ge(sel_cp, 3)
            v.wait_ge(xT_ld, 16)
            v.tensor_copy(xhi[:], xT).then_inc(xsplit, 1)
            v.wait_ge(xsplit, 1)
            v.tensor_tensor(xlo[:], xT, xhi[:].bitcast(F32), ALU.subtract).then_inc(xsplit, 1)
            v.wait_ge(iota_ready, 2)
            iota_b = iota_k[:].unsqueeze(1).to_broadcast([P, GB, NK])
            with v.Fori(0, NGG * NBB // 2) as i:
                for r in range(2):
                    tok = bass.ds((2 * i + r) * GB, GB)
                    wait_count(v, "dve", g_mm, 2 * i + r + 1)
                    v.tensor_tensor(oneh[r][1], iota_b, selT[:, 0, tok].unsqueeze(2).to_broadcast([P, GB, NK]), ALU.is_equal).then_inc(oh_row, 1)
                    v.tensor_tensor(oneh[r][0], iota_b, selT[:, 1, tok].unsqueeze(2).to_broadcast([P, GB, NK]), ALU.is_equal).then_inc(oh_key, 1)
            for n in range(2):
                v.wait_ge(g_out[n], 16 * (NGG // 2))
            v.memset(accT, 0.0).then_inc(zeroed, 1)
            v.sem_inc(v_add, 4)
            v.sem_inc(a_raw, 2)
            v.sem_inc(a_done, 2)
            v.wait_ge(g_mm, NGG * NBB + 2)
            v.sem_inc(u_used, RING)
            v.sem_inc(v_used, RING)
            v.wait_ge(zeroed, 1)
            v.wait_ge(rows_ld, 32)

            def hidden(c, e):
                h = hbuf[:, e % 2, :]
                wait_count(v, "dve", gelu_done, c * ET + e + 3)
                wait_count(v, "dve", gt_ld[e % 2], (c * (ET // 2) + e // 2) * 16 + 16)
                v.tensor_tensor(h, h, gbuf[:, e % 2, :], ALU.mult).then_inc(a_raw, 1)
                if e == 0:
                    wait_count(v, "dve", unit_free, c * NU + 2)
                wait_count(v, "dve", a_raw, c * ET + e + 3)
                v.tensor_copy(ahi[:, e, :], h).then_inc(a_split, 1)
                wait_count(v, "dve", a_split, c * ET + e + 1)
                v.tensor_tensor(alo[:, e, :], h, ahi[:, e, :].bitcast(F32), ALU.subtract).then_inc(a_done, 1)

            def add(c, d):
                wait_count(v, "dve", v_mm, c * KD + d + 1)
                wait_count(v, "dve", v_add, c * KD + d + 1)
                src = ps[1 + (d % 4) // 2][:, (d % 2) * 512:(d % 2) * 512 + TD]
                v.tensor_tensor(accT[:, d, :], accT[:, d, :], src, ALU.add).then_inc(v_add, 1)

            for gt in range(GT):
                with v.Fori(0, CPG) as cc:
                    c = cc + gt * CPG
                    for m in range(NU):
                        it = c * STEPS + m // 4
                        r = m % 2
                        if m % 4 == 0:
                            v.tensor_copy(gcol[:], ggate2[:, gt, bass.ds((cc * STEPS + m // 4) * RING, RING)]).then_inc(gcoef, 1)
                        if m % 4 < 2:
                            wait_count(v, "dve", u_ld[r], it * 16 + 16)
                            v.tensor_tensor_reduce(out=urow[r], in0=urow[r], in1=xg[:, gt, :], scale=1.0, scalar=0.0, op0=ALU.mult,
                                                   op1=ALU.add, accum_out=hid[:, r:r + 1]).then_inc(u_used, 1)
                            if r == 1:
                                wait_count(v, "dve", u_used, it * RING + 2 * RING)
                                v.sem_inc(ghid, 1)
                        else:
                            if r == 0:
                                wait_count(v, "dve", ggelu, it + 1)
                                wait_count(v, "dve", gcoef, 2 * it + 1)
                                v.tensor_tensor(act_w2[:], act_w[:], gcol[:], ALU.mult).then_inc(gcoef, 1)
                                wait_count(v, "dve", gcoef, 2 * it + 2)
                            wait_count(v, "dve", v_ld[r], it * 16 + 16)
                            v.scalar_tensor_tensor(x1g[:, gt, :], vrow[r], act_w2[:, r:r + 1], x1g[:, gt, :], ALU.mult, ALU.add).then_inc(v_used, 1)
                            wait_count(v, "dve", v_used, it * RING + RING + r + 1)
                        if 3 <= m < 2 * ET and m % 2 == 1:
                            hidden(c, m // 2 - 1)
                        elif m == 2 * ET:
                            hidden(c, ET - 1)
                        elif m > 2 * ET:
                            add(c, 2 * (m - 2 * ET) - 2)
                            add(c, 2 * (m - 2 * ET) - 1)
                    add(c, KD - 2)
                    add(c, KD - 1)
            v.wait_ge(v_add, CHUNKS * KD + 4)
            v.wait_ge(lo_done, CHUNKS * NU + 4)
            v.sem_inc(f_begin, 1)

            def final(i, t):
                rows = fin_rows(t)
                v.tensor_tensor_reduce(out=fin_junk, in0=rows, in1=rows, scale=1.0 / D, scalar=EPS,
                                       op0=ALU.mult, op1=ALU.add, accum_out=fin_small[:, 0, i:i + 1]).then_inc(f_ms, 1)
                v.wait_ge(f_ms, 2 * i + 1)
                v.sem_inc(f_ss, 1)
                v.wait_ge(f_root, i + 1)
                v.reciprocal(fin_small[:, 2, i:i + 1], fin_small[:, 1, i:i + 1]).then_inc(f_ms, 1)
                v.wait_ge(f_ms, 2 * i + 2)
                v.scalar_tensor_tensor(rows, rows, fin_small[:, 2, i:i + 1], fin_gain, ALU.mult, ALU.mult).then_inc(f_y, 1)

            v.wait_ge(f_ld, 32)
            for i, t in enumerate(FIN_ORDER):
                if t < DT:
                    for half in range(2):
                        v.wait_ge(f_tr, 2 * t + half + 1)
                        rows = fin_dense[:, t, half * 1024:(half + 1) * 1024]
                        v.tensor_tensor(rows, rows, ps[(2 * t + half) % 4][:], ALU.add).then_inc(f_add, 1)
                    v.wait_ge(f_add, 2 * t + 2)
                final(i, t)

        @block2.gpsimd
        def _(pool):
            pool.iota(iota_i2[:], pattern=[[1, NK]], base=0, channel_multiplier=0).then_inc(iota_ready, 1)
            pool.wait_ge(iota_ready, 1)
            pool.tensor_copy(iota_k[:], iota_i2[:]).then_inc(iota_ready, 1)
            pool.wait_ge(sel_cp, 3)
            with pool.Fori(0, NGG * NBB // 2) as i:
                for r in range(2):
                    row = oneh[r][1]
                    wait_count(pool, "pool", oh_row, 2 * i + r + 1)
                    pool.tensor_tensor(row, row, selT[:, 2, bass.ds((2 * i + r) * GB, GB)].unsqueeze(2).to_broadcast([P, GB, NK]),
                                       ALU.mult).then_inc(oh_done, 1)
            pool.sem_inc(lo_done, 4)
            for gt in range(GT):
                with pool.Fori(0, CPG) as cc:
                    c = cc + gt * CPG
                    for m in range(NU):
                        it = c * STEPS + m // 4
                        r, turn = m % 2, (m // 4) % 2
                        if m % 4 == 0:
                            pool.tensor_copy(cur_idx[:, turn, :], gidx2[:, gt, bass.ds((cc * STEPS + m // 4) * RING, RING)]).then_inc(idx_cur, 1)
                            wait_count(pool, "pool", idx_cur, it + 1)
                        rows, table, used, ld = (urow, peer_u, u_used, u_ld) if m % 4 < 2 else (vrow, peer_v, v_used, v_ld)
                        wait_count(pool, "pool", used, it * RING + r + 1)
                        pool.indirect_dma_start(out=rows[r], out_offset=None, in_=table,
                                                in_offset=bass.IndirectOffsetOnAxis(ap=cur_idx[:, turn, r:r + 1], axis=0)).then_inc(ld[r], 16)
                        wait_count(pool, "pool", hi_done, c * NU + m + 1)
                        pool.tensor_tensor(wlo[:, m % 2, :], raw[m % 4], whi[:, m % 2, :].bitcast(F32), ALU.subtract).then_inc(lo_done, 1)


def constant_matrices():
    import numpy as np
    i = np.arange(P)
    r, c = i[:, None], i[None, :]
    blk = (r // NT == c // NT)
    mats = [r == c, np.ones((P, P), bool), r <= c, (r <= c) & blk, blk]
    for l in range(LEVELS):
        s = 1 << l
        mats.append((r // (2 * s) == c // (2 * s)) & (r % (2 * s) < s) & (c % (2 * s) >= s))
    return np.ascontiguousarray(np.stack([m.astype(np.float32) for m in mats], 1))


def kernel(**inp):
    import numpy as np
    import concourse.bacc as bacc
    from concourse.bass_utils import run_bass_kernel_spmd as run

    a = {k: np.asarray(v) for k, v in inp.items()}

    def cols(v):
        return v.reshape(-1, P).T

    def tiles(w):
        k, n = w.shape
        return w.reshape(k // P, P, n // P, P).transpose(2, 1, 0, 3).reshape(n // P, P, k)

    w_in = a["w_in"][0]
    o = 2 * CONV + 3 * H * P
    w_glu, w_qkv, w_ba, w_z, w_g = (w_in[:, :2 * CONV], w_in[:, 2 * CONV:o], w_in[:, o:o + 2 * H],
                                    w_in[:, o + 2 * H:o + 2 * H + H * P], w_in[:, o + 2 * H + H * P:])
    tg, tq = tiles(w_glu), tiles(w_qkv)
    w_group = np.stack([tq[:H], tq[H:2 * H], tq[2 * H:], tg[NC:], tg[:NC]], 1).reshape(5 * NC, P, D)
    tgt, tp, to = tiles(w_g), tiles(a["conv_pw2"][0]), tiles(a["dn_w_o"][0])
    w_merge = np.stack([tgt[:KD], tgt[KD:], np.concatenate([tp, to], 2)], 1).reshape(3 * KD, P, D)
    cw = a["conv_dw_w"][0].T.reshape(NC, P, CW).transpose(1, 0, 2).reshape(P, -1)
    dw = a["dn_conv_w"][0].T.reshape(3 * H, P, DCW).transpose(1, 0, 2).reshape(P, -1)
    params = np.concatenate([cols(a["norm_mix_g"][0]), cw, cols(a["conv_dw_b"][0]), cols(a["conv_ln_g"][0]), cols(a["conv_ln_b"][0]),
                             dw, cols(a["dn_norm_g"][0]), np.broadcast_to(a["dn_dt_bias"][0], (P, H)),
                             np.broadcast_to(a["dn_a_log"][0], (P, H))], 1)
    u_units = a["peer_u"][0].reshape(NK, P, 2, 8, P).transpose(0, 2, 4, 3, 1).reshape(2 * NK, P, UNIT)
    v_units = a["peer_v"][0].reshape(CHUNKS, ET, P, KD // 2, 2, P).transpose(0, 3, 2, 4, 1, 5).reshape(CHUNKS * KD // 2, P, UNIT)
    ins = {
        "x_prompt": a["x_prompt"][0],
        "x_sample": a["x_sample"].reshape(P, D),
        "consts": constant_matrices(),
        "params": params,
        "conv_prefix": a["state_conformer_conv"][0].reshape(NB, CW - 1, NC, P).transpose(2, 3, 0, 1),
        "dconv_prefix": a["state_delta_conv"][0].reshape(NB, DCW - 1, 3 * H, P).transpose(3, 2, 0, 1).reshape(P, 3 * H * NB, DCW - 1),
        "state_in": a["state_delta"][0].transpose(2, 1, 0, 3).reshape(P, H * NB * P),
        "w_ba": w_ba.reshape(KD, P, 2 * H).transpose(1, 0, 2),
        "w_group": w_group,
        "w_z": tiles(w_z),
        "w_merge": w_merge,
        "w_out": a["w_out"][0].reshape(KD, P, NOC, OCW).transpose(2, 1, 0, 3).reshape(NOC, P, KD * OCW),
        "w_q": tiles(a["peer_w_q"][0]),
        "keys": a["peer_sub_keys"][0].reshape(HP, NK, P).transpose(2, 0, 1).reshape(P, HP * NK),
        "ffn_g": np.broadcast_to(a["norm_ffn_g"][0], (P, D)),
        "final_g": np.broadcast_to(a["norm_final_g"], (P, D)),
        "peer_u": a["peer_u"][0],
        "peer_v": a["peer_v"][0],
        "u_units": u_units,
        "v_units": v_units,
    }
    outs = {
        "y_prompt": (NP_TOK, D), "y_sample": (P, D),
        "conv_new_p": (NC, P, CW - 1), "dconv_new_p": (P, 3 * H, DCW - 1), "state_new_p": (P, H * P),
        "conv_new_s": (NC * NB, P, CW - 1), "dconv_new_s": (P, 3 * H * NB, DCW - 1), "state_new_s": (P, H * NB * P),
    }
    nc = bacc.Bacc("TRN2", target_bir_lowering=False, num_devices=1)
    arrays = {f"in_{k}": np.ascontiguousarray(v) for k, v in ins.items()}
    args = [nc.dram_tensor(k, v.shape, F32, kind="ExternalInput").ap() for k, v in arrays.items()]
    args += [nc.dram_tensor(f"out_{k}", s, F32, kind="ExternalOutput").ap() for k, s in outs.items()]
    build(nc, *args)
    r = run(nc, [arrays], core_ids=[0])
    g = {k: r.results[0][f"out_{k}"] for k in outs}
    return (
        g["y_prompt"].reshape(1, NP_TOK, D),
        g["y_sample"].reshape(NB, NT, D),
        g["conv_new_p"].transpose(2, 0, 1).reshape(1, 1, CW - 1, CONV),
        g["dconv_new_p"].transpose(2, 1, 0).reshape(1, 1, DCW - 1, 3 * H * P),
        g["state_new_p"].reshape(P, H, P).transpose(1, 0, 2).reshape(1, 1, H, P, P),
        g["conv_new_s"].reshape(NC, NB, P, CW - 1).transpose(1, 3, 0, 2).reshape(1, NB, CW - 1, CONV),
        g["dconv_new_s"].reshape(P, 3 * H, NB, DCW - 1).transpose(2, 3, 1, 0).reshape(1, NB, DCW - 1, 3 * H * P),
        g["state_new_s"].reshape(P, H, NB, P).transpose(2, 1, 0, 3).reshape(1, NB, H, P, P),
    )
```

```python
from contextlib import ExitStack

import concourse.bass as bass
from concourse import mybir

P = 128
D = 2048
NP_TOK = 512
NB, NT = 8, 16
T = NP_TOK + NB * NT
TILES = T // P
PT = NP_TOK // P
KD = D // P
CONV = 1024
CW = 31
NC = CONV // P
H = 8
DCW = 4
PH = 8
TOPK = 16
NK = 128
NE = NK * NK
HP = 2 * PH
SLOTS = PH * TOPK
EPS = 1e-6
LEVELS = 7
OCW = 256
NOC = D // OCW

F32 = mybir.dt.float32
F32R = mybir.dt.float32r
U32 = mybir.dt.uint32
ALU = mybir.AluOpType
ACT = mybir.ActivationFunctionType
X = mybir.AxisListType.X

PCOLS = {}
_o = 0
for _n, _w in (("mix_g", KD), ("conv_w", NC * CW), ("conv_b", NC), ("ln_g", NC), ("ln_b", NC),
               ("dconv_w", 3 * H * DCW), ("dn_g", 1), ("dt_bias", H), ("a_log", H)):
    PCOLS[_n] = (_o, _w)
    _o += _w
PW = _o

IDENT, ONES, TRI_P, TRI_S, BLK_S, LEV0 = range(6)
NCONST = LEV0 + LEVELS

KINDS = ("q", "k", "v", "gate", "glu")
QPAD = NP_TOK + DCW - 1 + NB * (NT + DCW - 1)
CPAD = NP_TOK + CW - 1 + NB * (NT + CW - 1)
QLEN = QPAD - (DCW - 1)
CLEN = CPAD - (CW - 1)
DT = 3
TD = DT * P
GT = TILES - DT
ET = 4
CHUNKS = NK // ET
UNIT = 8 * P
NU = 2 * ET + D // P // 2
RING = 2
STEPS = NU // (2 * RING)
GTOK = 48
SELW = (3 * DT + 2 * GT) * SLOTS
UW = 2 * UNIT
GB = 8


def build(nc, x_prompt, x_sample, consts, params, conv_prefix, dconv_prefix, state_in, w_ba, w_group, w_units,
          keys, ffn_g, final_g, peer_u, peer_v, u_units, v_units,
          y_prompt, y_sample, conv_new_p, dconv_new_p, state_new_p, conv_new_s, dconv_new_s, state_new_s):
    with ExitStack() as ctx:
        first = ctx.enter_context(ExitStack())

        def sb(name, shape, dt=F32):
            return first.enter_context(nc.sbuf_tensor(name, shape, dt))

        dram = {n: nc.dram_tensor(n, shape, F32, kind="Internal").ap() for n, shape in (
            ("xnT_spill", (P, KD, T)), ("cT_spill", (P, NC, T)), ("oT_spill", (P, H, T)), ("gates_T", (2 * KD + H, P, T)),
            ("mT_spill", (P, KD, T)), ("x1_spill", (P, TILES * D)), ("xg_spill", (P, GT, D)), ("xT_spill", (P, KD, T)),
            ("sel_spill", (P, SELW)), ("gates_dram", (NK, P, TD)))}
        xnT_spill, cT_spill, oT_spill, gates_T, mT_spill = (dram[n] for n in ("xnT_spill", "cT_spill", "oT_spill", "gates_T", "mT_spill"))
        x1_spill, xg_spill, xT_spill, sel_spill, gates_dram = (
            dram[n] for n in ("x1_spill", "xg_spill", "xT_spill", "sel_spill", "gates_dram"))
        first_sems = []

        def sem(name):
            first_sems.append(first.enter_context(nc.semaphore(name)))
            return first_sems[-1]

        cst = ctx.enter_context(nc.sbuf_tensor("cst", [P, NCONST, P], F32))
        par = ctx.enter_context(nc.sbuf_tensor("par", [P, PW], F32))
        ps = [ctx.enter_context(nc.psum_tensor(f"ps{i}", [P, 1024], F32)) for i in range(4)]

        XNT, CT, QT, KT, VT, WR, TM = 0, 10240, 15360, 20480, 25600, 30720, 40960
        END = 49152
        arena = sb("arena", [P, END])

        def at(off, *dims):
            n = 1
            for d in dims:
                n *= d
            v = arena[:, off:off + n]
            if len(dims) == 2:
                v = v.rearrange("p (a b) -> p a b", a=dims[0])
            elif len(dims) == 3:
                v = v.rearrange("p (a b c) -> p a b c", a=dims[0], b=dims[1])
            return v

        wba = sb("wba", [P, KD, 2 * H])
        dpre = sb("dpre", [P, 3 * H * NB, DCW - 1])
        dnew_p = sb("dnew_p", [P, 3 * H, DCW - 1])
        dnew_s = sb("dnew_s", [P, 3 * H * NB, DCW - 1])
        small = sb("small", [P, 136])
        epsc = sb("epsc", [P, 1])
        beta = sb("beta", [P, TILES, H])
        glog = sb("glog", [P, TILES, H])
        smalld = sb("smalld", [P, 256])

        ident = cst[:, IDENT, :]
        ones = cst[:, ONES, :]

        def pcol(name, i=0, n=1):
            o = PCOLS[name][0]
            return par[:, o + i:o + i + n]

        def ps8(i):
            return ps[i][:].rearrange("p (h c) -> p h c", h=8)

        xnT = at(XNT, KD, T)
        cT = at(CT, NC, T)
        qT = at(QT, H, T)
        kT = at(KT, H, T)
        vT = at(VT, H, T)
        xin = at(KT, TILES, D)

        ld_par, ld_x = sem("ld_par"), [sem(f"ld_x{t}") for t in range(TILES)]
        pace = {e: sem(f"pace_{e}") for e in ("sp", "act", "pe", "dve", "pool")}
        ready0 = sem("ready0")
        sumsq, msq, root, xscaled, xtr, xevac = (sem(n) for n in ("sumsq", "msq", "root", "xscaled", "xtr", "xevac"))
        ba_mm, ba_act, ba_dve = sem("ba_mm"), sem("ba_act"), sem("ba_dve")
        a_link, d_link, p_link = sem("a_link"), sem("d_link"), sem("p_link")

        def wreg(eng, name, s, v):
            eng.wait_ge(s, v)
            eng.sem_inc(pace[name], 1)

        class Link:

            def __init__(self, eng, name, s, base=0, loop=False):
                self.eng, self.name, self.s, self.base, self.n, self.loop = eng, name, s, base, 0, loop

            def __call__(self, ins):
                self.n += 1
                ins.then_inc(self.s, 1)
                if self.loop:
                    wreg(self.eng, self.name, self.s, self.base + self.n)
                else:
                    self.eng.wait_ge(self.s, self.base + self.n)

        mixer = ctx.enter_context(ExitStack())
        block = mixer.enter_context(nc.Block())

        pads = {"q": TM, "k": TM + QPAD, "v": TM + 2 * QPAD}
        CPB = TM + 3 * QPAD
        CACC = CPB + CPAD
        QACC = CACC + CPAD
        SIG = QACC + QPAD
        SQ = SIG + T
        RT = SQ + 2 * T
        assert RT + T <= END
        wring = {kd: at(WR + i * D, KD, P) for i, kd in enumerate(KINDS)}
        w_ld = {kd: sem(f"w_ld_{kd}") for kd in KINDS}
        mm = {kd: sem(f"mm_{kd}") for kd in KINDS}
        evac = {kd: sem(f"evac_{kd}") for kd in KINDS}
        conv_done = {kd: sem(f"conv_done_{kd}") for kd in "qkv"}
        silu_done = {kd: sem(f"silu_done_{kd}") for kd in "qkv"}
        stage_done = {kd: sem(f"stage_done_{kd}") for kd in "qkv"}
        prefix_done = {kd: sem(f"prefix_done_{kd}") for kd in "qkv"}
        prefix_done["c"], cstate_out = (ctx.enter_context(nc.semaphore(n)) for n in ("prefix_done_c", "cstate_out"))
        sq_done = {kd: sem(f"sq_done_{kd}") for kd in "qk"}
        mm_sum = {kd: sem(f"mm_sum_{kd}") for kd in "qk"}
        norm_root = {kd: sem(f"norm_root_{kd}") for kd in "qk"}
        norm_done = {kd: sem(f"norm_done_{kd}") for kd in "qk"}
        glu_done, cconv_done, cconv_out = sem("glu_done"), sem("cconv_done"), sem("cconv_out")
        dve_loop, dve_conv = sem("dve_loop"), sem("dve_conv")
        PSK = {"q": 0, "k": 1, "v": 2, "gate": 0, "glu": 1}

        def qpad(kd):
            return at(pads[kd], QPAD)

        def seg(buf, width, lead):
            return buf[:, NP_TOK + lead:NP_TOK + lead + NB * width].rearrange("p (b w) -> p b w", b=NB)

        ln_sum, ln_mean, ln_cent, ln_sq, ln_var, ln_root, ln_scaled, ln_out = (
            sem(n) for n in ("ln_sum", "ln_mean", "ln_cent", "ln_sq", "ln_var", "ln_root", "ln_scaled", "ln_out"))
        ln_sqmm = sem("ln_sqmm")
        LSQ = TM
        LMEAN = TM + 2 * T

        SLOT = [TM + 1024 * i for i in range(8)] + [WR + 8192, WR + 9216]
        kc, qc, vc, eb, qkd, atb, tb, ttb, xb, atl = (at(o, H, P) for o in SLOT)
        st_p = at(WR, H, P)
        st_s = at(WR, H, NB, P)
        st_s_dst = at(WR, 8192)
        dd = {n: sem(f"dd_{n}") for n in (
            "copied", "gsum", "gexp_in", "gexp", "trig", "rows", "ediff", "eexp", "kk", "qk", "at", "atl", "x", "xc",
            "tx", "t", "tt", "ktr", "kd", "ks", "r2", "dl", "dlc", "o2", "sup", "snew", "oroot", "oscaled",
            "otr", "out", "vtr", "vb", "ksT", "ksc", "oss", "dm", "grow", "init")}
        dd_link_d = sem("dd_link_d")
        st_ld, st_out = (ld_x[4], 16), sem("st_out")

        spilled = sem("spilled")
        out_done = sem("out_done")

        def count_s(per, k):
            prompt = {2 * 4: 2 * LEVELS, 2 * 4 - 2: 2 * LEVELS - 2, 2 * 4 + 1: 2 * LEVELS + 1, 4 * 4 - 2: 4 * LEVELS - 2}.get(per, per)
            return PT * prompt + k

        @block.sync
        def _(sp):
            for t in range(TILES):
                src = x_prompt[t * P:(t + 1) * P, :] if t < PT else x_sample
                sp.dma_start(xin[:, t, :], src).then_inc(ld_x[t], 16)
                if t == 0:
                    sp.dma_start(cst[:], consts).then_inc(ld_par, 16)
                    sp.dma_start(par[:], params).then_inc(ld_par, 16)
                    sp.dma_start(wba[:], w_ba).then_inc(ld_par, 16)
            sp.dma_start(dpre[:], dconv_prefix).then_inc(ld_par, 16)
            sp.wait_ge(xevac, 2 * TILES)
            sp.dma_start(xnT_spill, xnT).then_inc(spilled, 16)
            for kd in KINDS:
                sp.dma_start(wring[kd].rearrange("p k c -> p (k c)"), w_group[KINDS.index(kd)]).then_inc(w_ld[kd], 16)
            with sp.Fori(0, NC - 1) as c:
                for i, kd in enumerate(KINDS):
                    wreg(sp, "sp", mm[kd], c + 1)
                    sp.dma_start(wring[kd].rearrange("p k c -> p (k c)"),
                                 w_group[bass.ds((c + 1) * 5 + i, 1)].rearrange("a p n -> p (a n)")).then_inc(w_ld[kd], 16)
            sp.wait_ge(dd["snew"], PT * 2)
            sp.dma_start(state_new_p, at(WR, H * P)).then_inc(st_out, 16)
            sp.wait_ge(st_out, 16)
            sp.dma_start(st_s_dst, state_in).then_inc(st_ld[0], 16)
            sp.wait_ge(dd["snew"], PT * 2 + 2 * H)
            sp.dma_start(state_new_s, st_s_dst).then_inc(st_out, 16)
            sp.wait_ge(st_out, 32)
            sp.wait_ge(stage_done["v"], NC + 1)
            sp.wait_ge(stage_done["q"], NC + 1)
            sp.wait_ge(stage_done["k"], NC + 1)
            sp.dma_start(dconv_new_p, dnew_p[:]).then_inc(out_done, 16)
            sp.dma_start(dconv_new_s, dnew_s[:]).then_inc(out_done, 16)
            sp.wait_ge(ln_out, NC)
            sp.dma_start(cT_spill, cT).then_inc(spilled, 16)
            sp.wait_ge(dd["out"], TILES)
            sp.dma_start(oT_spill, qT).then_inc(spilled, 16)
            sp.wait_ge(spilled, 48)
            sp.wait_ge(out_done, 32)
            sp.wait_ge(cstate_out, 32 * NC)

        @block.tensor
        def _(pe):
            pe.wait_ge(ld_par, 48)
            for t in range(TILES):
                pe.wait_ge(xscaled, t + 1)
                for half in range(2):
                    n = 2 * t + half
                    if n >= 4:
                        pe.wait_ge(xevac, n - 3)
                    for k in range(8):
                        kk = half * 8 + k
                        m = pe.transpose(ps[n % 4][:, k * P:(k + 1) * P], xin[:, t, kk * P:(kk + 1) * P], ident)
                    m.then_inc(xtr, 1)
            pe.wait_ge(xevac, 2 * TILES)
            for t in range(TILES):
                for k in range(KD):
                    m = pe.matmul(ps[3][:, t * 2 * H:(t + 1) * 2 * H], xnT[:, k, t * P:(t + 1) * P], wba[:, k, :],
                                  start=k == 0, stop=k == KD - 1)
            m.then_inc(ba_mm, 1)

            def project(out, w, src, n=KD):
                for k in range(n):
                    pe.matmul(out[:, 0:NP_TOK], w[:, k, :], src[:, k, 0:NP_TOK], start=k == 0, stop=k == n - 1)
                    m = pe.matmul(out[:, NP_TOK:T], w[:, k, :], src[:, k, NP_TOK:T], start=k == 0, stop=k == n - 1)
                return m

            def sum_rows(out, src, start=True, stop=True):
                pe.matmul(out[:, 0:NP_TOK], ones, src[:, 0:NP_TOK], start=start, stop=stop)
                return pe.matmul(out[:, NP_TOK:T], ones, src[:, NP_TOK:T], start=start, stop=stop)

            pe.wait_ge(ba_act, 1)
            pe.wait_ge(ba_dve, 1)
            with pe.Fori(0, NC) as c:
                for kd in KINDS:
                    pe.wait_ge(w_ld[kd], c * 16 + 16)
                    if kd == "q":
                        pe.wait_ge(glu_done, c + 1)
                    elif kd == "k":
                        pe.wait_ge(glu_done, c + 1)
                    elif kd == "v":
                        pe.wait_ge(norm_root["k"], c + 1)
                    elif kd == "gate":
                        pe.wait_ge(evac["q"], c + 1)
                    else:
                        pe.wait_ge(evac["k"], c + 1)
                    project(ps[PSK[kd]], wring[kd], xnT).then_inc(mm[kd], 1)
                pe.wait_ge(sq_done["q"], c + 1)
                pe.wait_ge(norm_root["q"], c + 1)
                sum_rows(ps[3], at(SQ, T)).then_inc(mm_sum["q"], 1)
                pe.wait_ge(sq_done["k"], c + 1)
                pe.wait_ge(evac["v"], c + 1)
                sum_rows(ps[2], at(SQ + T, T)).then_inc(mm_sum["k"], 1)

            pe.wait_ge(cconv_out, NC)
            pe.wait_ge(evac["q"], NC + 0)
            pe.wait_ge(glu_done, NC + 1)
            for c in range(NC):
                m = sum_rows(ps[0], cT[:, c, :], start=c == 0, stop=c == NC - 1)
            m.then_inc(ln_sum, 1)
            for c in range(NC):
                pe.wait_ge(ln_sq, c + 1)
                sum_rows(ps[1], at(LSQ + (c % 2) * T, T), start=c == 0, stop=c == NC - 1).then_inc(ln_sqmm, 1)

            def delta(t, streams, w, tot):
                tri = cst[:, TRI_S if streams else TRI_P, :]
                blk = cst[:, BLK_S, :] if streams else ones
                lev = 4 if streams else LEVELS
                w(dd["copied"], tot(1, 1))
                w(dd["init"], tot(1, 1))
                gcur = smalld[:, 0:H]
                pe.matmul(ps[3][:, 0:H], tri, gcur, start=True, stop=True)
                pe.matmul(ps[3][:, H:2 * H], blk, gcur, start=True, stop=True).then_inc(dd["gsum"], 1)
                w(dd["trig"], tot(2, 1))
                for g in range(2):
                    pe.matmul(ps[0][:, g * 512:(g + 1) * 512], ones, at(SLOT[3] + g * 512, 512), start=True, stop=True).then_inc(dd["rows"], 1)
                w(dd["trig"], tot(2, 2))
                for g in range(2):
                    pe.matmul(ps[1][:, g * 512:(g + 1) * 512], ones, at(SLOT[8] + g * 512, 512), start=True, stop=True).then_inc(dd["rows"], 1)
                for h in range(H):
                    m = pe.matmul(ps[2][:, h * P:(h + 1) * P], kc[:, h, :], kc[:, h, :], start=True, stop=True)
                m.then_inc(dd["kk"], 1)
                w(dd["gexp_in"], tot(1, 1))
                for h in range(H):
                    m = pe.matmul(ps[3][:, h * P:(h + 1) * P], kc[:, h, :], qc[:, h, :], start=True, stop=True)
                m.then_inc(dd["qk"], 1)
                w(dd["ediff"], tot(1, 1))
                for h in range(H):
                    m = pe.transpose(ps[0][:, h * P:(h + 1) * P], vc[:, h, :], ident)
                m.then_inc(dd["vtr"], 1)
                for l in range(lev):
                    for g in range(2):
                        w(dd["atl"], tot(2 * lev, 2 * l + g + 1))
                        if l:
                            w(dd["t"], tot(2 * lev - 2, 2 * l - 1 + g))
                        else:
                            w(dd["at"], tot(2, 2))
                        for h in range(4 * g, 4 * g + 4):
                            m = pe.matmul(ps[1][:, h * P:(h + 1) * P], atl[:, h, :], tb[:, h, :], start=True, stop=True)
                        m.then_inc(dd["x"], 1)
                    for g in range(2):
                        w(dd["xc"], tot(2 * lev, 2 * l + g + 1))
                        w(dd["tt"], tot(2 * lev + 1, 2 * l + g if l else 1))
                        if l < lev - 1:
                            for h in range(4 * g, 4 * g + 4):
                                m = pe.matmul(ps[2][:, h * P:(h + 1) * P], ttb[:, h, :], xb[:, h, :], start=True, stop=True)
                            m.then_inc(dd["tx"], 1)
                        for h in range(4 * g, 4 * g + 4):
                            m = pe.matmul(ps[3][:, h * P:(h + 1) * P], xb[:, h, :], ttb[:, h, :], start=True, stop=True)
                        m.then_inc(dd["tx"], 1)
                w(dd["vb"], tot(1, 1))
                for h in range(H):
                    m = pe.transpose(ps[0][:, h * P:(h + 1) * P], kc[:, h, :], ident)
                m.then_inc(dd["ktr"], 1)
                w(dd["tt"], tot(2 * lev + 1, 2 * lev + 1))
                if not streams:
                    for h in range(H):
                        m = pe.matmul(ps[1][:, h * P:(h + 1) * P], kc[:, h, :], st_p[:, h, :], start=True, stop=True)
                    m.then_inc(dd["ks"], 1)
                    for h in range(H):
                        m = pe.matmul(ps[2][:, h * P:(h + 1) * P], qc[:, h, :], st_p[:, h, :], start=True, stop=True)
                    m.then_inc(dd["ks"], 1)
                else:
                    pe.wait_ge(st_ld[0], st_ld[1] + 16)
                    for j, src in enumerate((kc, qc)):
                        for h in range(H):
                            for b in range(NB):
                                m = pe.matmul(ps[1 + j][:, h * P + b * NT:h * P + (b + 1) * NT], st_s[:, h, b, :],
                                              src[:, h, b * NT:(b + 1) * NT], start=True, stop=True)
                        m.then_inc(dd["ksT"], 1)
                    for j in range(2):
                        pe.wait_ge(dd["ksc"], j + 1)
                        for h in range(H):
                            m = pe.transpose(ps[1 + j][:, h * P:(h + 1) * P], (eb if j == 0 else tb)[:, h, :], ident)
                        m.then_inc(dd["ks"], 1)
                w(dd["r2"], tot(1, 1))
                for h in range(H):
                    m = pe.matmul(ps[3][:, h * P:(h + 1) * P], ttb[:, h, :], vc[:, h, :], start=True, stop=True)
                m.then_inc(dd["dl"], 1)
                w(dd["dlc"], tot(1, 1))
                for h in range(H):
                    m = pe.matmul(ps[1][:, h * P:(h + 1) * P], qkd[:, h, :], atl[:, h, :], start=True, stop=True)
                m.then_inc(dd["o2"], 1)
                w(dd["kd"], tot(1, 1))
                if not streams:
                    for h in range(H):
                        m = pe.matmul(ps[3][:, h * P:(h + 1) * P], atb[:, h, :], atl[:, h, :], start=True, stop=True)
                    m.then_inc(dd["sup"], 1)
                else:
                    for h in range(H):
                        pe.wait_ge(dd["dm"], h + 1)
                        if h:
                            pe.wait_ge(dd["snew"], PT * 2 + 2 * h)
                        for g in range(2):
                            pe.matmul(ps[3][:, g * 512:(g + 1) * 512], atb[:, h, :],
                                      at(SLOT[3 if h % 2 else 6] + g * 512, 512), start=True, stop=True).then_inc(dd["sup"], 1)
                w(dd["oscaled"], tot(1, 1))
                for h in range(H):
                    m = pe.transpose(ps[0][:, h * P:(h + 1) * P], xb[:, h, :], ident)
                m.then_inc(dd["otr"], 1)

            pe.wait_ge(ln_root, 1)
            pe.wait_ge(ln_mean, 1)
            with pe.Fori(0, PT) as t:
                delta(t, False, lambda s, v: wreg(pe, "pe", s, v), lambda per, k: t * per + k)
            delta(PT, True, lambda s, v: pe.wait_ge(s, v), lambda per, k: count_s(per, k))

        @block.scalar
        def _(act):
            link = Link(act, "act", a_link)
            act.wait_ge(ready0, 1)
            for t in range(TILES):
                act.wait_ge(ld_x[t], 16)
                link(act.activation(at(CT, D), xin[:, t, :], ACT.Square, accum_out=small[:, t:t + 1]))
                act.sem_inc(sumsq, 1)
            act.wait_ge(msq, 1)
            act.activation(small[:, 16:16 + TILES], small[:, 8:8 + TILES], ACT.Sqrt).then_inc(root, 1)
            act.wait_ge(ba_mm, 1)
            ba = ps[3][:, 0:TILES * 2 * H].rearrange("p (t c) -> p t c", t=TILES)
            act.wait_ge(ba_dve, 1)
            link(act.activation(beta[:], ba[:, :, 0:H], ACT.Sigmoid))
            t1 = small[:, 72:112]
            link(act.activation(t1, small[:, 32:72], ACT.Abs))
            link(act.activation(t1, t1, ACT.Exp, scale=-1.0))
            link(act.activation(t1, t1, ACT.Ln, bias=1.0))
            link(act.activation(small[:, 112:120], pcol("a_log", 0, H), ACT.Exp))
            act.sem_inc(ba_act, 1)

            act.sem_inc(silu_done["v"], 1)
            act.sem_inc(norm_root["q"], 1)
            act.sem_inc(norm_root["k"], 1)
            with act.Fori(0, NC) as c:
                for i, kd in enumerate("qkv"):
                    wreg(act, "act", mm[kd], c + 1)
                    wreg(act, "act", conv_done[kd], c + 1)
                    wreg(act, "act", stage_done[kd], c + 1)
                    src = ps[PSK[kd]]
                    act.activation(qpad(kd)[:, DCW - 1:DCW - 1 + NP_TOK], src[:, 0:NP_TOK], ACT.Copy)
                    act.activation(seg(qpad(kd), NT + DCW - 1, DCW - 1)[:, :, DCW - 1:],
                                   src[:, NP_TOK:T].rearrange("p (b w) -> p b w", b=NB), ACT.Copy).then_inc(evac[kd], 1)
                    dst = {"q": QT, "k": KT, "v": VT}[kd]
                    full = at(dst, H, T)[:, bass.ds(c, 1), :].rearrange("p a n -> p (a n)")
                    wreg(act, "act", conv_done[kd], c + 2)
                    cv = at(QACC, QPAD)
                    act.activation(full[:, 0:NP_TOK], cv[:, 0:NP_TOK], ACT.Silu)
                    act.activation(full[:, NP_TOK:T].rearrange("p (b w) -> p b w", b=NB),
                                   seg(cv, NT + DCW - 1, DCW - 1)[:, :, 0:NT], ACT.Silu).then_inc(silu_done[kd], 1)
                    if kd != "v":
                        wreg(act, "act", silu_done[kd], c + 1)
                        act.activation(at(SQ + i * T, T), full, ACT.Square).then_inc(sq_done[kd], 1)
                wreg(act, "act", mm["gate"], c + 1)
                wreg(act, "act", glu_done, c + 1)
                act.activation(at(SIG, T), ps[0][:, 0:T], ACT.Sigmoid).then_inc(evac["gate"], 1)
                for i, kd in enumerate("qk"):
                    wreg(act, "act", mm_sum[kd], c + 1)
                    wreg(act, "act", norm_done["q" if kd == "k" else "k"], c + (2 if kd == "k" else 1))
                    act.activation(at(RT, T), ps[3 if kd == "q" else 2][:, 0:T], ACT.Sqrt, bias=epsc[:, 0:1]).then_inc(norm_root[kd], 1)

            for kd in "qkv":
                act.wait_ge(stage_done[kd], NC + 1)
            act.wait_ge(ln_sum, 1)
            act.wait_ge(norm_done["k"], NC + 1)
            act.activation(at(LMEAN, T), ps[0][:, 0:T], ACT.Copy, scale=1.0 / CONV).then_inc(ln_mean, 1)
            act.wait_ge(ln_cent, 1)
            for c in range(NC):
                if c >= 2:
                    act.wait_ge(ln_sqmm, c - 1)
                act.activation(at(LSQ + (c % 2) * T, T), cT[:, c, :], ACT.Square).then_inc(ln_sq, 1)
            act.wait_ge(ln_sqmm, NC)
            act.activation(at(LMEAN, T), ps[1][:, 0:T], ACT.Sqrt, bias=epsc[:, 0:1], scale=1.0 / CONV).then_inc(ln_root, 1)
            act.wait_ge(ln_scaled, 1)
            for c in range(NC):
                act.activation(cT[:, c, :], cT[:, c, :], ACT.Silu, bias=pcol("ln_b", c), scale=pcol("ln_g", c)).then_inc(ln_out, 1)

            def delta(t, streams, w, tot, tile):
                lev = 4 if streams else LEVELS
                last_r = ps8(0)
                for dst, src in ((kc, kT), (qc, qT), (vc, vT)):
                    m = act.activation(dst, src[:, :, tile], ACT.Copy)
                m.then_inc(dd["copied"], 1)
                w(dd["gexp_in"], tot(1, 1))
                act.activation(smalld[:, 32:48], smalld[:, 16:32], ACT.Exp).then_inc(dd["gexp"], 1)
                w(dd["rows"], tot(4, 2))
                if streams:
                    act.activation(smalld[:, 64:128].rearrange("p (h b) -> p h b", h=H),
                                   last_r[:, :, NT - 1::NT], ACT.Exp).then_inc(dd["grow"], 1)
                else:
                    act.activation(smalld[:, 64:72], last_r[:, :, P - 1:P].rearrange("p h a -> p (h a)"), ACT.Exp).then_inc(dd["grow"], 1)
                w(dd["ediff"], tot(1, 1))
                act.activation(eb, eb, ACT.Exp).then_inc(dd["eexp"], 1)
                for l in range(lev):
                    for g in range(2):
                        w(dd["x"], tot(2 * lev, 2 * l + g + 1))
                        if l:
                            w(dd["tx"], tot(4 * lev - 2, 4 * l))
                        else:
                            w(dd["at"], tot(2, 2))
                        act.activation(xb[:, 4 * g:4 * g + 4, :], ps8(1)[:, 4 * g:4 * g + 4, :], ACT.Copy).then_inc(dd["xc"], 1)
                if streams:
                    for j in range(2):
                        act.wait_ge(dd["ksT"], j + 1)
                        act.activation(eb if j == 0 else tb, ps8(1 + j), ACT.Copy).then_inc(dd["ksc"], 1)
                w(dd["dl"], tot(1, 1))
                act.activation(atl, ps8(3), ACT.Copy).then_inc(dd["dlc"], 1)
                w(dd["oss"], tot(1, 1))
                act.activation(smalld[:, 144:152], smalld[:, 136:144], ACT.Sqrt).then_inc(dd["oroot"], 1)
                w(dd["otr"], tot(1, 1))
                act.activation(qT[:, :, tile], ps8(0), ACT.Copy).then_inc(dd["out"], 1)

            act.wait_ge(ln_out, NC)
            act.wait_ge(ready0, 2)
            act.wait_ge(cstate_out, 32 * NC)
            with act.Fori(0, PT) as t:
                delta(t, False, lambda s, v: wreg(act, "act", s, v), lambda per, k: t * per + k, bass.ds(t * P, P))
            delta(PT, True, lambda s, v: act.wait_ge(s, v), lambda per, k: count_s(per, k), slice(PT * P, T))

        @block.vector
        def _(v):
            v.memset(epsc[:], EPS)
            v.memset(at(pads["q"], DCW - 1), 0.0)
            v.memset(at(pads["k"], DCW - 1), 0.0)
            v.memset(at(pads["v"], DCW - 1), 0.0)
            v.memset(smalld[:], 0.0)
            v.memset(small[:], 0.0).then_inc(ready0, 1)
            link = Link(v, "dve", d_link)
            v.wait_ge(sumsq, TILES)
            link(v.tensor_scalar(small[:, 8:8 + TILES], small[:, 0:TILES], 1.0 / D, EPS, ALU.mult, ALU.add))
            v.sem_inc(msq, 1)
            v.wait_ge(root, 1)
            link(v.reciprocal(small[:, 24:24 + TILES], small[:, 16:16 + TILES]))
            v.wait_ge(ld_par, 64)
            mixg = pcol("mix_g", 0, KD)

            def evac_x(n):
                t, half = n // 2, n % 2
                v.wait_ge(xtr, n + 1)
                v.tensor_tensor(xnT[:, 8 * half:8 * half + 8, t * P:(t + 1) * P], ps8(n % 4),
                                mixg[:, 8 * half:8 * half + 8].unsqueeze(2).to_broadcast([P, 8, P]), ALU.mult).then_inc(xevac, 1)
            for t in range(TILES):
                v.tensor_scalar(xin[:, t, :], xin[:, t, :], small[:, 24 + t:25 + t], None, ALU.mult).then_inc(xscaled, 1)
                if t:
                    evac_x(2 * t - 2)
                    evac_x(2 * t - 1)
            evac_x(2 * TILES - 2)
            evac_x(2 * TILES - 1)
            v.wait_ge(ba_mm, 1)
            ba = ps[3][:, 0:TILES * 2 * H].rearrange("p (t c) -> p t c", t=TILES)
            ax = small[:, 32:72].rearrange("p (t h) -> p t h", t=TILES)
            link(v.tensor_tensor(ax, ba[:, :, H:2 * H], pcol("dt_bias", 0, H).unsqueeze(1).to_broadcast([P, TILES, H]), ALU.add))
            v.sem_inc(ba_dve, 1)
            v.wait_ge(ba_act, 1)
            link(v.scalar_tensor_tensor(ax, ax, 0.0, small[:, 72:112].rearrange("p (t h) -> p t h", t=TILES), ALU.max, ALU.add))
            link(v.scalar_tensor_tensor(glog[:], ax, -1.0, small[:, 112:120].unsqueeze(1).to_broadcast([P, TILES, H]), ALU.mult, ALU.mult))
            v.memset(at(CPB, CW - 1), 0.0)
            for s in (*conv_done.values(), glu_done, cconv_done):
                v.sem_inc(s, 1)
            for s in norm_done.values():
                v.sem_inc(s, 1)

            NTAP = DCW * 3 + CW
            with v.Fori(0, NC) as c:
                n = [0]

                def step(ins):
                    n[0] += 1
                    ins.then_inc(dve_loop, 1)
                    wreg(v, "dve", dve_loop, c * NL + n[0])
                NL = 3 * (DCW - 1) + 2 + CW - 1
                for i, kd in enumerate("qkv"):
                    wreg(v, "dve", evac[kd], c + 1)
                    wreg(v, "dve", prefix_done[kd], c + 1)
                    wreg(v, "dve", silu_done["qkv"[i - 1]], c + 1)
                    pad, dst = at(pads[kd], QPAD), at(QACC, QLEN)
                    for j in range(DCW):
                        wc = par[:, bass.ds(c * DCW + (PCOLS["dconv_w"][0] + i * H * DCW + j), 1)]
                        if j == 0:
                            step(v.tensor_scalar(dst, pad[:, j:j + QLEN], wc, None, ALU.mult))
                        else:
                            ins = v.scalar_tensor_tensor(dst, pad[:, j:j + QLEN], wc, dst, ALU.mult, ALU.add)
                            if j < DCW - 1:
                                step(ins)
                            else:
                                ins.then_inc(conv_done[kd], 1)
                wreg(v, "dve", mm["glu"], c + 1)
                wreg(v, "dve", evac["gate"], c + 1)
                wreg(v, "dve", prefix_done["c"], c * 16 + 16)
                cp, sg = at(CPB, CPAD), at(SIG, T)
                v.tensor_tensor(cp[:, CW - 1:CW - 1 + NP_TOK], ps[1][:, 0:NP_TOK], sg[:, 0:NP_TOK], ALU.mult)
                v.tensor_tensor(seg(cp, NT + CW - 1, CW - 1)[:, :, CW - 1:], ps[1][:, NP_TOK:T].rearrange("p (b w) -> p b w", b=NB),
                                sg[:, NP_TOK:T].rearrange("p (b w) -> p b w", b=NB), ALU.mult).then_inc(glu_done, 1)
                for i, kd in enumerate("qk"):
                    wreg(v, "dve", norm_root[kd], c + 2)
                    full = at(QT if kd == "q" else KT, H, T)[:, bass.ds(c, 1), :].rearrange("p a n -> p (a n)")
                    step(v.reciprocal(at(RT, T), at(RT, T)))
                    v.scalar_tensor_tensor(full, full, float(P) ** -0.5 if kd == "q" else 1.0, at(RT, T), ALU.mult, ALU.mult).then_inc(norm_done[kd], 1)
                wreg(v, "dve", glu_done, c + 2)
                dst = at(CACC, CLEN)
                for j in range(CW):
                    wc = par[:, bass.ds(c * CW + (PCOLS["conv_w"][0] + j), 1)]
                    if j == 0:
                        step(v.tensor_scalar(dst, cp[:, j:j + CLEN], wc, par[:, bass.ds(c + PCOLS["conv_b"][0], 1)], ALU.mult, ALU.add))
                    elif j < CW - 1:
                        step(v.scalar_tensor_tensor(dst, cp[:, j:j + CLEN], wc, dst, ALU.mult, ALU.add))
                    else:
                        fullc = cT[:, bass.ds(c, 1), :].rearrange("p a n -> p (a n)")
                        v.scalar_tensor_tensor(fullc[:, 0:NP_TOK], cp[:, j:j + NP_TOK], wc, dst[:, 0:NP_TOK], ALU.mult, ALU.add)
                        v.scalar_tensor_tensor(fullc[:, NP_TOK:T].rearrange("p (b w) -> p b w", b=NB),
                                               seg(cp, NT + CW - 1, CW - 1)[:, :, CW - 1:], wc,
                                               seg(at(CACC, CPAD), NT + CW - 1, CW - 1)[:, :, 0:NT], ALU.mult, ALU.add).then_inc(cconv_out, 1)
                assert n[0] == NL, (n[0], NL)
                wreg(v, "dve", cconv_out, c + 1)
                v.sem_inc(cconv_done, 1)

            v.wait_ge(ln_mean, 1)
            mean = at(LMEAN, T).unsqueeze(1).to_broadcast([P, NC, T])
            v.tensor_tensor(cT, cT, mean, ALU.subtract).then_inc(ln_cent, 1)
            v.wait_ge(ln_root, 1)
            link(v.reciprocal(at(LMEAN, T), at(LMEAN, T)))
            v.tensor_tensor(cT, cT, mean, ALU.mult).then_inc(ln_scaled, 1)

            def bc(col):
                return col.unsqueeze(2).to_broadcast([P, H, P])

            def bm(mat, n=H):
                return mat.unsqueeze(1).to_broadcast([P, n, P])

            def delta(t, streams, w, tot, gsrc, bsrc, lk):
                tri = cst[:, TRI_S if streams else TRI_P, :]
                lev = 4 if streams else LEVELS
                gcur, bcur = smalld[:, 0:H], smalld[:, 8:8 + H]
                lk(v.tensor_copy(gcur, gsrc))
                lk(v.tensor_copy(bcur, bsrc))
                v.sem_inc(dd["init"], 1)
                w(dd["copied"], tot(1, 1))
                v.tensor_tensor(eb, bm(tri), bc(gcur), ALU.mult).then_inc(dd["trig"], 1)
                v.tensor_tensor(xb, bm(ident), bc(bcur), ALU.mult).then_inc(dd["trig"], 1)
                w(dd["gsum"], tot(1, 1))
                G, toend = smalld[:, 16:24], smalld[:, 24:32]
                lk(v.tensor_copy(smalld[:, 48:64], ps[3][:, 0:16]))
                lk(v.tensor_copy(G, smalld[:, 48:56]))
                lk(v.tensor_tensor(toend, smalld[:, 56:64], smalld[:, 48:56], ALU.subtract))
                v.sem_inc(dd["gexp_in"], 1)
                w(dd["rows"], tot(4, 4))
                w(dd["grow"], tot(1, 1))
                lk(v.tensor_tensor(eb, ps8(0), bc(smalld[:, 48:56]), ALU.subtract))
                v.tensor_scalar(eb, eb, 0.0, None, ALU.min).then_inc(dd["ediff"], 1)
                w(dd["eexp"], tot(1, 1))
                lk(v.tensor_tensor(eb, eb, bm(tri), ALU.mult))
                w(dd["kk"], tot(1, 1))
                lk(v.tensor_tensor(atb, eb, ps8(2), ALU.mult))
                v.tensor_tensor(atb, atb, ps8(1), ALU.mult).then_inc(dd["at"], 1)
                w(dd["qk"], tot(1, 1))
                v.tensor_tensor(qkd, eb, ps8(3), ALU.mult).then_inc(dd["at"], 1)
                lk(v.tensor_copy(tb, bm(ident)))
                v.tensor_copy(ttb, bm(ident)).then_inc(dd["tt"], 1)
                w(dd["at"], tot(2, 2))
                w(dd["gexp"], tot(1, 1))
                w(dd["vtr"], tot(1, 1))
                v.tensor_tensor(vc, ps8(0), bc(bcur), ALU.mult).then_inc(dd["vb"], 1)
                lk(v.tensor_tensor(smalld[:, 128:136], bcur, smalld[:, 32:40], ALU.mult))
                for g in range(2):
                    hs = slice(4 * g, 4 * g + 4)
                    v.tensor_tensor(atl[:, hs, :], atb[:, hs, :], bm(cst[:, LEV0, :], 4), ALU.mult).then_inc(dd["atl"], 1)
                for l in range(lev):
                    for g in range(2):
                        hs = slice(4 * g, 4 * g + 4)
                        if l < lev - 1:
                            w(dd["x"], tot(2 * lev, 2 * l + g + 1))
                            v.tensor_tensor(atl[:, hs, :], atb[:, hs, :], bm(cst[:, LEV0 + l + 1, :], 4), ALU.mult).then_inc(dd["atl"], 1)
                    if l == 0:
                        w(dd["tt"], tot(2 * lev + 1, 1))
                    for g in range(2):
                        hs = slice(4 * g, 4 * g + 4)
                        if l < lev - 1:
                            w(dd["tx"], tot(4 * lev - 2, 4 * l + 2 * g + 1))
                            if l:
                                w(dd["t"], tot(2 * lev - 2, 2 * l - 1 + g))
                            v.tensor_tensor(tb[:, hs, :], tb[:, hs, :], ps8(2)[:, hs, :], ALU.subtract).then_inc(dd["t"], 1)
                            w(dd["tx"], tot(4 * lev - 2, 4 * l + 2 * g + 2))
                        else:
                            w(dd["tx"], tot(4 * lev - 2, 4 * l + g + 1))
                        if l:
                            w(dd["tt"], tot(2 * lev + 1, 2 * l + g))
                        v.tensor_tensor(ttb[:, hs, :], ttb[:, hs, :], ps8(3)[:, hs, :], ALU.subtract).then_inc(dd["tt"], 1)
                w(dd["ktr"], tot(1, 1))
                v.tensor_tensor(atb, ps8(0), bc(smalld[:, 40:48]), ALU.mult).then_inc(dd["kd"], 1)
                w(dd["ks"], tot(2, 1))
                w(dd["vb"], tot(1, 1))
                w(dd["tt"], tot(2 * lev + 1, 2 * lev + 1))
                if streams:
                    w(dd["ks"], tot(2, 2))
                lk(v.tensor_tensor(tb, ps8(1), bc(smalld[:, 128:136]), ALU.mult))
                v.tensor_tensor(vc, vc, tb, ALU.subtract).then_inc(dd["r2"], 1)
                w(dd["ks"], tot(2, 2))
                lk(v.tensor_tensor(xb, ps8(2), bc(smalld[:, 32:40]), ALU.mult))
                w(dd["o2"], tot(1, 1))
                lk(v.tensor_tensor(xb, xb, ps8(1), ALU.add))
                w(dd["r2"], tot(1, 1))
                lk(v.tensor_tensor(eb, xb, xb, ALU.mult))
                lk(v.tensor_reduce(smalld[:, 152:160], eb, X, ALU.add))
                lk(v.tensor_scalar(smalld[:, 136:144], smalld[:, 152:160], 1.0 / P, EPS, ALU.mult, ALU.add))
                v.sem_inc(dd["oss"], 1)
                w(dd["oroot"], tot(1, 1))
                lk(v.reciprocal(smalld[:, 160:168], smalld[:, 144:152]))
                v.tensor_tensor(xb, xb, bc(smalld[:, 160:168]), ALU.mult).then_inc(dd["oscaled"], 1)
                if not streams:
                    w(dd["sup"], tot(1, 1))
                    lk(v.tensor_tensor(st_p, st_p, bc(smalld[:, 64:72]), ALU.mult))
                    v.tensor_tensor(st_p, st_p, ps8(3), ALU.add).then_inc(dd["snew"], 2)
                    w(dd["snew"], tot(2, 2))
                else:
                    bmask = cst[:, BLK_S, :]
                    w(dd["dlc"], tot(1, 1))
                    w(dd["oscaled"], tot(1, 1))
                    for h in range(H):
                        dmb = at(SLOT[3 if h % 2 else 6], NB, P)
                        if h >= 2:
                            v.wait_ge(dd["sup"], PT + 2 * (h - 1))
                        v.tensor_tensor(dmb, atl[:, h, :].unsqueeze(1).to_broadcast([P, NB, P]),
                                        bmask[:, NT - 1::NT].unsqueeze(2).to_broadcast([P, NB, P]), ALU.mult).then_inc(dd["dm"], 1)
                        glb = smalld[:, 64 + NB * h:64 + NB * h + NB].unsqueeze(2).to_broadcast([P, NB, P])
                        lk(v.tensor_tensor(st_s[:, h, :, :], st_s[:, h, :, :], glb, ALU.mult))
                        v.wait_ge(dd["sup"], PT + 2 * h + 2)
                        v.tensor_tensor(st_s[:, h, :, :], st_s[:, h, :, :], ps8(3), ALU.add).then_inc(dd["snew"], 2)

            v.wait_ge(ln_out, NC)
            link(v.memset(st_p, 0.0))
            v.sem_inc(ready0, 1)
            with v.Fori(0, PT) as t:
                NLK = 18
                lk = Link(v, "dve", dd_link_d, base=t * NLK, loop=True)
                delta(t, False, lambda s, val: wreg(v, "dve", s, val), lambda per, k: t * per + k,
                      glog[:, bass.ds(t, 1), :].rearrange("p a h -> p (a h)"), beta[:, bass.ds(t, 1), :].rearrange("p a h -> p (a h)"), lk)
                assert lk.n == NLK, lk.n
            delta(PT, True, lambda s, val: v.wait_ge(s, val), lambda per, k: count_s(per, k), glog[:, PT, :], beta[:, PT, :],
                  Link(v, "dve", dd_link_d, base=PT * NLK))

        @block.gpsimd
        def _(pool):
            pool.wait_ge(ld_par, 64)
            for s in stage_done.values():
                pool.sem_inc(s, 1)
            pool.wait_ge(cconv_done, 1)
            with pool.Fori(0, NC) as c:
                for i, kd in enumerate("qkv"):
                    wreg(pool, "pool", conv_done[kd], c + 1)
                    sg = seg(qpad(kd), NT + DCW - 1, DCW - 1)
                    pool.tensor_copy(sg[:, :, 0:DCW - 1], dpre[:, bass.ds(c * NB + i * H * NB, NB), :]).then_inc(prefix_done[kd], 1)
                for i, kd in enumerate("qkv"):
                    wreg(pool, "pool", evac[kd], c + 1)
                    pool.tensor_copy(dnew_p[:, bass.ds(c + i * H, 1), :].rearrange("p a n -> p (a n)"), qpad(kd)[:, NP_TOK:NP_TOK + DCW - 1])
                    pool.tensor_copy(dnew_s[:, bass.ds(c * NB + i * H * NB, NB), :],
                                     seg(qpad(kd), NT + DCW - 1, DCW - 1)[:, :, NT:]).then_inc(stage_done[kd], 1)
                wreg(pool, "pool", cconv_done, c + 1)
                cp = at(CPB, CPAD)
                sg = seg(cp, NT + CW - 1, CW - 1)
                pool.dma_start(sg[:, :, 0:CW - 1], conv_prefix[bass.ds(c, 1)].rearrange("a p b n -> p (a b) n")).then_inc(prefix_done["c"], 16)
                wreg(pool, "pool", glu_done, c + 2)
                pool.dma_start(conv_new_p[bass.ds(c, 1)].rearrange("a p n -> p (a n)"), cp[:, NP_TOK:NP_TOK + CW - 1]).then_inc(cstate_out, 16)
                pool.dma_start(conv_new_s[bass.ds(c * NB, NB)].rearrange("b p n -> p b n"), sg[:, :, NT:]).then_inc(cstate_out, 16)
                wreg(pool, "pool", cstate_out, c * 32 + 32)

        mixer.close()

        class Stage:

            def __init__(self, name):
                self.name, self.mem, self.sems = name, ctx.enter_context(ExitStack()), []
                self.pace = {e: self.sem(f"pace_{e}") for e in ("sp", "act", "pe", "dve", "pool")}
                self.run = ctx.enter_context(ExitStack())

            def sb(self, name, shape, dt=F32):
                return self.mem.enter_context(nc.sbuf_tensor(f"{self.name}_{name}", shape, dt))

            def sem(self, name):
                self.sems.append(self.mem.enter_context(nc.semaphore(f"{self.name}_{name}")))
                return self.sems[-1]

            def count(self, eng, name, s, v):
                eng.wait_ge(s, v)
                eng.sem_inc(self.pace[name], 1)

            def block(self):
                return self.run.enter_context(nc.Block())

            def end(self):
                self.run.close()
                clear_semaphores(self.sems)
                self.mem.close()

        def clear_semaphores(sems):
            with nc.Block() as between:
                @between.gpsimd
                def _(pool):
                    for s in sems:
                        pool.sem_clear(s)

        clear_semaphores(first_sems)
        first.close()

        class Units:

            def __init__(self, st, base, raw):
                self.st, self.base, self.raw = st, base, raw
                self.hi, self.lo = (st.sb(n, [P, 2, UW], F32R) for n in ("whi", "wlo"))
                self.ld = [st.sem(f"unit_ld{i}") for i in range(4)]
                self.hi_done, self.lo_done, self.done = (st.sem(n) for n in ("hi_done", "lo_done", "unit_done"))

            def load(self, sp, i, r):
                self.st.count(sp, "sp", self.lo_done, 4 * i + r + 1)
                sp.dma_start(self.raw[r % 4], w_units[bass.ds(4 * i + (r + self.base), 1)].rearrange("a p n -> p (a n)")).then_inc(self.ld[r % 4], 16)

            def high(self, act, i, r):
                self.st.count(act, "act", self.ld[r % 4], 16 * i + 16 * (r // 4) + 16)
                self.st.count(act, "act", self.done, 4 * i + r + 1)
                act.activation(self.hi[:, r % 2, :], self.raw[r % 4], ACT.Copy).then_inc(self.hi_done, 1)

            def low(self, pool, i, r):
                self.st.count(pool, "pool", self.hi_done, 4 * i + r + 1)
                pool.tensor_tensor(self.lo[:, r % 2, :], self.raw[r % 4], self.hi[:, r % 2, :].bitcast(F32), ALU.subtract).then_inc(self.lo_done, 1)

            def products(self, pe, i, r, parts, cols):
                self.st.count(pe, "pe", self.hi_done, 4 * i + r + 1)
                k0 = 0
                for out, n, xh, xl in parts:
                    wh = self.hi[:, r % 2, :].rearrange("p (k c) -> p k c", c=P)
                    for k in range(n):
                        for x in (xh, xl):
                            for o, c in cols:
                                pe.matmul(out[:, o:o + c.stop - c.start], wh[:, k0 + k, :], x[:, k, c], start=k == 0 and x is xh, stop=False)
                    k0 += n
                self.st.count(pe, "pe", self.lo_done, 4 * i + r + 5)
                k0 = 0
                for out, n, xh, xl in parts:
                    wl = self.lo[:, r % 2, :].rearrange("p (k c) -> p k c", c=P)
                    for k in range(n):
                        for o, c in cols:
                            m = pe.matmul(out[:, o:o + c.stop - c.start], wl[:, k0 + k, :], xh[:, k, c], start=False, stop=k == n - 1)
                    k0 += n
                m.then_inc(self.done, 1)

            def stream(self, block, n):
                @block.gpsimd
                def _(pool):
                    pool.sem_inc(self.lo_done, 4)
                    self.low(pool, 0, 0)
                    with pool.Fori(0, n // 4) as i:
                        for r in range(4):
                            self.low(pool, i, r + 1)

            def loads(self, sp, n):
                self.load(sp, 0, 0)
                with sp.Fori(0, n // 4) as i:
                    for r in range(4):
                        self.load(sp, i, r + 1)

        HT = T // 2
        TCOLS = [(0, slice(0, HT)), (512, slice(HT, T))]

        def halves(a):
            return a.rearrange("p (a b) -> p a b", a=2)[:, :, 0:HT]

        def piece(a, k):
            n = a.shape[1] // 4
            return a[:, k * n:(k + 1) * n, :]

        def load_pieces(sp, dst, src, loaded):
            for k in range(4):
                sp.dma_start(piece(dst, k), piece(src, k)).then_inc(loaded[k], 16)

        def split_hi(act, src, hi, loaded, counts, hi_done):
            for k in range(4):
                act.wait_ge(loaded[k], counts)
                act.activation(piece(hi, k), piece(src, k), ACT.Copy).then_inc(hi_done, 1)

        def split_lo(v, src, hi, lo, hi_done, lo_done):
            for k in range(4):
                v.wait_ge(hi_done, k + 1)
                v.tensor_tensor(piece(lo, k), piece(src, k), piece(hi, k).bitcast(F32), ALU.subtract).then_inc(lo_done, 1)

        st = Stage("g")
        xhi, xlo = (st.sb(n, [P, KD, T], F32R) for n in ("xhi", "xlo"))
        xf = st.sb("xf", [P, KD, T])
        raw4 = st.sb("raw", [P, 4, UW])
        units = Units(st, 0, [raw4[:, i, :] for i in range(4)])
        gout = st.sb("gout", [P, 4, T])
        x_in, x_hi = [st.sem(f"x_in{k}") for k in range(4)], st.sem("x_hi")
        x_split, g_act = st.sem("x_split"), st.sem("g_act")
        g_st, g_free = st.sem("g_st"), st.sem("g_free")
        NU1 = H + 2 * KD
        block = st.block()

        @block.sync
        def _(sp, st=st, units=units):
            load_pieces(sp, xf, xnT_spill, x_in)
            sp.sem_inc(g_free, 4)
            units.load(sp, 0, 0)
            with sp.Fori(0, NU1 // 4) as i:
                for r in range(4):
                    units.load(sp, i, r + 1)
                    st.count(sp, "sp", g_act, 4 * i + r + 5)
                    sp.dma_start(gates_T[bass.ds(4 * i + r, 1)].rearrange("a p n -> p (a n)"), gout[:, r, :]).then_inc(g_st, 16)
                    st.count(sp, "sp", g_st, 64 * i + 16 * r + 16)
                    sp.sem_inc(g_free, 1)

        @block.tensor
        def _(pe, st=st, units=units):
            pe.wait_ge(x_split, 4)
            pe.sem_inc(units.done, 2)
            with pe.Fori(0, NU1 // 4) as i:
                for r in range(4):
                    st.count(pe, "pe", g_act, 4 * i + r + 1)
                    units.products(pe, i, r, [(ps[r], KD, xhi, xlo)], TCOLS)

        @block.scalar
        def _(act, st=st, units=units):
            act.sem_inc(g_act, 4)
            split_hi(act, xf, xhi, x_in, 16, x_hi)
            units.high(act, 0, 0)

            def column(i, r, func):
                units.high(act, i, r + 1)
                st.count(act, "act", units.done, 4 * i + r + 3)
                st.count(act, "act", g_free, 4 * i + r + 1)
                act.activation(gout[:, r, :].rearrange("p (a b) -> p a b", a=2), halves(ps[r][:]), func).then_inc(g_act, 1)
            with act.Fori(0, 2 * KD // 4) as i:
                for r in range(4):
                    column(i, r, ACT.Sigmoid)
            with act.Fori(2 * KD // 4, NU1 // 4) as i:
                for r in range(4):
                    column(i, r, ACT.Silu)

        @block.vector
        def _(v, st=st):
            split_lo(v, xf, xhi, xlo, x_hi, x_split)

        units.stream(block, NU1)
        st.end()

        st = Stage("m")
        chi, clo, ohi, olo = (st.sb(n, [P, NC, T], F32R) for n in ("chi", "clo", "ohi", "olo"))
        cz, of = st.sb("cz", [P, NC, T]), st.sb("of", [P, H, T])
        raw4 = st.sb("raw", [P, 4, UW])
        units = Units(st, H + 2 * KD, [raw4[:, i, :] for i in range(4)])
        gin = [cz[:, 2 * i:2 * i + 2, :] for i in range(2)]
        mout = [cz[:, 4 + i, :] for i in range(2)]
        c_in, o_scaled = ([st.sem(f"{n}{k}") for k in range(4)] for n in ("c_in", "o_scaled"))
        o_in, z_in, c_hi, o_hi, c_split, o_split, mg_t, mg_out, m_st, m_free = (
            st.sem(n) for n in ("o_in", "z_in", "c_hi", "o_hi", "c_split", "o_split", "mg_t", "mg_out", "m_st", "m_free"))
        gin_ld = [st.sem(f"gin_ld{i}") for i in range(2)]
        block = st.block()

        @block.sync
        def _(sp, st=st, units=units):
            load_pieces(sp, cz, cT_spill, c_in)
            sp.dma_start(of[:], oT_spill).then_inc(o_in, 16)
            sp.sem_inc(m_free, 2)
            units.load(sp, 0, 0)
            sp.wait_ge(c_split, 4)
            sp.dma_start(cz[:], gates_T[2 * KD:].rearrange("a p n -> p a n")).then_inc(z_in, 16)
            sp.wait_ge(o_scaled[3], 1)

            def gates(n, slot):
                for j in range(2):
                    sp.dma_start(gin[slot][:, j, :], gates_T[bass.ds(n + j * KD, 1)].rearrange("a p n -> p (a n)")).then_inc(gin_ld[slot], 16)
            gates(0, 0)
            with sp.Fori(0, KD // 4) as i:
                for r in range(4):
                    units.load(sp, i, r + 1)
                    st.count(sp, "sp", mg_out, 4 * i + r + 2)
                    gates(4 * i + r + 1, (r + 1) % 2)
                    st.count(sp, "sp", mg_out, 4 * i + r + 3)
                    sp.dma_start(mT_spill[:, bass.ds(4 * i + r, 1), :].rearrange("p a n -> p (a n)"), mout[r % 2]).then_inc(m_st, 16)
                    st.count(sp, "sp", m_st, 64 * i + 16 * r + 16)
                    sp.sem_inc(m_free, 1)
            sp.wait_ge(gin_ld[0], 16 * 2 * (KD // 2 + 1))

        @block.tensor
        def _(pe, st=st, units=units):
            pe.wait_ge(c_split, 4)
            pe.wait_ge(o_split, 4)
            pe.sem_inc(units.done, 2)
            with pe.Fori(0, KD // 4) as i:
                for r in range(4):
                    st.count(pe, "pe", mg_out, 4 * i + r + 1)
                    a = 2 * (r % 2)
                    units.products(pe, i, r, [(ps[a], NC, chi, clo), (ps[a + 1], H, ohi, olo)], TCOLS)

        @block.scalar
        def _(act, st=st, units=units):
            split_hi(act, cz, chi, c_in, 16, c_hi)
            split_hi(act, of, ohi, o_scaled, 1, o_hi)
            units.high(act, 0, 0)
            with act.Fori(0, KD // 4) as i:
                for r in range(4):
                    units.high(act, i, r + 1)

        @block.vector
        def _(v, st=st, units=units):
            split_lo(v, cz, chi, clo, c_hi, c_split)
            v.wait_ge(o_in, 16)
            v.wait_ge(z_in, 16)
            for k in range(4):
                v.scalar_tensor_tensor(piece(of, k), piece(cz, k), par[:, PCOLS["dn_g"][0]:PCOLS["dn_g"][0] + 1], piece(of, k),
                                       ALU.mult, ALU.mult).then_inc(o_scaled[k], 1)
            split_lo(v, of, ohi, olo, o_hi, o_split)
            v.sem_inc(mg_out, 2)
            with v.Fori(0, KD // 4) as i:
                for r in range(4):
                    g = gin[r % 2]
                    a = 2 * (r % 2)
                    st.count(v, "dve", gin_ld[r % 2], 64 * i + 32 * (r // 2) + 32)
                    st.count(v, "dve", units.done, 4 * i + r + 3)
                    st.count(v, "dve", m_free, 4 * i + r + 1)
                    for j in range(2):
                        g3 = g[:, j, :].rearrange("p (a b) -> p a b", a=2)
                        v.tensor_tensor(g3, g3, halves(ps[a + j][:]), ALU.mult).then_inc(mg_t, 1)
                    st.count(v, "dve", mg_t, 8 * i + 2 * r + 2)
                    v.tensor_tensor(mout[r % 2], g[:, 0, :], g[:, 1, :], ALU.add).then_inc(mg_out, 1)

        units.stream(block, KD)
        st.end()

        st = Stage("o")
        mhi, mlo = (st.sb(n, [P, KD, T], F32R) for n in ("mhi", "mlo"))
        xbuf = st.sb("xbuf", [P, TILES * D])
        mf = xbuf[:].rearrange("p (k t) -> p k t", k=KD)
        x1 = xbuf[:].rearrange("p (t d) -> p t d", t=TILES)
        raw4 = st.sb("raw", [P, 4, UW])
        units = Units(st, H + 3 * KD, [raw4[:, i, :] for i in range(4)])
        gain, junk, xt_out = raw4[:, 0, :], raw4[:, 1, :], [raw4[:, 2, i * 1024:(i + 1) * 1024] for i in range(2)]
        nsm = st.sb("nsm", [P, 4, TILES])
        m_in = [st.sem(f"m_in{k}") for k in range(4)]
        m_hi, m_split, xr_ld, wo_mm, wo_add, g_ld, n_sq, n_ms, n_root, n_rs, n_done, n_tr, n_evac, spill_done = (
            st.sem(n) for n in ("m_hi", "m_split", "xr_ld", "wo_mm", "wo_add", "g_ld", "n_sq", "n_ms", "n_root", "n_rs", "n_done", "n_tr",
                                "n_evac", "spill_done"))
        x1_out = [st.sem(f"x1_out{t}") for t in range(TILES)]
        xt_st = [st.sem(f"xt_st{i}") for i in range(2)]
        block = st.block()

        @block.sync
        def _(sp, st=st, units=units):
            load_pieces(sp, mf, mT_spill, m_in)
            units.load(sp, 0, 0)
            sp.wait_ge(m_split, 4)
            sp.dma_start(x1[:, 0:PT, :], x_prompt.rearrange("(t p) d -> p t d", p=P)).then_inc(xr_ld, 16)
            sp.dma_start(x1[:, PT, :], x_sample).then_inc(xr_ld, 16)
            with sp.Fori(0, 2 * NOC // 4) as i:
                for r in range(4):
                    units.load(sp, i, r + 1)
            sp.wait_ge(units.lo_done, 2 * NOC + 5)
            sp.dma_start(gain, ffn_g).then_inc(g_ld, 16)
            for t in range(TILES):
                sp.wait_ge(wo_add, TILES * (NOC - 1) + t + 1 + TILES)
                sp.dma_start(x1_spill[:, t * D:(t + 1) * D], x1[:, t, :]).then_inc(x1_out[t], 16)
            for n in range(2 * TILES):
                t, half = n // 2, n % 2
                sp.wait_ge(n_evac, n + 1)
                sp.dma_start(xT_spill[:, 8 * half:8 * half + 8, t * P:(t + 1) * P],
                             xt_out[half].rearrange("p (k c) -> p k c", k=8)).then_inc(xt_st[half], 16)
            sp.wait_ge(n_done, TILES)
            sp.dma_start(xg_spill, x1[:, DT:, :]).then_inc(spill_done, 16)
            sp.wait_ge(spill_done, 16)
            for s in (*xt_st, ):
                sp.wait_ge(s, 16 * TILES)

        @block.tensor
        def _(pe, st=st, units=units):
            pe.wait_ge(m_split, 4)
            pe.sem_inc(units.done, 2)
            with pe.Fori(0, 2 * NOC // 4) as i:
                for r in range(4):
                    kh = r % 2
                    oc5 = (2 * i + r // 2) * TILES
                    st.count(pe, "pe", units.hi_done, 4 * i + r + 1)
                    wh, wl = (w[:, r % 2, :].rearrange("p (k c) -> p k c", k=8) for w in (units.hi, units.lo))

                    def bank(t):
                        return ps[t // 2][:, (t % 2) * 512:(t % 2) * 512 + OCW]
                    for t in range(TILES):
                        if kh == 0:
                            st.count(pe, "pe", wo_add, oc5 + t + 1)
                        for k in range(8):
                            for x in (mhi, mlo):
                                pe.matmul(bank(t), x[:, 8 * kh + k, t * P:(t + 1) * P], wh[:, k, :], start=kh == 0 and k == 0 and x is mhi, stop=False)
                    st.count(pe, "pe", units.lo_done, 4 * i + r + 5)
                    for t in range(TILES):
                        for k in range(8):
                            m = pe.matmul(bank(t), mhi[:, 8 * kh + k, t * P:(t + 1) * P], wl[:, k, :], start=False, stop=kh == 1 and k == 7)
                        if kh == 1:
                            m.then_inc(wo_mm, 1)
                    if kh == 0:
                        m.then_inc(units.done, 1)
                    else:
                        st.count(pe, "pe", wo_mm, oc5 + TILES)
                        pe.sem_inc(units.done, 1)
            pe.wait_ge(wo_add, NOC * TILES + TILES)
            for n in range(2 * TILES):
                t, half = n // 2, n % 2
                pe.wait_ge(n_done, t + 1)
                if n >= 4:
                    pe.wait_ge(n_evac, n - 3)
                for k in range(8):
                    kk = half * 8 + k
                    m = pe.transpose(ps[n % 4][:, k * P:(k + 1) * P], x1[:, t, kk * P:(kk + 1) * P], ident)
                m.then_inc(n_tr, 1)

        @block.scalar
        def _(act, st=st, units=units):
            split_hi(act, mf, mhi, m_in, 16, m_hi)
            units.high(act, 0, 0)
            with act.Fori(0, 2 * NOC // 4) as i:
                for r in range(4):
                    units.high(act, i, r + 1)
            act.wait_ge(units.lo_done, 2 * NOC + 5)
            for t in range(TILES):
                act.wait_ge(wo_add, TILES * (NOC - 1) + t + 1 + TILES)
                act.activation(junk, x1[:, t, :], ACT.Square, accum_out=nsm[:, 0, t:t + 1]).then_inc(n_sq, 1)
                act.wait_ge(n_sq, t + 1)
            act.wait_ge(n_ms, 1)
            act.activation(nsm[:, 2, :], nsm[:, 1, :], ACT.Sqrt).then_inc(n_root, 1)

        @block.vector
        def _(v, st=st, units=units):
            v.memset(nsm[:], 0.0)
            split_lo(v, mf, mhi, mlo, m_hi, m_split)
            v.sem_inc(wo_add, TILES)
            v.wait_ge(xr_ld, 32)
            with v.Fori(0, NOC) as oc:
                for t in range(TILES):
                    st.count(v, "dve", wo_mm, oc * TILES + t + 1)
                    dst = x1[:, t, bass.ds(oc * OCW, OCW)]
                    v.tensor_tensor(dst, dst, ps[t // 2][:, (t % 2) * 512:(t % 2) * 512 + OCW], ALU.add).then_inc(wo_add, 1)
            v.wait_ge(n_sq, TILES)
            v.tensor_scalar(nsm[:, 1, :], nsm[:, 0, :], 1.0 / D, EPS, ALU.mult, ALU.add).then_inc(n_ms, 1)
            v.wait_ge(n_root, 1)
            v.reciprocal(nsm[:, 3, :], nsm[:, 2, :]).then_inc(n_rs, 1)
            v.wait_ge(n_rs, 1)
            v.wait_ge(g_ld, 16)

            def evac(n):
                v.wait_ge(n_tr, n + 1)
                if n >= 2:
                    v.wait_ge(xt_st[n % 2], 16 * (n // 2))
                v.tensor_copy(xt_out[n % 2], ps[n % 4][:]).then_inc(n_evac, 1)
            for t in range(TILES):
                v.wait_ge(x1_out[t], 16)
                v.scalar_tensor_tensor(x1[:, t, :], x1[:, t, :], nsm[:, 3, t:t + 1], gain, ALU.mult, ALU.mult).then_inc(n_done, 1)
                if t:
                    evac(2 * t - 2)
                    evac(2 * t - 1)
            evac(2 * TILES - 2)
            evac(2 * TILES - 1)

        units.stream(block, 2 * NOC)
        st.end()

        st = Stage("q")
        x2hi, x2lo = (st.sb(n, [P, KD, T], F32R) for n in ("x2hi", "x2lo"))
        raw4 = st.sb("raw", [P, 4, UW])
        units = Units(st, H + 3 * KD + 2 * NOC, [raw4[:, i, :] for i in range(4)])
        qa = st.sb("qa", [P, KD * T])
        xf2 = qa[:].rearrange("p (k t) -> p k t", k=KD)
        used = [0]

        def area(*dims):
            n = 1
            for d in dims:
                n *= d
            o = used[0]
            used[0] += n
            assert used[0] <= KD * T
            w = qa[:, o:o + n]
            return w if len(dims) == 1 else w.rearrange("p (a b) -> p a b", a=dims[0])

        keyT = area(HP, NK)
        qh, sc, sc2 = area(T), area(TILES, P), area(TILES, P)
        stop_, itop = area(TILES, HP * TOPK), area(TILES, HP * TOPK)
        topbuf = area(TILES, TOPK)
        itop_u = area(TILES, TOPK).bitcast(U32)
        selbuf = area(SELW)
        chosen = selbuf[:, 0:3 * DT * SLOTS].rearrange("p (a s) -> p a s", s=SLOTS)
        gidx = selbuf[:, 3 * DT * SLOTS:(3 * DT + GT) * SLOTS].rearrange("p (a s) -> p a s", s=SLOTS).bitcast(U32)
        ggate = selbuf[:, (3 * DT + GT) * SLOTS:].rearrange("p (a s) -> p a s", s=SLOTS)
        posu = area(SLOTS).bitcast(U32)
        posi = area(2, SLOTS).bitcast(U32)
        iota_i, iota16 = st.sb("iota_i", [P, TOPK], mybir.dt.int32), st.sb("iota16", [P, TOPK])
        x_in = [st.sem(f"x_in{k}") for k in range(4)]
        x_hi, x_split, key_ld, q_evac, s_mm, s_evac, tk_done, tk_link, sel_link, sel_pre, sel_exp, iota_st, selected, spill_done = (
            st.sem(n) for n in ("x_hi", "x_split", "key_ld", "q_evac", "s_mm", "s_evac", "tk_done", "tk_link", "sel_link", "sel_pre",
                                "sel_exp", "iota_st", "selected", "spill_done"))

        def gate_of(t):
            return chosen[:, 3 * t + 2, :] if t < DT else ggate[:, t - DT, :]

        block = st.block()

        @block.sync
        def _(sp, st=st, units=units):
            load_pieces(sp, xf2, xT_spill, x_in)
            units.load(sp, 0, 0)
            with sp.Fori(0, HP // 4) as i:
                for r in range(4):
                    units.load(sp, i, r + 1)
            sp.wait_ge(selected, 1)
            sp.dma_start(sel_spill, selbuf).then_inc(spill_done, 16)
            sp.wait_ge(spill_done, 16)

        @block.tensor
        def _(pe, st=st, units=units):
            pe.wait_ge(x_split, 4)
            pe.wait_ge(key_ld, 16)
            pe.sem_inc(units.done, 2)
            with pe.Fori(0, HP // 4) as i:
                for r in range(4):
                    j = 4 * i + r
                    st.count(pe, "pe", q_evac, j + 1)
                    units.products(pe, i, r, [(ps[r % 2], KD, x2hi, x2lo)], TCOLS)
                    st.count(pe, "pe", q_evac, j + 3)
                    st.count(pe, "pe", s_evac, j + 1)
                    for t in range(TILES):
                        m = pe.matmul(ps[2 + r % 2][:, t * P:(t + 1) * P], qh[:, t * P:(t + 1) * P],
                                      keyT[:, bass.ds(j, 1), :].rearrange("p a n -> p (a n)"), start=True, stop=True)
                    m.then_inc(s_mm, 1)

        @block.scalar
        def _(act, st=st, units=units):
            split_hi(act, xf2, x2hi, x_in, 16, x_hi)
            act.wait_ge(x_split, 4)
            act.dma_start(keyT.rearrange("p a b -> p (a b)"), keys).then_inc(key_ld, 16)
            act.sem_inc(q_evac, 2)
            act.sem_inc(s_evac, 2)
            units.high(act, 0, 0)
            with act.Fori(0, HP // 4) as i:
                for r in range(4):
                    j = 4 * i + r
                    units.high(act, i, r + 1)
                    st.count(act, "act", units.done, j + 3)
                    st.count(act, "act", s_evac, j + 2)
                    act.activation(qh.rearrange("p (a b) -> p a b", a=2), halves(ps[r % 2][:]), ACT.Copy).then_inc(q_evac, 1)
                    st.count(act, "act", s_mm, j + 1)
                    st.count(act, "act", tk_done, j + 1)
                    act.activation(sc.rearrange("p a b -> p (a b)"), ps[2 + r % 2][:, 0:T], ACT.Copy).then_inc(s_evac, 1)
            for t in range(TILES):
                act.wait_ge(sel_pre, t + 1)
                act.activation(gate_of(t), gate_of(t), ACT.Exp).then_inc(sel_exp, 1)

        @block.vector
        def _(v, st=st, units=units):
            split_lo(v, xf2, x2hi, x2lo, x_hi, x_split)
            v.wait_ge(x_split, 4)
            v.sem_inc(tk_done, 1)
            NTK = 3 * TILES + 2
            with v.Fori(0, HP) as j:
                n = [0]

                def tk(ins):
                    n[0] += 1
                    ins.then_inc(tk_link, 1)
                st.count(v, "dve", s_evac, j + 3)
                top = topbuf
                for t in range(TILES):
                    tk(v.max(top[:, t, 0:8], sc[:, t, :]))
                st.count(v, "dve", tk_link, j * NTK + TILES)
                for t in range(TILES):
                    v.max_index(itop_u[:, t, 0:8], top[:, t, 0:8], sc[:, t, :])
                    tk(v.match_replace(sc2[:, t, :], top[:, t, 0:8], sc[:, t, :], -3.0e38))
                st.count(v, "dve", tk_link, j * NTK + 2 * TILES)
                for t in range(TILES):
                    tk(v.max(top[:, t, 8:16], sc2[:, t, :]))
                st.count(v, "dve", tk_link, j * NTK + 3 * TILES)
                for t in range(TILES):
                    ins = v.max_index(itop_u[:, t, 8:16], top[:, t, 8:16], sc2[:, t, :])
                tk(ins)
                st.count(v, "dve", tk_link, j * NTK + 3 * TILES + 1)
                v.tensor_copy(stop_[:, :, bass.ds(j * TOPK, TOPK)], top)
                tk(v.tensor_copy(itop[:, :, bass.ds(j * TOPK, TOPK)], itop_u))
                st.count(v, "dve", tk_link, j * NTK + NTK)
                v.sem_inc(tk_done, 1)
            v.wait_ge(s_evac, HP + 2)
            v.wait_ge(units.lo_done, HP + 5)
            sl = Link(v, "dve", sel_link)
            v.wait_ge(iota_st, 2)
            rw = raw4[:].rearrange("p a b -> p (a b)")
            cand = rw[:, 0:0 + PH * TOPK * TOPK].rearrange("p (a b) -> p a b", a=PH)
            cand2 = rw[:, 2048:2048 + PH * TOPK * TOPK].rearrange("p (a b) -> p a b", a=PH)
            oh = rw[:, 4096:4096 + PH * TOPK * TOPK].rearrange("p (a b) -> p a b", a=PH * TOPK)
            oh4 = rw[:, 4096:4096 + PH * TOPK * TOPK].rearrange("p (h a b) -> p h a b", h=PH, a=TOPK)
            val = rw[:, 6144:6144 + PH * TOPK]
            posf = rw[:, 6272:6272 + 2 * PH * TOPK].rearrange("p (a b) -> p a b", a=2)
            got = rw[:, 6528:6528 + 2 * PH * TOPK].rearrange("p (a b) -> p a b", a=2)
            stf = rw[:, 6784:6784 + PH * TOPK].rearrange("p (a b) -> p a b", a=PH)
            red = rw[:, 6912:6912 + PH]
            for t in range(TILES):
                s4 = stop_[:, t, :].rearrange("p (h q k) -> p h q k", h=PH, q=2)
                i4 = itop[:, t, :].rearrange("p (h q k) -> p h q k", h=PH, q=2)
                sl(v.tensor_tensor(cand.rearrange("p h (a b) -> p h a b", a=TOPK), s4[:, :, 0, :].unsqueeze(3).to_broadcast([P, PH, TOPK, TOPK]),
                                   s4[:, :, 1, :].unsqueeze(2).to_broadcast([P, PH, TOPK, TOPK]), ALU.add))
                pu = posu.rearrange("p (h k) -> p h k", h=PH)
                for h in range(PH):
                    ins = v.max(stf[:, h, 0:8], cand[:, h, :])
                sl(ins)
                for h in range(PH):
                    v.max_index(pu[:, h, 0:8], stf[:, h, 0:8], cand[:, h, :])
                    ins = v.match_replace(cand2[:, h, :], stf[:, h, 0:8], cand[:, h, :], -3.0e38)
                sl(ins)
                for h in range(PH):
                    ins = v.max(stf[:, h, 8:16], cand2[:, h, :])
                sl(ins)
                for h in range(PH):
                    ins = v.max_index(pu[:, h, 8:16], stf[:, h, 8:16], cand2[:, h, :])
                sl(ins)
                gt = gate_of(t).rearrange("p (h k) -> p h k", h=PH)
                v.tensor_tensor(gt, stf, stf[:, :, 0:1].to_broadcast([P, PH, TOPK]), ALU.subtract).then_inc(sel_pre, 1)
                v.tensor_scalar(posi[:, 0, :], posu, 4, None, ALU.logical_shift_right)
                sl(v.tensor_scalar(posi[:, 1, :], posu, 15, None, ALU.bitwise_and))
                sl(v.tensor_copy(posf, posi))
                for q in range(2):
                    sl(v.tensor_tensor(oh, iota16[:].unsqueeze(1).to_broadcast([P, PH * TOPK, TOPK]),
                                       posf[:, q, :].unsqueeze(2).to_broadcast([P, PH * TOPK, TOPK]), ALU.is_equal))
                    for h in range(PH):
                        ins = v.tensor_tensor(oh4[:, h], oh4[:, h], i4[:, h, q, :].unsqueeze(1).to_broadcast([P, TOPK, TOPK]), ALU.mult)
                    sl(ins)
                    sl(v.tensor_reduce(chosen[:, 3 * t + q, :] if t < DT else got[:, q, :], oh, X, ALU.add))
                if t >= DT:
                    sl(v.scalar_tensor_tensor(val, got[:, 0, :], float(NK), got[:, 1, :], ALU.mult, ALU.add))
                    sl(v.tensor_copy(gidx[:, t - DT, :], val))
                v.wait_ge(sel_exp, t + 1)
                sl(v.tensor_reduce(red, gt, X, ALU.add))
                sl(v.reciprocal(red, red))
                sl(v.tensor_tensor(gt, gt, red.unsqueeze(2).to_broadcast([P, PH, TOPK]), ALU.mult))
            v.sem_inc(selected, 1)

        @block.gpsimd
        def _(pool, units=units):
            pool.iota(iota_i[:], pattern=[[1, TOPK]], base=0, channel_multiplier=0).then_inc(iota_st, 1)
            pool.wait_ge(iota_st, 1)
            pool.tensor_copy(iota16[:], iota_i[:]).then_inc(iota_st, 1)
            pool.sem_inc(units.lo_done, 4)
            units.low(pool, 0, 0)
            with pool.Fori(0, HP // 4) as i:
                for r in range(4):
                    units.low(pool, i, r + 1)

        st.end()

        def sb2(name, shape, dt=F32):
            return ctx.enter_context(nc.sbuf_tensor(name, shape, dt))

        def sem2(name):
            return ctx.enter_context(nc.semaphore(name))

        xhi, xlo = sb2("xhi", [P, KD, TD], F32R), sb2("xlo", [P, KD, TD], F32R)
        whi, wlo = sb2("whi", [P, 2, UNIT], F32R), sb2("wlo", [P, 2, UNIT], F32R)
        ahi, alo = sb2("ahi", [P, ET, TD], F32R), sb2("alo", [P, ET, TD], F32R)
        rows2 = sb2("rows2", [P, 2 * GT * D])
        x1g = rows2[:, 0:GT * D].rearrange("p (t d) -> p t d", t=GT)
        xg = rows2[:, GT * D:2 * GT * D].rearrange("p (t d) -> p t d", t=GT)
        xT = rows2[:, 0:KD * TD].rearrange("p (k t) -> p k t", k=KD)
        assert KD * TD <= 2 * GT * D
        sel = sb2("sel", [P, SELW])
        chosen2 = sel[:, 0:3 * DT * SLOTS].rearrange("p (a s) -> p a s", s=SLOTS)
        gidx2 = sel[:, 3 * DT * SLOTS:(3 * DT + GT) * SLOTS].rearrange("p (a s) -> p a s", s=SLOTS).bitcast(U32)
        ggate2 = sel[:, (3 * DT + GT) * SLOTS:].rearrange("p (a s) -> p a s", s=SLOTS)
        gbuf, hbuf = sb2("gbuf", [P, 2, TD]), sb2("hbuf", [P, 2, TD])
        work = sb2("work", [P, KD * TD + 4 * D + 4 * UNIT])

        def wk(off, *dims):
            n = 1
            for d in dims:
                n *= d
            w = work[:, off:off + n]
            if len(dims) == 2:
                w = w.rearrange("p (a b) -> p a b", a=dims[0])
            return w

        ROWS, RAW = KD * TD, KD * TD + 4 * D
        accT = wk(0, KD, TD)
        urow = [wk(ROWS + i * D, D) for i in range(2)]
        vrow = [wk(ROWS + (2 + i) * D, D) for i in range(2)]
        raw = [wk(RAW + i * UNIT, UNIT) for i in range(4)]
        stage = [wk(0, NK, GTOK), wk(NK * GTOK, NK, GTOK)]
        OH = 2 * NK * GTOK
        oneh = [[wk(OH + (2 * i + q) * GB * NK, GB, NK) for q in range(2)] for i in range(2)]
        selT = wk(OH + 4 * GB * NK, 3, TD)
        fin_dense = wk(ROWS, DT, D)
        fin_gain = wk(ROWS + DT * D, D)
        fin_junk = wk(RAW, D)
        iota_i2, iota_k = sb2("iota_i2", [P, NK], mybir.dt.int32), sb2("iota_k", [P, NK])
        cur_idx = sb2("cur_idx", [P, 2, RING], U32)
        hid, act_w, gcol, act_w2 = (sb2(n, [P, RING]) for n in ("hid", "act_w", "gcol", "act_w2"))
        fin_small = sb2("fin_small", [P, 3, TILES])

        pace2 = {e: sem2(f"pace2_{e}") for e in ("sp", "act", "pe", "dve", "pool")}

        def wait_count(eng, name, s, v):
            eng.wait_ge(s, v)
            eng.sem_inc(pace2[name], 1)

        sel_ld, rows_ld, xhi_done, xsplit, iota_ready = (sem2(n) for n in ("sel_ld", "rows_ld", "xhi_done", "xsplit", "iota_ready"))
        xT_ld = [sem2(f"xT_ld{k}") for k in range(4)]
        sel_tr, sel_cp, oh_key, oh_row, oh_done, g_mm, g_evac = (
            sem2(n) for n in ("sel_tr", "sel_cp", "oh_key", "oh_row", "oh_done", "g_mm", "g_evac"))
        g_out = [sem2("g_out0"), sem2("g_out1")]
        un_ld = [sem2(f"un_ld{i}") for i in range(4)]
        gt_ld = [sem2("gt_ld0"), sem2("gt_ld1")]
        hi_done, lo_done, unit_free, hid_mm, v_mm = (sem2(n) for n in ("hi_done", "lo_done", "unit_free", "hid_mm", "v_mm"))
        gelu_done, a_raw, a_split, a_done, v_add, zeroed = (sem2(n) for n in ("gelu_done", "a_raw", "a_split", "a_done", "v_add", "zeroed"))
        idx_cur, ghid, ggelu, gcoef, u_used, v_used = (sem2(n) for n in ("idx_cur", "ghid", "ggelu", "gcoef", "u_used", "v_used"))
        u_ld = [sem2(f"u_ld{i}") for i in range(RING)]
        v_ld = [sem2(f"v_ld{i}") for i in range(RING)]
        f_begin, f_tr, f_add, f_ld, f_ss, f_ms, f_root, f_y, f_out = (
            sem2("f_" + n) for n in ("begin", "tr", "add", "ld", "ss", "ms", "root", "y", "out"))
        NBB = GTOK // GB
        NGG = TD // GTOK
        CPG = CHUNKS // GT
        block2 = ctx.enter_context(nc.Block())

        def fin_rows(t):
            return fin_dense[:, t, :] if t < DT else x1g[:, t - DT, :]

        FIN_ORDER = [*range(DT, TILES), *range(DT)]

        @block2.sync
        def _(sp):
            sp.dma_start(sel[:], sel_spill).then_inc(sel_ld, 16)
            load_pieces(sp, xT, xT_spill[:, :, 0:TD], xT_ld)
            sp.wait_ge(xsplit, 4)
            sp.dma_start(rows2[:, 0:GT * D], x1_spill[:, DT * D:]).then_inc(rows_ld, 16)
            sp.dma_start(rows2[:, GT * D:], xg_spill.rearrange("p t d -> p (t d)")).then_inc(rows_ld, 16)
            for n in range(NGG):
                sp.wait_ge(g_evac, (n + 1) * NBB + 2)
                sp.dma_start(gates_dram.rearrange("i j t -> j i t")[:, :, n * GTOK:(n + 1) * GTOK], stage[n % 2]).then_inc(g_out[n % 2], 16)
            for n in range(2):
                sp.wait_ge(g_out[n], 16 * (NGG // 2))
            sp.wait_ge(g_mm, NGG * NBB + 2)
            sp.wait_ge(sel_cp, 3)
            with sp.Fori(0, CHUNKS) as c:
                for m in range(NU):
                    wait_count(sp, "sp", lo_done, c * NU + m + 1)
                    src = u_units[bass.ds(c * (2 * ET) + m, 1)] if m < 2 * ET else v_units[bass.ds(c * (NU - 2 * ET) + m - 2 * ET, 1)]
                    sp.dma_start(raw[m % 4], src.rearrange("a p n -> p (a n)")).then_inc(un_ld[m % 4], 16)
                    if m % 2 == 0 and 2 <= m <= 2 * ET:
                        e = m // 2 - 1
                        wait_count(sp, "sp", a_raw, c * ET + e + 1)
                        sp.dma_start(gbuf[:, e % 2, :], gates_dram[bass.ds(c * ET + e, 1)].rearrange("a p n -> p (a n)")).then_inc(gt_ld[e % 2], 16)
            sp.wait_ge(f_begin, 1)
            sp.dma_start(fin_gain, final_g).then_inc(f_ld, 16)
            sp.dma_start(wk(ROWS, DT * D), x1_spill[:, 0:DT * D]).then_inc(f_ld, 16)
            for i, t in enumerate(FIN_ORDER):
                sp.wait_ge(f_y, i + 1)
                dst = y_prompt[t * P:(t + 1) * P, :] if t < PT else y_sample
                sp.dma_start(dst, fin_rows(t)).then_inc(f_out, 16)
            sp.wait_ge(f_out, 16 * TILES)

        @block2.tensor
        def _(pe):
            pe.wait_ge(sel_ld, 16)
            for a in range(3):
                for t in range(DT):
                    m = pe.transpose(ps[a // 2][:, (a % 2) * 512 + t * P:(a % 2) * 512 + (t + 1) * P], chosen2[:, 3 * t + a, :], ident)
            m.then_inc(sel_tr, 1)
            pe.wait_ge(sel_cp, 3)
            pe.sem_inc(g_mm, 2)
            with pe.Fori(0, NGG * NBB // 2) as i:
                for r in range(2):
                    wait_count(pe, "pe", oh_key, 2 * i + r + 1)
                    wait_count(pe, "pe", oh_done, 2 * i + r + 1)
                    wait_count(pe, "pe", g_evac, 2 * i + r + 1)
                    for b in range(GB):
                        m = pe.matmul(ps[2 + r][:, b * P:(b + 1) * P], oneh[r][0][:, b, :], oneh[r][1][:, b, :], start=True, stop=True)
                    m.then_inc(g_mm, 1)
            pe.wait_ge(g_evac, NGG * NBB + 2)
            pe.wait_ge(xsplit, 4)
            pe.sem_inc(unit_free, 2)
            with pe.Fori(0, CHUNKS) as c:
                for m in range(NU):
                    wait_count(pe, "pe", hi_done, c * NU + m + 1)
                    if m < 2 * ET:
                        e, half = m // 2, m % 2
                        out = ps[0][:, (e % 2) * 512:(e % 2) * 512 + TD]
                        if half == 0:
                            wait_count(pe, "pe", gelu_done, c * ET + e + 1)
                        h3, l3 = (w[:, m % 2, :].rearrange("p (k c) -> p k c", k=8) for w in (whi, wlo))
                        for k in range(8):
                            pe.matmul(out, h3[:, k, :], xhi[:, 8 * half + k, :], start=half == 0 and k == 0, stop=False)
                            pe.matmul(out, h3[:, k, :], xlo[:, 8 * half + k, :], start=False, stop=False)
                        wait_count(pe, "pe", lo_done, c * NU + m + 5)
                        for k in range(8):
                            mmi = pe.matmul(out, l3[:, k, :], xhi[:, 8 * half + k, :], start=False, stop=half == 1 and k == 7)
                        mmi.then_inc(unit_free, 1)
                        if half == 1:
                            wait_count(pe, "pe", unit_free, c * NU + m + 3)
                            pe.sem_inc(hid_mm, 1)
                    else:
                        h4, l4 = (w[:, m % 2, :].rearrange("p (d e c) -> p d e c", d=2, e=ET) for w in (whi, wlo))
                        for q in range(2):
                            d = 2 * (m - 2 * ET) + q
                            out = ps[1 + (d % 4) // 2][:, (d % 2) * 512:(d % 2) * 512 + TD]
                            wait_count(pe, "pe", v_add, c * KD + d + 1)
                            for e in range(ET):
                                if d == 0:
                                    wait_count(pe, "pe", a_done, c * ET + e + 3)
                                pe.matmul(out, h4[:, q, e, :], ahi[:, e, :], start=e == 0, stop=False)
                                pe.matmul(out, h4[:, q, e, :], alo[:, e, :], start=False, stop=False)
                            if q == 0:
                                wait_count(pe, "pe", lo_done, c * NU + m + 5)
                            for e in range(ET):
                                mmi = pe.matmul(out, l4[:, q, e, :], ahi[:, e, :], start=False, stop=e == ET - 1)
                            mmi.then_inc(v_mm, 1)
                        wait_count(pe, "pe", v_mm, c * KD + d + 1)
                        pe.sem_inc(unit_free, 1)
            pe.wait_ge(f_begin, 1)
            for t in range(DT):
                for half in range(2):
                    n = 2 * t + half
                    if n >= 4:
                        pe.wait_ge(f_add, n - 3)
                    for k in range(8):
                        mt = pe.transpose(ps[n % 4][:, k * P:(k + 1) * P], accT[:, half * 8 + k, t * P:(t + 1) * P], ident)
                    mt.then_inc(f_tr, 1)

        @block2.scalar
        def _(act):
            act.sem_inc(g_evac, 2)
            split_hi(act, xT, xhi, xT_ld, 16, xhi_done)
            for n in range(NGG):
                if n >= 2:
                    act.wait_ge(g_out[n % 2], 16 * (n // 2))
                for b in range(NBB):
                    q = n * NBB + b
                    act.wait_ge(g_mm, q + 3)
                    act.activation(stage[n % 2][:, :, b * GB:(b + 1) * GB],
                                   ps[2 + q % 2][:].rearrange("p (b i) -> p i b", b=GB), ACT.Copy).then_inc(g_evac, 1)
            act.sem_inc(gelu_done, 2)

            def gelu_tile(c, e):
                wait_count(act, "act", hid_mm, c * ET + e + 1)
                wait_count(act, "act", a_done, c * ET + e + 1)
                act.activation(hbuf[:, e % 2, :], ps[0][:, (e % 2) * 512:(e % 2) * 512 + TD], ACT.Gelu_apprx_tanh).then_inc(gelu_done, 1)

            with act.Fori(0, CHUNKS) as c:
                for m in range(NU):
                    wait_count(act, "act", un_ld[m % 4], (c * (NU // 4) + m // 4) * 16 + 16)
                    wait_count(act, "act", unit_free, c * NU + m + 1)
                    act.activation(whi[:, m % 2, :], raw[m % 4], ACT.Copy).then_inc(hi_done, 1)
                    if 3 <= m < 2 * ET and m % 2 == 1:
                        gelu_tile(c, m // 2 - 1)
                    if m == 2 * ET:
                        gelu_tile(c, ET - 1)
                    if m % 4 == 2:
                        wait_count(act, "act", ghid, c * STEPS + m // 4 + 1)
                        act.activation(act_w[:], hid[:], ACT.Gelu_apprx_tanh).then_inc(ggelu, 1)
            for i in range(TILES):
                act.wait_ge(f_ss, i + 1)
                act.activation(fin_small[:, 1, i:i + 1], fin_small[:, 0, i:i + 1], ACT.Sqrt).then_inc(f_root, 1)

        @block2.vector
        def _(v):
            v.wait_ge(sel_tr, 1)
            for a in range(3):
                v.tensor_copy(selT[:, a, :], ps[a // 2][:, (a % 2) * 512:(a % 2) * 512 + TD]).then_inc(sel_cp, 1)
            v.wait_ge(sel_cp, 3)
            split_lo(v, xT, xhi, xlo, xhi_done, xsplit)
            v.wait_ge(iota_ready, 2)
            iota_b = iota_k[:].unsqueeze(1).to_broadcast([P, GB, NK])
            with v.Fori(0, NGG * NBB // 2) as i:
                for r in range(2):
                    tok = bass.ds((2 * i + r) * GB, GB)
                    wait_count(v, "dve", g_mm, 2 * i + r + 1)
                    v.tensor_tensor(oneh[r][1], iota_b, selT[:, 0, tok].unsqueeze(2).to_broadcast([P, GB, NK]), ALU.is_equal).then_inc(oh_row, 1)
                    v.tensor_tensor(oneh[r][0], iota_b, selT[:, 1, tok].unsqueeze(2).to_broadcast([P, GB, NK]), ALU.is_equal).then_inc(oh_key, 1)
            for n in range(2):
                v.wait_ge(g_out[n], 16 * (NGG // 2))
            v.memset(accT, 0.0).then_inc(zeroed, 1)
            v.sem_inc(v_add, 4)
            v.sem_inc(a_raw, 2)
            v.sem_inc(a_done, 2)
            v.wait_ge(g_mm, NGG * NBB + 2)
            v.sem_inc(u_used, RING)
            v.sem_inc(v_used, RING)
            v.wait_ge(zeroed, 1)
            v.wait_ge(rows_ld, 32)

            def hidden(c, e):
                h = hbuf[:, e % 2, :]
                wait_count(v, "dve", gelu_done, c * ET + e + 3)
                wait_count(v, "dve", gt_ld[e % 2], (c * (ET // 2) + e // 2) * 16 + 16)
                v.tensor_tensor(h, h, gbuf[:, e % 2, :], ALU.mult).then_inc(a_raw, 1)
                if e == 0:
                    wait_count(v, "dve", unit_free, c * NU + 2)
                wait_count(v, "dve", a_raw, c * ET + e + 3)
                v.tensor_copy(ahi[:, e, :], h).then_inc(a_split, 1)
                wait_count(v, "dve", a_split, c * ET + e + 1)
                v.tensor_tensor(alo[:, e, :], h, ahi[:, e, :].bitcast(F32), ALU.subtract).then_inc(a_done, 1)

            def add(c, d):
                wait_count(v, "dve", v_mm, c * KD + d + 1)
                wait_count(v, "dve", v_add, c * KD + d + 1)
                src = ps[1 + (d % 4) // 2][:, (d % 2) * 512:(d % 2) * 512 + TD]
                v.tensor_tensor(accT[:, d, :], accT[:, d, :], src, ALU.add).then_inc(v_add, 1)

            for gt in range(GT):
                with v.Fori(0, CPG) as cc:
                    c = cc + gt * CPG
                    for m in range(NU):
                        it = c * STEPS + m // 4
                        r = m % 2
                        if m % 4 == 0:
                            v.tensor_copy(gcol[:], ggate2[:, gt, bass.ds((cc * STEPS + m // 4) * RING, RING)]).then_inc(gcoef, 1)
                        if m % 4 < 2:
                            wait_count(v, "dve", u_ld[r], it * 16 + 16)
                            v.tensor_tensor_reduce(out=urow[r], in0=urow[r], in1=xg[:, gt, :], scale=1.0, scalar=0.0, op0=ALU.mult,
                                                   op1=ALU.add, accum_out=hid[:, r:r + 1]).then_inc(u_used, 1)
                            if r == 1:
                                wait_count(v, "dve", u_used, it * RING + 2 * RING)
                                v.sem_inc(ghid, 1)
                        else:
                            if r == 0:
                                wait_count(v, "dve", ggelu, it + 1)
                                wait_count(v, "dve", gcoef, 2 * it + 1)
                                v.tensor_tensor(act_w2[:], act_w[:], gcol[:], ALU.mult).then_inc(gcoef, 1)
                                wait_count(v, "dve", gcoef, 2 * it + 2)
                            wait_count(v, "dve", v_ld[r], it * 16 + 16)
                            v.scalar_tensor_tensor(x1g[:, gt, :], vrow[r], act_w2[:, r:r + 1], x1g[:, gt, :], ALU.mult, ALU.add).then_inc(v_used, 1)
                            wait_count(v, "dve", v_used, it * RING + RING + r + 1)
                        if 3 <= m < 2 * ET and m % 2 == 1:
                            hidden(c, m // 2 - 1)
                        elif m == 2 * ET:
                            hidden(c, ET - 1)
                        elif m > 2 * ET:
                            add(c, 2 * (m - 2 * ET) - 2)
                            add(c, 2 * (m - 2 * ET) - 1)
                    add(c, KD - 2)
                    add(c, KD - 1)
            v.wait_ge(v_add, CHUNKS * KD + 4)
            v.wait_ge(lo_done, CHUNKS * NU + 4)
            v.sem_inc(f_begin, 1)

            def final(i, t):
                rows = fin_rows(t)
                v.tensor_tensor_reduce(out=fin_junk, in0=rows, in1=rows, scale=1.0 / D, scalar=EPS,
                                       op0=ALU.mult, op1=ALU.add, accum_out=fin_small[:, 0, i:i + 1]).then_inc(f_ms, 1)
                v.wait_ge(f_ms, 2 * i + 1)
                v.sem_inc(f_ss, 1)
                v.wait_ge(f_root, i + 1)
                v.reciprocal(fin_small[:, 2, i:i + 1], fin_small[:, 1, i:i + 1]).then_inc(f_ms, 1)
                v.wait_ge(f_ms, 2 * i + 2)
                v.scalar_tensor_tensor(rows, rows, fin_small[:, 2, i:i + 1], fin_gain, ALU.mult, ALU.mult).then_inc(f_y, 1)

            v.wait_ge(f_ld, 32)
            for i, t in enumerate(FIN_ORDER):
                if t < DT:
                    for half in range(2):
                        v.wait_ge(f_tr, 2 * t + half + 1)
                        rows = fin_dense[:, t, half * 1024:(half + 1) * 1024]
                        v.tensor_tensor(rows, rows, ps[(2 * t + half) % 4][:], ALU.add).then_inc(f_add, 1)
                    v.wait_ge(f_add, 2 * t + 2)
                final(i, t)

        @block2.gpsimd
        def _(pool):
            pool.iota(iota_i2[:], pattern=[[1, NK]], base=0, channel_multiplier=0).then_inc(iota_ready, 1)
            pool.wait_ge(iota_ready, 1)
            pool.tensor_copy(iota_k[:], iota_i2[:]).then_inc(iota_ready, 1)
            pool.wait_ge(sel_cp, 3)
            with pool.Fori(0, NGG * NBB // 2) as i:
                for r in range(2):
                    row = oneh[r][1]
                    wait_count(pool, "pool", oh_row, 2 * i + r + 1)
                    pool.tensor_tensor(row, row, selT[:, 2, bass.ds((2 * i + r) * GB, GB)].unsqueeze(2).to_broadcast([P, GB, NK]),
                                       ALU.mult).then_inc(oh_done, 1)
            pool.sem_inc(lo_done, 4)
            gidx_all = sel[:, 3 * DT * SLOTS:(3 * DT + GT) * SLOTS].bitcast(U32)

            def rows(step, turn, r, dst, table, used, ld):
                wait_count(pool, "pool", used, step * RING + r + 1)
                pool.indirect_dma_start(out=dst[r], out_offset=None, in_=table,
                                        in_offset=bass.IndirectOffsetOnAxis(ap=cur_idx[:, turn, r:r + 1], axis=0)).then_inc(ld[r], 16)

            def index(step, turn):
                pool.tensor_copy(cur_idx[:, turn, :], gidx_all[:, bass.ds(step * RING, RING)]).then_inc(idx_cur, 1)
                wait_count(pool, "pool", idx_cur, step + 1)

            def chunk(c, last):
                for m in range(NU):
                    step, turn, r = c * STEPS + m // 4, (m // 4) % 2, m % 2
                    if m % 4 < 2:
                        rows(step, turn, r, vrow, peer_v, v_used, v_ld)
                    elif not (last and m // 4 == STEPS - 1):
                        if r == 0:
                            index(step + 1, 1 - turn)
                        rows(step + 1, 1 - turn, r, urow, peer_u, u_used, u_ld)
                    wait_count(pool, "pool", hi_done, c * NU + m + 1)
                    pool.tensor_tensor(wlo[:, m % 2, :], raw[m % 4], whi[:, m % 2, :].bitcast(F32), ALU.subtract).then_inc(lo_done, 1)

            pool.tensor_copy(cur_idx[:, 0, :], gidx_all[:, 0:RING]).then_inc(idx_cur, 1)
            pool.wait_ge(idx_cur, 1)
            for r in range(RING):
                pool.wait_ge(u_used, r + 1)
                pool.indirect_dma_start(out=urow[r], out_offset=None, in_=peer_u,
                                        in_offset=bass.IndirectOffsetOnAxis(ap=cur_idx[:, 0, r:r + 1], axis=0)).then_inc(u_ld[r], 16)
            with pool.Fori(0, CHUNKS - 1) as c:
                chunk(c, False)
            chunk(CHUNKS - 1, True)


def constant_matrices():
    import numpy as np
    i = np.arange(P)
    r, c = i[:, None], i[None, :]
    blk = (r // NT == c // NT)
    mats = [r == c, np.ones((P, P), bool), r <= c, (r <= c) & blk, blk]
    for l in range(LEVELS):
        s = 1 << l
        mats.append((r // (2 * s) == c // (2 * s)) & (r % (2 * s) < s) & (c % (2 * s) >= s))
    return np.ascontiguousarray(np.stack([m.astype(np.float32) for m in mats], 1))


def kernel(**inp):
    import numpy as np
    import concourse.bacc as bacc
    from concourse.bass_utils import run_bass_kernel_spmd as run

    a = {k: np.asarray(v) for k, v in inp.items()}

    def cols(v):
        return v.reshape(-1, P).T

    def tiles(w):
        k, n = w.shape
        return w.reshape(k // P, P, n // P, P).transpose(2, 1, 0, 3).reshape(n // P, P, k)

    w_in = a["w_in"][0]
    o = 2 * CONV + 3 * H * P
    w_glu, w_qkv, w_ba, w_z, w_g = (w_in[:, :2 * CONV], w_in[:, 2 * CONV:o], w_in[:, o:o + 2 * H],
                                    w_in[:, o + 2 * H:o + 2 * H + H * P], w_in[:, o + 2 * H + H * P:])
    tg, tq = tiles(w_glu), tiles(w_qkv)
    w_group = np.stack([tq[:H], tq[H:2 * H], tq[2 * H:], tg[NC:], tg[:NC]], 1).reshape(5 * NC, P, D)
    tgt, tp, to = tiles(w_g), tiles(a["conv_pw2"][0]), tiles(a["dn_w_o"][0])
    w_o2 = a["w_out"][0].reshape(2, 8, P, NOC, OCW).transpose(3, 0, 2, 1, 4).reshape(2 * NOC, P, UW)
    keys = a["peer_sub_keys"][0].reshape(HP, NK, P).transpose(2, 0, 1).reshape(P, HP * NK)
    w_units = np.concatenate([tgt, tiles(w_z), np.concatenate([tp, to], 2), w_o2, tiles(a["peer_w_q"][0]), keys[None]], 0)
    cw = a["conv_dw_w"][0].T.reshape(NC, P, CW).transpose(1, 0, 2).reshape(P, -1)
    dw = a["dn_conv_w"][0].T.reshape(3 * H, P, DCW).transpose(1, 0, 2).reshape(P, -1)
    params = np.concatenate([cols(a["norm_mix_g"][0]), cw, cols(a["conv_dw_b"][0]), cols(a["conv_ln_g"][0]), cols(a["conv_ln_b"][0]),
                             dw, cols(a["dn_norm_g"][0]), np.broadcast_to(a["dn_dt_bias"][0], (P, H)),
                             np.broadcast_to(a["dn_a_log"][0], (P, H))], 1)
    u_units = a["peer_u"][0].reshape(NK, P, 2, 8, P).transpose(0, 2, 4, 3, 1).reshape(2 * NK, P, UNIT)
    v_units = a["peer_v"][0].reshape(CHUNKS, ET, P, KD // 2, 2, P).transpose(0, 3, 2, 4, 1, 5).reshape(CHUNKS * KD // 2, P, UNIT)
    ins = {
        "x_prompt": a["x_prompt"][0],
        "x_sample": a["x_sample"].reshape(P, D),
        "consts": constant_matrices(),
        "params": params,
        "conv_prefix": a["state_conformer_conv"][0].reshape(NB, CW - 1, NC, P).transpose(2, 3, 0, 1),
        "dconv_prefix": a["state_delta_conv"][0].reshape(NB, DCW - 1, 3 * H, P).transpose(3, 2, 0, 1).reshape(P, 3 * H * NB, DCW - 1),
        "state_in": a["state_delta"][0].transpose(2, 1, 0, 3).reshape(P, H * NB * P),
        "w_ba": w_ba.reshape(KD, P, 2 * H).transpose(1, 0, 2),
        "w_group": w_group,
        "w_units": w_units,
        "keys": keys,
        "ffn_g": np.broadcast_to(a["norm_ffn_g"][0], (P, D)),
        "final_g": np.broadcast_to(a["norm_final_g"], (P, D)),
        "peer_u": a["peer_u"][0],
        "peer_v": a["peer_v"][0],
        "u_units": u_units,
        "v_units": v_units,
    }
    outs = {
        "y_prompt": (NP_TOK, D), "y_sample": (P, D),
        "conv_new_p": (NC, P, CW - 1), "dconv_new_p": (P, 3 * H, DCW - 1), "state_new_p": (P, H * P),
        "conv_new_s": (NC * NB, P, CW - 1), "dconv_new_s": (P, 3 * H * NB, DCW - 1), "state_new_s": (P, H * NB * P),
    }
    nc = bacc.Bacc("TRN2", target_bir_lowering=False, num_devices=1)
    arrays = {f"in_{k}": np.ascontiguousarray(v) for k, v in ins.items()}
    args = [nc.dram_tensor(k, v.shape, F32, kind="ExternalInput").ap() for k, v in arrays.items()]
    args += [nc.dram_tensor(f"out_{k}", s, F32, kind="ExternalOutput").ap() for k, s in outs.items()]
    build(nc, *args)
    r = run(nc, [arrays], core_ids=[0])
    g = {k: r.results[0][f"out_{k}"] for k in outs}
    return (
        g["y_prompt"].reshape(1, NP_TOK, D),
        g["y_sample"].reshape(NB, NT, D),
        g["conv_new_p"].transpose(2, 0, 1).reshape(1, 1, CW - 1, CONV),
        g["dconv_new_p"].transpose(2, 1, 0).reshape(1, 1, DCW - 1, 3 * H * P),
        g["state_new_p"].reshape(P, H, P).transpose(1, 0, 2).reshape(1, 1, H, P, P),
        g["conv_new_s"].reshape(NC, NB, P, CW - 1).transpose(1, 3, 0, 2).reshape(1, NB, CW - 1, CONV),
        g["dconv_new_s"].reshape(P, 3 * H, NB, DCW - 1).transpose(2, 3, 1, 0).reshape(1, NB, DCW - 1, 3 * H * P),
        g["state_new_s"].reshape(P, H, NB, P).transpose(2, 1, 0, 3).reshape(1, NB, H, P, P),
    )
```
